# Optimizing a Trainium2 kernel written in Bass

```python
import jax
import jax.numpy as jnp
from jax import lax
import numpy as np

D_MODEL = 1024
BATCH = 1
SEQ = 1024
DEPTH = 1
DEC_BATCH = 8
DEC_SEQ = 1
PAST_LEN = 2048
PAGE_SIZE = 128

HEAD_DIM = 64
NSA_HEADS = 8
NSA_GROUPS = 2
HPG = NSA_HEADS // NSA_GROUPS
ROT_DIM = HEAD_DIM // 4
ROPE_THETA = 500000.0
CMP_BLK = 32
CMP_STRIDE = 16
CMP_HID = HEAD_DIM
SLC_BLK = 64
N_SEL = 16
WINDOW = 512
Q_BLK = 128
HG_HEADS = 4
HG_FDIM = 128
HG_IDIM = 128
HG_CHUNK = 64
D_FF = 2816
CONV_W = 3
EPS = 1e-6
NEG = -1e30

NSA_WIDTH = NSA_HEADS * HEAD_DIM
KV_WIDTH = NSA_GROUPS * HEAD_DIM
HG_FWIDTH = HG_HEADS * HG_FDIM
HG_IWIDTH = HG_HEADS * HG_IDIM
IN_SPLITS = (NSA_WIDTH, KV_WIDTH, KV_WIDTH, KV_WIDTH, KV_WIDTH, KV_WIDTH, KV_WIDTH, 3 * NSA_HEADS,
             HG_FWIDTH, HG_FWIDTH, HG_IWIDTH, HG_IWIDTH, D_MODEL, D_MODEL)
N_IN = sum(IN_SPLITS)

kernel_name = 'nsa_hgrn2_gated_hybrid_step'

def rms_norm(x, g):
    xf = x.astype(jnp.float32)
    xf = xf * lax.rsqrt(jnp.mean(xf * xf, axis=-1, keepdims=True) + EPS)
    return xf.astype(x.dtype) * g

def modulate(x, shift, scale):
    return x * (1.0 + scale[:, None, :]) + shift[:, None, :]

def split_in(z):
    cuts = [int(c) for c in np.cumsum(IN_SPLITS)[:-1]]
    return jnp.split(z, cuts, axis=-1)

def rope(x, pos):
    half = ROT_DIM // 2
    inv = ROPE_THETA ** (-jnp.arange(0, ROT_DIM, 2, dtype=jnp.float32) / ROT_DIM)
    ang = pos.astype(jnp.float32)[:, None] * inv[None, :]
    cos = jnp.cos(ang)[None, :, None, :].astype(x.dtype)
    sin = jnp.sin(ang)[None, :, None, :].astype(x.dtype)
    x1 = x[..., :half]
    x2 = x[..., half:ROT_DIM]
    return jnp.concatenate([x1 * cos - x2 * sin, x2 * cos + x1 * sin, x[..., ROT_DIM:]], axis=-1)

def masked_softmax(s, mask):
    s = jnp.where(mask, s, NEG)
    m = jnp.max(s, axis=-1, keepdims=True)
    e = jnp.where(mask, jnp.exp(s - m), 0.0)
    return e / jnp.maximum(jnp.sum(e, axis=-1, keepdims=True), 1e-30)

def compress_one(rows, w1, w2, pe):
    b, t, g, d = rows.shape
    n_half = CMP_BLK // CMP_STRIDE
    nsub = t // CMP_STRIDE
    nc = nsub - n_half + 1
    sub = rows[:, :nsub * CMP_STRIDE].reshape(b, nsub, CMP_STRIDE, g, d)
    w = w1.reshape(n_half, CMP_STRIDE, d, CMP_HID)
    proj = jnp.einsum('bnsgd,rsdh->rbngh', sub, w)
    hid = jnp.einsum('rsd,rsdh->h', pe.reshape(n_half, CMP_STRIDE, d), w)
    for r in range(n_half):
        hid = hid + proj[r, :, r:r + nc]
    return jax.nn.gelu(hid) @ w2

def compress(k_rows, v_rows, w1, w2, pe):
    kc = compress_one(k_rows, w1[0], w2[0], pe[0])
    vc = compress_one(v_rows, w1[1], w2[1], pe[1])
    cmp_end = jnp.arange(kc.shape[1]) * CMP_STRIDE + (CMP_BLK - 1)
    return kc, vc, cmp_end

def overlap_matrix(nc, ns):
    start = jnp.arange(nc) * CMP_STRIDE
    end = start + CMP_BLK - 1
    s0 = jnp.arange(ns) * SLC_BLK
    s1 = s0 + SLC_BLK - 1
    return ((start[:, None] <= s1[None, :]) & (end[:, None] >= s0[None, :])).astype(jnp.float32)

def nsa_block(q, qpos, gates, kc, vc, cmp_end, gather_sel, kw, vw, kw_pos, ns):
    b, tq = q.shape[:2]
    scale = HEAD_DIM ** -0.5
    qg = q.reshape(b, tq, NSA_GROUPS, HPG, HEAD_DIM)
    s = jnp.einsum('bqgjd,bngd->bgjqn', qg, kc).astype(jnp.float32) * scale
    p = masked_softmax(s, cmp_end[None, :] <= qpos[:, None])
    o_cmp = jnp.einsum('bgjqn,bngd->bqgjd', p.astype(vc.dtype), vc)
    imp = jnp.einsum('bgjqn,nm->bgqm', p, overlap_matrix(kc.shape[1], ns))
    blk = jnp.arange(ns)[None, :]
    cur = (qpos // SLC_BLK)[:, None]
    valid = blk * SLC_BLK <= qpos[:, None]
    forced = (blk == 0) | (blk == cur) | (blk == cur - 1)
    score = jnp.where(forced, 1e9, jnp.where(valid, imp, -1e9))
    _, idx = lax.top_k(score, min(N_SEL, ns))
    ks, vs, kpos = gather_sel(idx)
    s = jnp.einsum('bqgjd,bgqkd->bgjqk', qg, ks).astype(jnp.float32) * scale
    p = masked_softmax(s, (kpos <= qpos[None, None, :, None])[:, :, None])
    o_slc = jnp.einsum('bgjqk,bgqkd->bqgjd', p.astype(vs.dtype), vs)
    s = jnp.einsum('bqgjd,bkgd->bgjqk', qg, kw).astype(jnp.float32) * scale
    dist = qpos[:, None] - kw_pos[None, :]
    p = masked_softmax(s, (dist >= 0) & (dist < WINDOW) & (kw_pos[None, :] >= 0))
    o_win = jnp.einsum('bgjqk,bkgd->bqgjd', p.astype(vw.dtype), vw)
    g = jax.nn.sigmoid(gates.astype(jnp.float32)).reshape(b, tq, NSA_GROUPS, HPG, 3)
    o = g[..., 0:1] * o_cmp + g[..., 1:2] * o_slc + g[..., 2:3] * o_win
    return o.astype(q.dtype).reshape(b, tq, NSA_WIDTH)

def nsa_project(parts, pos, q_gain, k_gain):
    q_raw, kc, vc, ks, vs, kw, vw, gates = parts
    b, t = q_raw.shape[:2]
    q = rope(rms_norm(q_raw.reshape(b, t, NSA_HEADS, HEAD_DIM), q_gain), pos)

    def key(k, j):
        return rope(rms_norm(k.reshape(b, t, NSA_GROUPS, HEAD_DIM), k_gain[j]), pos)

    def val(v):
        return v.reshape(b, t, NSA_GROUPS, HEAD_DIM)

    return q, gates, (key(kc, 0), val(vc), key(ks, 1), val(vs), key(kw, 2), val(vw))

def nsa_prompt(q, gates, rows, cmp_w1, cmp_w2, cmp_pe):
    kc_r, vc_r, ks_r, vs_r, kw_r, vw_r = rows
    b, t = q.shape[:2]
    kc, vc, cmp_end = compress(kc_r, vc_r, cmp_w1, cmp_w2, cmp_pe)
    ns = t // SLC_BLK
    kb = ks_r.reshape(b, ns, SLC_BLK, NSA_GROUPS, HEAD_DIM).transpose(0, 3, 1, 2, 4)
    vb = vs_r.reshape(b, ns, SLC_BLK, NSA_GROUPS, HEAD_DIM).transpose(0, 3, 1, 2, 4)
    pad = ((0, 0), (WINDOW, 0), (0, 0), (0, 0))
    kpad = jnp.pad(kw_r, pad)
    vpad = jnp.pad(vw_r, pad)
    bi = jnp.arange(b)[:, None, None, None]
    gi = jnp.arange(NSA_GROUPS)[None, :, None, None]

    def gather_sel(idx):
        tq, n = idx.shape[2], idx.shape[3]
        kpos = (idx[..., None] * SLC_BLK + jnp.arange(SLC_BLK)).reshape(b, NSA_GROUPS, tq, n * SLC_BLK)
        ks = kb[bi, gi, idx].reshape(b, NSA_GROUPS, tq, n * SLC_BLK, HEAD_DIM)
        vs = vb[bi, gi, idx].reshape(b, NSA_GROUPS, tq, n * SLC_BLK, HEAD_DIM)
        return ks, vs, kpos

    def block(i):
        q0 = i * Q_BLK
        qpos = q0 + jnp.arange(Q_BLK)
        kw = lax.dynamic_slice_in_dim(kpad, q0, WINDOW + Q_BLK, axis=1)
        vw = lax.dynamic_slice_in_dim(vpad, q0, WINDOW + Q_BLK, axis=1)
        kw_pos = q0 - WINDOW + jnp.arange(WINDOW + Q_BLK)
        qb = lax.dynamic_slice_in_dim(q, q0, Q_BLK, axis=1)
        gb = lax.dynamic_slice_in_dim(gates, q0, Q_BLK, axis=1)
        return nsa_block(qb, qpos, gb, kc, vc, cmp_end, gather_sel, kw, vw, kw_pos, ns)

    out = lax.map(block, jnp.arange(t // Q_BLK))
    return out.transpose(1, 0, 2, 3).reshape(b, t, NSA_WIDTH)

def nsa_sample(q, gates, rows, pos, cmp_w1, cmp_w2, cmp_pe, pk_c, pv_c, pk_s, pv_s, win_k, win_v, page_table):
    kc_r, vc_r, ks_r, vs_r, kw_r, vw_r = rows
    db, t = q.shape[:2]
    n_pages = page_table.shape[1]
    past = n_pages * PAGE_SIZE

    def past_rows(pool):
        return pool[page_table].reshape(db, past, NSA_GROUPS, HEAD_DIM)

    kc, vc, cmp_end = compress(jnp.concatenate([past_rows(pk_c), kc_r], axis=1),
                               jnp.concatenate([past_rows(pv_c), vc_r], axis=1), cmp_w1, cmp_w2, cmp_pe)
    ns = -(-(past + t) // SLC_BLK)
    bi = jnp.arange(db)[:, None, None, None, None]
    gi = jnp.arange(NSA_GROUPS)[None, :, None, None, None]

    def gather_sel(idx):
        tq, n = idx.shape[2], idx.shape[3]
        kpos = idx[..., None] * SLC_BLK + jnp.arange(SLC_BLK)
        phys = page_table[bi, jnp.clip(kpos // PAGE_SIZE, 0, n_pages - 1)]
        off = kpos % PAGE_SIZE
        new_i = jnp.clip(kpos - past, 0, t - 1)
        is_past = (kpos < past)[..., None]

        def sel(pool, new):
            return jnp.where(is_past, pool[phys, off, gi], new[bi, new_i, gi]).reshape(
                db, NSA_GROUPS, tq, n * SLC_BLK, HEAD_DIM)

        return sel(pk_s, ks_r), sel(pv_s, vs_r), kpos.reshape(db, NSA_GROUPS, tq, n * SLC_BLK)

    win_buf = win_k.shape[1]
    kw = jnp.concatenate([win_k, kw_r], axis=1)
    vw = jnp.concatenate([win_v, vw_r], axis=1)
    kw_pos = past - win_buf + jnp.arange(win_buf + t)
    out = nsa_block(q, pos, gates, kc, vc, cmp_end, gather_sel, kw, vw, kw_pos, ns)
    return out, kw[:, -win_buf:], vw[:, -win_buf:]

def chunk_recurrence(q, k, v, g, s0):
    b, t, hh, _ = q.shape
    idim = v.shape[-1]
    L = min(HG_CHUNK, t)
    pad = (-t) % L
    if pad:
        q, k, v, g = (jnp.pad(a, ((0, 0), (0, pad), (0, 0), (0, 0))) for a in (q, k, v, g))
    nc = (t + pad) // L

    def chunks(a):
        return a.reshape(b, nc, L, hh, a.shape[-1]).transpose(1, 0, 3, 2, 4)

    causal = (jnp.arange(L)[:, None] >= jnp.arange(L)[None, :])[:, :, None]

    def step(s, inp):
        qc, kc, vc, gc = inp
        bcum = jnp.cumsum(gc, axis=2)
        o = jnp.einsum('bhlf,bhfi->bhli', qc * jnp.exp(bcum), s)
        decay = jnp.exp(jnp.where(causal, bcum[:, :, :, None, :] - bcum[:, :, None, :, :], NEG))
        a = jnp.einsum('bhtf,bhsf,bhtsf->bhts', qc, kc, decay)
        o = o + jnp.einsum('bhts,bhsi->bhti', a, vc)
        blast = bcum[:, :, -1:, :]
        s = jnp.exp(blast[:, :, 0, :])[..., None] * s + jnp.einsum('bhsf,bhsi->bhfi', kc * jnp.exp(blast - bcum), vc)
        return s, o

    s_fin, o = lax.scan(step, s0, (chunks(q), chunks(k), chunks(v), chunks(g)))
    o = o.transpose(1, 0, 3, 2, 4).reshape(b, nc * L, hh, idim)[:, :t]
    return o, s_fin

def hgrn2(hq, hf, hi, hg, lb, norm_g, state0):
    b, t = hq.shape[:2]
    shp = (b, t, HG_HEADS, HG_FDIM)
    lbh = lb.reshape(HG_HEADS, HG_FDIM)
    f = lbh + (1.0 - lbh) * jax.nn.sigmoid(hf.reshape(shp).astype(jnp.float32))
    o, s_new = chunk_recurrence(hq.reshape(shp).astype(jnp.float32), 1.0 - f,
                                hi.reshape(b, t, HG_HEADS, HG_IDIM).astype(jnp.float32), jnp.log(f),
                                state0.astype(jnp.float32))
    o = rms_norm(o.astype(hq.dtype), norm_g) * jax.nn.silu(hg.reshape(b, t, HG_HEADS, HG_IDIM))
    return o.reshape(b, t, HG_IWIDTH), s_new.astype(state0.dtype)

def conv_ffn(h, w_up, conv_w, conv_b, w_down, buf):
    t = h.shape[1]
    u, v = jnp.split(h @ w_up, 2, axis=-1)
    u_ext = jnp.concatenate([buf.astype(u.dtype), u], axis=1)
    y = conv_b
    for j in range(CONV_W):
        y = y + conv_w[j] * u_ext[:, j:j + t]
    return (jax.nn.silu(y) * v) @ w_down, u_ext[:, -(CONV_W - 1):]

def layer_step(x, c, pos, lw, lb, hg_state0, conv_buf0, nsa_cache=None, page_table=None):
    sh1, sc1, g1, sh2, sc2, g2 = jnp.split(c @ lw['ada_w'] + lw['ada_b'], 6, axis=-1)
    h = modulate(rms_norm(x, lw['norm_attn']), sh1, sc1)
    parts = split_in(h @ lw['w_in'])
    q, gates, rows = nsa_project(parts[:8], pos, lw['q_gain'], lw['k_gain'])
    if nsa_cache is None:
        o_nsa = nsa_prompt(q, gates, rows, lw['cmp_w1'], lw['cmp_w2'], lw['cmp_pe'])
        w = min(WINDOW, x.shape[1])
        nsa_new = rows[:4] + (rows[4][:, -w:], rows[5][:, -w:])
    else:
        o_nsa, wk, wv = nsa_sample(q, gates, rows, pos, lw['cmp_w1'], lw['cmp_w2'], lw['cmp_pe'],
                                   *nsa_cache, page_table)
        nsa_new = rows[:4] + (wk, wv)
    o_hg, s_hg = hgrn2(parts[8], parts[9], parts[10], parts[11], lb, lw['hg_norm'], hg_state0)
    mix = jax.nn.sigmoid(parts[12]) * (o_nsa @ lw['w_br_nsa']) + jax.nn.sigmoid(parts[13]) * (o_hg @ lw['w_br_hg'])
    x = x + g1[:, None, :] * (mix @ lw['w_out'])
    h2 = modulate(rms_norm(x, lw['norm_ffn']), sh2, sc2)
    f_out, conv_new = conv_ffn(h2, lw['w_up'], lw['conv_w'], lw['conv_b'], lw['w_down'], conv_buf0)
    x = x + g2[:, None, :] * f_out
    return x, nsa_new + (s_hg, conv_new)

def setup_inputs(seed: int = 0) -> dict:
    key = jax.random.key(seed)
    ks = jax.random.split(key, 32)

    def nrm(k, shape, s=1.0):
        return s * jax.random.normal(k, shape, jnp.float32)

    n_pages = PAST_LEN // PAGE_SIZE
    used = DEC_BATCH * n_pages
    n_phys = used + max(1, used // 4)
    win_buf = min(WINDOW, PAST_LEN)
    page_table = jax.random.permutation(ks[0], n_phys)[:used].reshape(DEC_BATCH, n_pages).astype(jnp.int32)
    pool = (DEPTH, n_phys, PAGE_SIZE, NSA_GROUPS, HEAD_DIM)
    win = (DEPTH, DEC_BATCH, win_buf, NSA_GROUPS, HEAD_DIM)
    return {
        'x_prompt': nrm(ks[1], (BATCH, SEQ, D_MODEL)),
        'x_sample': nrm(ks[2], (DEC_BATCH, DEC_SEQ, D_MODEL)),
        'cache_cmp_k': nrm(ks[3], pool),
        'cache_cmp_v': nrm(ks[4], pool),
        'cache_slc_k': nrm(ks[5], pool),
        'cache_slc_v': nrm(ks[6], pool),
        'cache_win_k': nrm(ks[7], win),
        'cache_win_v': nrm(ks[8], win),
        'state_hgrn': nrm(ks[9], (DEPTH, DEC_BATCH, HG_HEADS, HG_FDIM, HG_IDIM), 0.5),
        'state_ffn_conv': nrm(ks[10], (DEPTH, DEC_BATCH, CONV_W - 1, D_FF)),
        'page_table': page_table,
        'c_prompt': nrm(ks[11], (BATCH, D_MODEL)),
        'c_sample': nrm(ks[12], (DEC_BATCH, D_MODEL)),
        'ada_w': nrm(ks[13], (DEPTH, D_MODEL, 6 * D_MODEL), 0.5 * D_MODEL ** -0.5),
        'ada_b': nrm(ks[14], (DEPTH, 6 * D_MODEL), 0.01),
        'norm_attn': 1.0 + nrm(ks[15], (DEPTH, D_MODEL), 0.1),
        'norm_ffn': 1.0 + nrm(ks[16], (DEPTH, D_MODEL), 0.1),
        'w_in': nrm(ks[17], (DEPTH, D_MODEL, N_IN), D_MODEL ** -0.5),
        'q_gain': 1.0 + nrm(ks[18], (DEPTH, HEAD_DIM), 0.1),
        'k_gain': 1.0 + nrm(ks[19], (DEPTH, 3, HEAD_DIM), 0.1),
        'cmp_w1': nrm(ks[20], (DEPTH, 2, CMP_BLK * HEAD_DIM, CMP_HID), (CMP_BLK * HEAD_DIM) ** -0.5),
        'cmp_w2': nrm(ks[21], (DEPTH, 2, CMP_HID, HEAD_DIM), CMP_HID ** -0.5),
        'cmp_pe': nrm(ks[22], (DEPTH, 2, CMP_BLK, HEAD_DIM), 0.1),
        'hg_lb': nrm(ks[23], (DEPTH + 1, HG_FWIDTH)),
        'hg_norm': 1.0 + nrm(ks[24], (DEPTH, HG_IDIM), 0.1),
        'w_br_nsa': nrm(ks[25], (DEPTH, NSA_WIDTH, D_MODEL), NSA_WIDTH ** -0.5),
        'w_br_hg': nrm(ks[26], (DEPTH, HG_IWIDTH, D_MODEL), HG_IWIDTH ** -0.5),
        'w_out': nrm(ks[27], (DEPTH, D_MODEL, D_MODEL), D_MODEL ** -0.5),
        'w_up': nrm(ks[28], (DEPTH, D_MODEL, 2 * D_FF), D_MODEL ** -0.5),
        'conv_w': nrm(ks[29], (DEPTH, CONV_W, D_FF), CONV_W ** -0.5),
        'conv_b': nrm(ks[30], (DEPTH, D_FF), 0.01),
        'w_down': nrm(ks[31], (DEPTH, D_FF, D_MODEL), D_FF ** -0.5),
    }

def reference(x_prompt, x_sample, cache_cmp_k, cache_cmp_v, cache_slc_k, cache_slc_v, cache_win_k, cache_win_v,
              state_hgrn, state_ffn_conv, page_table, c_prompt, c_sample, ada_w, ada_b, norm_attn, norm_ffn, w_in,
              q_gain, k_gain, cmp_w1, cmp_w2, cmp_pe, hg_lb, hg_norm, w_br_nsa, w_br_hg, w_out, w_up, conv_w,
              conv_b, w_down):
    lb_all = jnp.cumsum(jax.nn.softmax(hg_lb.astype(jnp.float32), axis=0), axis=0)
    b, t = x_prompt.shape[:2]
    db, tn = x_sample.shape[:2]
    pos_p = jnp.arange(t)
    pos_s = PAST_LEN + jnp.arange(tn)
    xp, xs = x_prompt, x_sample
    p_states, s_states = [], []
    for l in range(DEPTH):
        lw = dict(ada_w=ada_w[l], ada_b=ada_b[l], norm_attn=norm_attn[l], norm_ffn=norm_ffn[l], w_in=w_in[l],
                  q_gain=q_gain[l], k_gain=k_gain[l], cmp_w1=cmp_w1[l], cmp_w2=cmp_w2[l], cmp_pe=cmp_pe[l],
                  hg_norm=hg_norm[l], w_br_nsa=w_br_nsa[l], w_br_hg=w_br_hg[l], w_out=w_out[l], w_up=w_up[l],
                  conv_w=conv_w[l], conv_b=conv_b[l], w_down=w_down[l])
        hg0 = jnp.zeros((b, HG_HEADS, HG_FDIM, HG_IDIM), xp.dtype)
        cb0 = jnp.zeros((b, CONV_W - 1, D_FF), xp.dtype)
        xp, st_p = layer_step(xp, c_prompt, pos_p, lw, lb_all[l], hg0, cb0)
        nsa_cache = (cache_cmp_k[l], cache_cmp_v[l], cache_slc_k[l], cache_slc_v[l], cache_win_k[l], cache_win_v[l])
        xs, st_s = layer_step(xs, c_sample, pos_s, lw, lb_all[l], state_hgrn[l], state_ffn_conv[l],
                              nsa_cache, page_table)
        p_states.append(st_p)
        s_states.append(st_s)
    p_ck, p_cv, p_sk, p_sv, p_wk, p_wv, p_hg, p_cf = [jnp.stack(a) for a in zip(*p_states)]
    s_ck, s_cv, s_sk, s_sv, s_wk, s_wv, s_hg, s_cf = [jnp.stack(a) for a in zip(*s_states)]
    return (xp, xs, p_ck, p_cv, p_sk, p_sv, p_wk, p_wv, p_hg, p_cf,
            s_ck, s_cv, s_sk, s_sv, s_wk, s_wv, s_hg, s_cf)


_drawn_inputs = setup_inputs


def setup_inputs(seed=0):
    import zlib

    import numpy as np

    out = dict(_drawn_inputs(seed))
    spreads = {}
    factors = {'cache_cmp_k': 7.027,
     'cache_cmp_v': 5.256,
     'cache_slc_k': 8.0,
     'cache_slc_v': 7.208,
     'ada_b': 3.379,
     'q_gain': 8.0,
     'cmp_pe': 6.632,
     'conv_b': 8.0}
    for name, (base, spread) in spreads.items():
        noise = np.random.default_rng([zlib.crc32(name.encode()), seed]).standard_normal(out[name].shape)
        drawn = base * np.exp(spread * noise) if base else spread * noise
        out[name] = jnp.asarray(drawn.astype(out[name].dtype))
    for name, factor in factors.items():
        out[name] = (out[name] * factor).astype(out[name].dtype)
    return out
```

```python
from contextlib import ExitStack

import numpy as np

import concourse.bass as bass
import concourse.mybir as mybir

F32 = mybir.dt.float32
BF16 = mybir.dt.bfloat16
I32 = mybir.dt.int32
U32 = mybir.dt.uint32
U8 = mybir.dt.uint8
ALU = mybir.AluOpType
ACT = mybir.ActivationFunctionType
AX = mybir.AxisListType

P = 128
D = 1024
KT = D // P
SEQ = 1024
NB = 8
TOK = SEQ + NB
TT = SEQ // P
CH = TOK // 3
HD = 64
NH = 8
NG = 2
HPG = NH // NG
CMP_STRIDE = 16
NSUB_P = SEQ // CMP_STRIDE
NC_P = NSUB_P - 1
PAST = 2048
NSUB_S = PAST // CMP_STRIDE
NC_S = NSUB_S - 1
PAGE = 128
PAGES = PAST // PAGE
SUB_PER_PAGE = PAGE // CMP_STRIDE
SLC = 64
NSEL = 16
NS_S = PAST // SLC + 1
WIN = 512
HGH = 4
DFF = 2816
FT = DFF // P
EPS = 1e-6
X3 = 4128
NEG = -1e30
SCALE = HD ** -0.5

C_Q, C_KC, C_VS, C_GATE, C_HQ, C_HF, C_HI, C_HG, C_GA, C_GB = (
    0, 512, 896, 1280, 1304, 1816, 2328, 2840, 3352, 4376)
SH1, SC1, G1, SH2, SC2, G2 = (KT * i for i in range(6))


class Core:
    pass


class Unit:

    def __init__(self, kind, t, h, lo, n, last):
        self.kind, self.t, self.h, self.lo, self.n, self.last = kind, t, h, lo, n, last


def rows_of(t):
    return P if t < TT else NB


class Chain:

    def __init__(self, sem):
        self.sem, self.base, self.n, self.per = sem, 0, 0, None

    def link(self, eng, ins):
        self.n += 1
        ins.then_inc(self.sem, 1)
        eng.wait_ge(self.sem, self.base + self.n)

    def enter(self, i, per):
        self.before = self.base + self.n
        self.base, self.n, self.per = self.before + i * per, 0, per

    def leave(self, times):
        assert self.n == self.per, (self.n, self.per)
        self.base, self.n = self.before + self.per * times, 0


def constants():
    q = np.arange(P)[:, None]
    k = np.arange(P)[None, :]
    add = np.zeros((P, 2, P), np.float32)
    add[:, 0] = np.where(k <= q, 0.0, NEG)
    add[:, 1] = np.where(k > q, 0.0, NEG)
    cmp_ok = np.zeros((P, TT, HD), np.float32)
    for t in range(TT):
        cmp_ok[:, t, :NC_P] = (np.arange(NC_P)[None] * CMP_STRIDE + 31) <= (t * P + q)
    inv = (np.float32(500000.0) ** (-np.arange(0, 16, 2, dtype=np.float32) / np.float32(16))).astype(np.float32)
    pos = np.concatenate([np.arange(SEQ), np.full(NB, PAST)]).astype(np.float32)
    ang = (pos[:, None] * inv[None]).astype(np.float32)
    cos, sin = np.cos(ang), np.sin(ang)
    rope = np.concatenate([cos, cos, sin, sin], axis=1).astype(np.float32)
    start = np.arange(NC_S) * CMP_STRIDE
    s0 = np.arange(NS_S) * SLC
    over = ((start[:, None] <= s0[None] + SLC - 1) & (start[:, None] + 31 >= s0[None])).astype(np.float32)
    own = (np.arange(HD)[:, None] // NH == np.arange(NB)[None]).astype(np.float32)
    lower = (np.arange(NS_S)[None, :] < np.arange(NS_S)[:, None]).astype(np.float32)
    lower = np.broadcast_to(lower.reshape(1, -1), (HD, NS_S * NS_S))
    levels = np.zeros((P, 8, P), np.int32)
    s, t = q, k
    levels[:, 7] = s == t
    for n in range(7):
        m = 64 >> n
        levels[:, n] = (s // (2 * m) == t // (2 * m)) & (s % (2 * m) < m) & (t % (2 * m) >= m)
    return {
        "c_ident": np.eye(P, dtype=np.float32),
        "c_add": add,
        "c_cmp_add": np.where(cmp_ok > 0, 0.0, NEG).astype(np.float32),
        "c_cmp_mul": cmp_ok,
        "c_rope": rope,
        "c_over": over,
        "c_own": own,
        "c_lower": np.ascontiguousarray(lower),
        "c_sub": (np.arange(P)[:, None] % SUB_PER_PAGE).astype(np.float32),
        "c_levels": levels,
    }


def allocate(nc):
    sb = nc.alloc_sbuf_tensor
    s = Core()
    s.xT = sb("xT", [P, KT, TOK], F32)
    s.hT = sb("hT", [P, KT, TOK], F32)
    s.ring = sb("ring", [P, 8192], F32)
    s.work = sb("work", [P, 25904], F32)
    s.ident = sb("ident", [P, P], F32)
    s.identb = sb("identb", [P, P], BF16)
    s.ones = sb("ones", [P, P], F32)
    s.add = sb("add", [P, 2, P], BF16)
    s.rope = sb("rope", [P, TT + 1, 32], F32)
    s.gain = sb("gain", [P, 4, HD], F32)
    s.vec = sb("vec", [P, 80], F32)
    s.conv = sb("conv", [P, 4, FT], F32)
    s.mod = sb("mod", [P, 6 * KT, NB + 1], F32)
    s.A1 = sb("A1", [P, KT, NB + 1], F32)
    s.A2 = sb("A2", [P, KT, NB + 1], F32)
    s.cT = sb("cT", [P, KT, NB + 1], F32)
    s.eps = sb("eps", [P, 1], F32)
    s.gidx = sb("gidx", [P, NB], U32)
    s.psall = nc.alloc_psum_tensor("psall", [P, 8 * 512], F32)
    s.ps = [s.psall[:, 512 * i:512 * (i + 1)] for i in range(8)]
    s.sem = nc.alloc_semaphore
    s.dve_chain = Chain(s.sem("dve_chain"))
    s.act_chain = Chain(s.sem("act_chain"))
    s.pool_chain = Chain(s.sem("pool_chain"))
    s.oN = view(s.work, 0, 4, TOK)
    s.oH = view(s.work, 4128, 4, TOK)
    s.qT = view(s.work, 8256, 4, TOK)
    s.ksT = view(s.work, 12384, TOK)
    s.kwT = view(s.work, 13416, TOK)
    s.vkv = view(s.work, 14448, TT + 1, 2, P)
    s.vhi = view(s.work, 16752, TT + 1, 512)
    s.gates = view(s.work, 21360, TT + 1, 24)
    s.kcT = view(s.work, 21576, NB + 1, P)
    s.vc = view(s.work, 22728, NB + 1, P)
    return s


def view(t, start, *shape):
    n = 1
    for x in shape:
        n *= x
    v = t[:, start:start + n]
    if len(shape) == 1:
        return v
    names = "abcd"[:len(shape)]
    return v.rearrange(f"p ({' '.join(names)}) -> p {' '.join(names)}", **dict(zip(names, shape)))


def bc(ap, shape):
    return ap.to_broadcast(list(shape))


def stage_modulation(nc, s, T):
    x_tm = view(s.work, 0, TT + 1, D)
    rows = view(s.work, 9216, P)
    crow = view(s.work, 9344, P)
    c_tm = view(s.work, 9472, D)
    add_f = view(s.work, 10496, 2, P)
    panel = [view(s.ring, 2048 * i, KT, 256) for i in range(4)]
    small, x_in, c_in = s.sem("m_small"), s.sem("m_x_in"), s.sem("m_c_in")
    loaded = [s.sem(f"m_loaded{i}") for i in range(4)]
    panel_used, tr_done = s.sem("m_panel_used"), s.sem("m_tr_done")
    evac_v, evac_a, ada_done = s.sem("m_evac_v"), s.sem("m_evac_a"), s.sem("m_ada_done")
    ready = s.sem("m_cT_ready")
    ada = T["ada_w"].rearrange("(k p) n -> p k n", p=P)
    NGRP = 2 * (TT + 1)

    with nc.Block() as block:
        @block.sync
        def _(sp):
            sp.dma_start(s.ident[:, :], T["c_ident"]).then_inc(c_in, 16)
            sp.dma_start(c_tm[0:1, :], T["c_prompt"]).then_inc(c_in, 16)
            sp.dma_start(c_tm[1:NB + 1, :], T["c_sample"]).then_inc(c_in, 16)
            for n in range(4):
                sp.dma_start(panel[n], ada[:, :, n * 256:(n + 1) * 256]).then_inc(loaded[n], 16)
            with sp.Fori(0, 5) as i:
                for n in range(4):
                    sp.wait_ge(panel_used, i * 4 + n + 1)
                    sp.dma_start(panel[n], ada[:, :, bass.ds(i * 1024 + (n + 4) * 256, 256)]).then_inc(loaded[n], 16)

        @block.gpsimd
        def _(pool):
            for new, old in ((T["s_wk"], T["cache_win_k"]), (T["s_wv"], T["cache_win_v"])):
                pool.dma_start(new[0, :, 0:WIN - 1].rearrange("b t g d -> b (t g d)"),
                               old[0, :, 1:WIN].rearrange("b t g d -> b (t g d)")).then_inc(small, 16)
            pool.wait_ge(small, 32)

        @block.scalar
        def _(act):
            act.dma_start(rows[0:48, :], T["ada_b"][0].rearrange("(r p) -> r p", p=P)).then_inc(x_in, 16)
            act.dma_start(rows[48:56, :], T["norm_attn"][0].rearrange("(r p) -> r p", p=P)).then_inc(x_in, 16)
            act.dma_start(rows[56:64, :], T["norm_ffn"][0].rearrange("(r p) -> r p", p=P)).then_inc(x_in, 16)
            act.dma_start(rows[64:72, :], T["hg_lb"].rearrange("a (r p) -> (a r) p", p=P)).then_inc(x_in, 16)
            act.dma_start(rows[72:73, :], T["hg_norm"]).then_inc(x_in, 16)
            act.dma_start(crow[0:66, :], T["conv_w"][0].rearrange("j (r p) -> (j r) p", p=P)).then_inc(x_in, 16)
            act.dma_start(crow[66:88, :], T["conv_b"][0].rearrange("(r p) -> r p", p=P)).then_inc(x_in, 16)
            act.dma_start(x_tm[:, 0:TT, :], T["x_prompt"][0].rearrange("(t p) d -> p t d", p=P)).then_inc(x_in, 16)
            act.dma_start(x_tm[0:NB, TT, :], T["x_sample"].rearrange("b t d -> (b t) d")).then_inc(x_in, 16)
            act.dma_start(add_f, T["c_add"]).then_inc(x_in, 16)
            act.dma_start(s.rope[:, 0:TT, :], T["c_rope"][0:SEQ].rearrange("(t p) c -> p t c", p=P)).then_inc(x_in, 16)
            act.dma_start(s.rope[0:NB, TT, :], T["c_rope"][SEQ:TOK]).then_inc(x_in, 16)
            act.dma_start(s.gain[:, 0, :], T["q_gain"].partition_broadcast(P).rearrange("p a d -> p (a d)")).then_inc(x_in, 16)
            act.dma_start(s.gain[:, 1:4, :], T["k_gain"][0].partition_broadcast(P)).then_inc(x_in, 16)
            for g in range(1, NGRP, 2):
                t, half = g // 2, g % 2
                n = rows_of(t)
                act.wait_ge(tr_done, 4 + g)
                act.activation(s.xT[:, 4 * half:4 * half + 4, t * P:t * P + n],
                               view(s.ps[2 + g % 4], 0, 4, P)[:, :, 0:n], ACT.Copy).then_inc(evac_a, 1)
            act.wait_ge(x_in, 224)

        @block.tensor
        def _(pe):
            pe.wait_ge(c_in, 48)
            for k in range(KT):
                last = pe.transpose(s.ps[1][:, 9 * k:9 * k + 9], c_tm[0:9, k * P:(k + 1) * P], s.ident[0:9, 0:9])
            last.then_inc(tr_done, 1)
            pe.wait_ge(x_in, 224)
            pe.transpose(s.ps[2][:, 0:73], rows[0:73, :], s.ident[0:73, 0:73]).then_inc(tr_done, 1)
            pe.transpose(s.ps[3][:, 0:88], crow[0:88, :], s.ident[0:88, 0:88]).then_inc(tr_done, 1)
            for g in range(NGRP):
                t, half = g // 2, g % 2
                n = rows_of(t)
                if g < 2:
                    pe.wait_ge(evac_v, 3)
                elif g >= 4:
                    if g % 2:
                        pe.wait_ge(evac_a, (g - 4) // 2 + 1)
                    else:
                        pe.wait_ge(evac_v, 3 + (g - 4) // 2 + 1)
                for j in range(4):
                    k = 4 * half + j
                    last = pe.transpose(s.ps[2 + g % 4][:, j * P:j * P + n], x_tm[0:n, t, k * P:(k + 1) * P],
                                        s.ident[0:n, 0:n])
                last.then_inc(tr_done, 1)
            pe.wait_ge(ready, 1)
            with pe.Fori(0, 6) as i:
                for n in range(4):
                    pe.wait_ge(loaded[n], i * 16 + 16)
                    for h in range(2):
                        for k in range(KT):
                            last = pe.matmul(s.ps[0][:, bass.ds(i * 72 + (2 * n + h) * 9, 9)],
                                             panel[n][:, k, h * P:(h + 1) * P], s.cT[:, k, :],
                                             start=(k == 0), stop=(k == KT - 1))
                    last.then_inc(panel_used, 1)
            pe.wait_ge(panel_used, 24)
            pe.sem_inc(ada_done, 1)

        @block.vector
        def _(v):
            ch = s.dve_chain
            v.memset(s.ones[:, :], 1.0)
            ch.link(v, v.memset(s.eps[:, :], EPS))
            v.wait_ge(tr_done, 1)
            v.tensor_copy(s.cT[:, :, :], view(s.ps[1], 0, KT, 9)).then_inc(ready, 1)
            v.wait_ge(c_in, 48)
            v.tensor_copy(s.identb[:, :], s.ident[:, :])
            v.wait_ge(tr_done, 3)
            v.wait_ge(x_in, 224)
            v.tensor_copy(s.add[:, :, :], add_f)
            v.tensor_copy(s.vec[:, 0:73], s.ps[2][:, 0:73]).then_inc(evac_v, 1)
            v.tensor_copy(s.conv[:, :, :], view(s.ps[3], 0, 4, FT)).then_inc(evac_v, 1)
            v.wait_ge(evac_v, 2)
            v.nop().then_inc(evac_v, 1)
            for g in range(0, NGRP, 2):
                t, half = g // 2, g % 2
                n = rows_of(t)
                v.wait_ge(tr_done, 4 + g)
                v.tensor_copy(s.xT[:, 4 * half:4 * half + 4, t * P:t * P + n],
                              view(s.ps[2 + g % 4], 0, 4, P)[:, :, 0:n]).then_inc(evac_v, 1)
            v.wait_ge(ada_done, 1)
            ch.link(v, v.tensor_tensor(s.mod[:, :, :], view(s.ps[0], 0, 48, 9),
                                       bc(s.vec[:, 0:48].unsqueeze(2), (P, 48, 9)), ALU.add))
            for A, sc, g in ((s.A1, SC1, 48), (s.A2, SC2, 56)):
                ch.link(v, v.tensor_scalar(A[:, :, :], s.mod[:, sc:sc + KT, :], 1.0, None, ALU.add))
                ch.link(v, v.tensor_tensor(A[:, :, :], A[:, :, :], bc(s.vec[:, g:g + KT].unsqueeze(2), (P, KT, 9)),
                                           ALU.mult))


def stage_norm(nc, s, name, A, shift):
    sq = [view(s.ring, 1032 * i, TOK) for i in range(2)]
    lnv = view(s.ring, 2064, TOK)
    rstd = view(s.ring, 3096, TOK)
    tmp = view(s.ring, 4128, KT, NB)
    squared, summed, used = s.sem(f"{name}_squared"), s.sem(f"{name}_summed"), s.sem(f"{name}_used")
    rstd_ready, scaled = s.sem(f"{name}_rstd"), s.sem(f"{name}_scaled")

    with nc.Block() as block:
        @block.scalar
        def _(act):
            ch = s.act_chain
            for k in range(KT):
                if k >= 2:
                    act.wait_ge(used, k - 1)
                act.activation(sq[k % 2], s.xT[:, k, :], ACT.Square).then_inc(squared, 1)
            act.wait_ge(summed, 1)
            for c in range(3):
                last = act.activation(lnv[:, c * CH:(c + 1) * CH], s.ps[c][:, 0:CH], ACT.Ln,
                                      bias=s.eps[:, 0:1], scale=1.0 / D)
            ch.link(act, last)
            act.activation(rstd, lnv, ACT.Exp, scale=-0.5).then_inc(rstd_ready, 1)
            for k in range(KT):
                act.wait_ge(scaled, k + 1)
                last = act.activation(s.hT[:, k, 0:SEQ], s.hT[:, k, 0:SEQ], ACT.Identity,
                                      bias=s.mod[:, shift + k, 0:1])
            ch.link(act, last)

        @block.tensor
        def _(pe):
            for k in range(KT):
                pe.wait_ge(squared, k + 1)
                for c in range(3):
                    last = pe.matmul(s.ps[c][:, 0:CH], s.ones[:, :], sq[k % 2][:, c * CH:(c + 1) * CH],
                                     start=(k == 0), stop=(k == KT - 1))
                last.then_inc(used, 1)
            pe.wait_ge(used, KT)
            pe.sem_inc(summed, 1)

        @block.vector
        def _(v):
            ch = s.dve_chain
            v.wait_ge(rstd_ready, 1)
            for k in range(KT):
                v.scalar_tensor_tensor(out=s.hT[:, k, 0:SEQ], in0=s.xT[:, k, 0:SEQ], scalar=A[:, k, 0:1],
                                       in1=rstd[:, 0:SEQ], op0=ALU.mult, op1=ALU.mult).then_inc(scaled, 1)
            ch.link(v, v.tensor_tensor(tmp, s.xT[:, :, SEQ:TOK], A[:, :, 1:NB + 1], ALU.mult))
            ch.link(v, v.tensor_tensor(tmp, tmp, bc(rstd[:, SEQ:TOK].unsqueeze(1), (P, KT, NB)), ALU.mult))
            ch.link(v, v.tensor_tensor(s.hT[:, :, SEQ:TOK], tmp, s.mod[:, shift:shift + KT, 1:NB + 1], ALU.add))


def stage_token_major(nc, s, T):
    groups = ((C_Q, 512), (C_KC, 384), (C_VS, 408), (C_HI, 512))
    weights = [view(s.ring, 4096 * (g % 2), KT, w) for g, (_, w) in enumerate(groups)]
    w_in = T["w_in"][0].rearrange("(k p) n -> p k n", p=P)
    F = 21576
    sq = [view(s.work, F + 512 * i, 512) for i in range(2)]
    stat = [view(s.work, F + 1024 + 64 * i, 64) for i in range(2)]
    rot = [view(s.work, F + 1152 + 256 * i, 256) for i in range(2)]
    qn = [view(s.work, F + 1664 + 512 * i, 512) for i in range(2)]
    kn = [view(s.work, F + 2688 + 384 * i, 384) for i in range(2)]
    NT = TT + 1
    UNITS = 4 * NT
    n_psum = 3
    w_loaded = [s.sem(f"t_w{i}") for i in range(4)]
    mm, act_free, dve_free = s.sem("t_mm"), s.sem("t_act_free"), s.sem("t_dve_free")
    squared, summed, rstd_ready = s.sem("t_squared"), s.sem("t_summed"), s.sem("t_rstd")
    normed, turned, turn_read = s.sem("t_normed"), s.sem("t_turned"), s.sem("t_turn_read")
    copied = s.sem("t_copied")
    sent = [s.sem(f"t_sent{i}") for i in range(2)]
    sent_v = s.sem("t_sent_v")

    with nc.Block() as block:
        @block.gpsimd
        def _(pool):
            for g, (c, w) in enumerate(groups):
                if g >= 2:
                    pool.wait_ge(mm, (g - 1) * NT)
                pool.dma_start(weights[g], w_in[:, :, c:c + w]).then_inc(w_loaded[g], 16)

        @block.sync
        def _(sp):
            for u in range(NT, 3 * NT):
                g, t = u // NT, u % NT
                n = rows_of(t)
                st = kn[u % 2]
                sp.wait_ge(normed, u + 1)
                sp.wait_ge(copied, u + 1)
                rows = slice(t * P, t * P + P)
                flat = lambda a: a.rearrange("t g d -> t (g d)")
                if g == 1:
                    for j, (pr, sa) in enumerate(((T["p_ck"], T["s_ck"]), (T["p_cv"], T["s_cv"]), (T["p_sk"], T["s_sk"]))):
                        dst = flat(pr[0, 0, rows]) if t < TT else flat(sa[0, :, 0])
                        sp.dma_start(dst, st[0:n, j * P:(j + 1) * P]).then_inc(sent[u % 2], 16)
                else:
                    dst = flat(T["p_sv"][0, 0, rows]) if t < TT else flat(T["s_sv"][0, :, 0])
                    sp.dma_start(dst, s.vkv[0:n, t, 0, :]).then_inc(sent_v, 16)
                    if t >= TT - WIN // P:
                        rows = slice((t - TT + WIN // P) * P, (t - TT + WIN // P + 1) * P)
                        dst = flat(T["p_wk"][0, 0, rows]) if t < TT else flat(T["s_wk"][0, :, WIN - 1])
                        sp.dma_start(dst, st[0:n, 0:P]).then_inc(sent[u % 2], 16)
                        dst = flat(T["p_wv"][0, 0, rows]) if t < TT else flat(T["s_wv"][0, :, WIN - 1])
                        sp.dma_start(dst, s.vkv[0:n, t, 1, :]).then_inc(sent_v, 16)
            sp.wait_ge(copied, UNITS)
            sp.dma_start(T["hi_rows"], s.vhi[0:NB, TT, :]).then_inc(sent_v, 16)
            sp.dma_start(T["gate_rows"], s.gates[0:NB, TT, :]).then_inc(sent_v, 16)
            sp.wait_ge(sent_v, 16 * (NT + WIN // P + 1 + 2))
            for b in range(2):
                sp.wait_ge(sent[b], 16 * sum((3 if u < 2 * NT else u % NT >= TT - WIN // P)
                                             for u in range(NT, 3 * NT) if u % 2 == b))

        @block.tensor
        def _(pe):
            def turn(u):
                g, t = u // NT, u % NT
                if u < 0 or g > 2:
                    return
                n = rows_of(t)
                pe.wait_ge(normed, u + 1)
                if u >= 2:
                    pe.wait_ge(turn_read, u - 1)
                out = s.ps[6 + u % 2]
                if g == 0:
                    for j in range(HPG):
                        last = pe.transpose(out[:, j * P:j * P + n], qn[u % 2][0:n, j * P:(j + 1) * P],
                                            s.ident[0:n, 0:n])
                else:
                    at = 256 if g == 1 else 0
                    last = pe.transpose(out[:, 0:n], kn[u % 2][0:n, at:at + P], s.ident[0:n, 0:n])
                last.then_inc(turned, 1)

            for u in range(UNITS):
                g, t = u // NT, u % NT
                n, w = rows_of(t), groups[g][1]
                if t == 0:
                    pe.wait_ge(w_loaded[g], 16)
                if u >= n_psum:
                    pe.wait_ge(act_free, u - n_psum + 1)
                    pe.wait_ge(dve_free, u - n_psum + 1)
                for k in range(KT):
                    last = pe.matmul(s.ps[u % n_psum][0:n, 0:w], s.hT[:, k, t * P:t * P + n], weights[g][:, k, :],
                                     start=(k == 0), stop=(k == KT - 1))
                last.then_inc(mm, 1)
                turn(u - 1)

        @block.scalar
        def _(act):
            ch = s.act_chain

            def evacuate(u):
                g, t = u // NT, u % NT
                n = rows_of(t)
                act.wait_ge(turned, u + 1)
                cols = slice(t * P, t * P + n)
                if g == 0:
                    src = view(s.ps[6 + u % 2], 0, HPG, P)[:, :, 0:n]
                    act.activation(s.qT[:, :, cols], src, ACT.Copy).then_inc(turn_read, 1)
                else:
                    dst = s.ksT if g == 1 else s.kwT
                    act.activation(dst[:, cols], s.ps[6 + u % 2][:, 0:n], ACT.Copy).then_inc(turn_read, 1)

            for u in range(UNITS):
                g, t = u // NT, u % NT
                n = rows_of(t)
                ps = s.ps[u % n_psum]
                act.wait_ge(mm, u + 1)
                if g == 3:
                    ch.link(act, act.activation(s.vhi[0:n, t, :], ps[0:n, :], ACT.Copy))
                    act.nop().then_inc(act_free, 1)
                    act.nop().then_inc(copied, 1)
                    if u == 3 * NT:
                        evacuate(u - 1)
                    continue
                if u >= 2:
                    act.wait_ge(summed, u - 1)
                if g == 0:
                    act.activation(sq[u % 2][0:n, :], ps[0:n, :], ACT.Square).then_inc(squared, 1)
                elif g == 1:
                    if u >= NT + 2:
                        act.wait_ge(sent[u % 2], 16 * 3 * ((u - NT) // 2))
                    act.activation(kn[u % 2][0:n, P:2 * P], ps[0:n, P:2 * P], ACT.Copy)
                    act.activation(sq[u % 2][0:n, 0:384], ps[0:n, 0:384], ACT.Square).then_inc(squared, 1)
                else:
                    act.activation(s.vkv[0:n, t, :, :], ps[0:n, 0:512].rearrange("p (a c) -> p a c", a=2)[:, :, 0:P],
                                   ACT.Copy)
                    act.activation(s.gates[0:n, t, :], ps[0:n, 384:408], ACT.Exp, scale=-1.0)
                    act.activation(sq[u % 2][0:n, 0:P], ps[0:n, P:2 * P], ACT.Square).then_inc(squared, 1)
                act.wait_ge(squared, u + 1)
                act.nop().then_inc(act_free, 1)
                act.nop().then_inc(copied, 1)
                if u >= 1:
                    evacuate(u - 1)
                act.wait_ge(summed, u + 1)
                st = stat[u % 2]
                ch.link(act, act.activation(st[0:n, 8:16], st[0:n, 0:8], ACT.Ln, bias=s.eps[0:n, 0:1],
                                            scale=1.0 / HD))
                act.activation(st[0:n, 16:24], st[0:n, 8:16], ACT.Exp, scale=-0.5).then_inc(rstd_ready, 1)

        @block.vector
        def _(v):
            ch = s.dve_chain
            for i in range(2):
                ch.link(v, v.memset(stat[i], 1.0))
            ch.link(v, v.tensor_scalar(s.gain[:, 0, :], s.gain[:, 0, :], SCALE, None, ALU.mult))
            for u in range(3 * NT):
                g, t = u // NT, u % NT
                n = rows_of(t)
                ps, st, sqt = s.ps[u % n_psum], stat[u % 2], sq[u % 2]
                if g == 0:
                    kinds, heads, gain, out = NG, HPG, 0, qn[u % 2]
                elif g == 1:
                    kinds, heads, gain, out = 2, NG, 1, kn[u % 2]
                else:
                    kinds, heads, gain, out = 1, NG, 3, kn[u % 2]

                def parts(tile, at=0):
                    if g == 1:
                        return tile[0:n, 0:384].rearrange("p (k h d) -> p k h d", k=3, d=HD)[:, 0:3:2]
                    return tile[0:n, at:at + kinds * heads * HD].rearrange("p (k h d) -> p k h d", k=kinds, d=HD)
                v.wait_ge(squared, u + 1)
                sums = st[0:n, 0:kinds * heads].rearrange("p (k h) -> p k h", k=kinds)
                v.tensor_reduce(sums, parts(sqt), AX.X, ALU.add).then_inc(summed, 1)
                v.wait_ge(rstd_ready, u + 1)
                shape = (n, kinds, heads, HD)
                rstd = st[0:n, 16:16 + kinds * heads].rearrange("p (k h) -> p k h", k=kinds).unsqueeze(3)
                dst = parts(out) if g else out[0:n, :].rearrange("p (h k d) -> p k h d", k=NG, d=HD)
                if u >= 2:
                    v.wait_ge(turned, u - 1)
                if g >= 1 and u >= NT + 2:
                    done = sum((3 if w < 2 * NT else w % NT >= TT - WIN // P)
                               for w in range(NT, u - 1) if w % 2 == u % 2)
                    v.wait_ge(sent[u % 2], 16 * done)
                ch.link(v, v.tensor_tensor(dst, parts(ps, P if g == 2 else 0), bc(rstd, shape), ALU.mult))
                v.nop().then_inc(dve_free, 1)
                for kd in range(kinds):
                    row = s.gain[0:n, gain + (kd if g else 0), :].unsqueeze(1)
                    last = v.tensor_tensor(dst[:, kd], dst[:, kd], bc(row, (n, heads, HD)), ALU.mult)
                ch.link(v, last)
                for kd in range(kinds):
                    x = dst[:, kd, :, 0:16]
                    a, b = (r[0:n, kd * 128:kd * 128 + heads * 16].rearrange("p (h c) -> p h c", c=16) for r in rot)
                    v.tensor_tensor(a, x, bc(s.rope[0:n, t, 0:16].unsqueeze(1), (n, heads, 16)), ALU.mult)
                    ch.link(v, v.tensor_tensor(b, x, bc(s.rope[0:n, t, 16:32].unsqueeze(1), (n, heads, 16)), ALU.mult))
                    v.tensor_tensor(x[:, :, 0:8], a[:, :, 0:8], b[:, :, 8:16], ALU.subtract)
                    ch.link(v, v.tensor_tensor(x[:, :, 8:16], a[:, :, 8:16], b[:, :, 0:8], ALU.add))
                if g == 2:
                    ga = s.gates[0:n, t, :]
                    ch.link(v, v.tensor_scalar(ga, ga, 1.0, None, ALU.add))
                    ch.link(v, v.reciprocal(ga, ga))
                v.nop().then_inc(normed, 1)
            for u in range(3 * NT, UNITS):
                v.nop().then_inc(dve_free, 1)


def wait(eng, sem, value):
    if not isinstance(value, int) or value > 0:
        eng.wait_ge(sem, value)


def stage_compress(nc, s, T):
    rows = [view(s.ring, 2048 * a, CMP_STRIDE, P) for a in range(2)]
    pairs = [view(s.ring, 4096 + 2048 * a, NG, 8, P) for a in range(2)]
    w1 = view(s.work, X3 + 1888, 2, 8, 2 * HD)
    w2 = view(s.work, 24392, 3, HD)
    pe_rows = view(s.work, X3 + 128, P)
    peT = view(s.work, X3 + 256, 2, 2, 8)
    pe_h = view(s.work, X3 + 288, 2)
    lifted = [view(s.work, X3 + 320 + 256 * a, NG, P) for a in range(2)]
    hid = [view(s.work, X3 + 832 + 256 * a, NG, P) for a in range(2)]
    act_h = [view(s.work, X3 + 1344 + 256 * a, NG, P) for a in range(2)]
    pages = view(s.work, X3 + 1856, NB)
    pages_f = view(s.work, X3 + 1864, NB)
    sub = view(s.work, X3 + 1872, 1)
    small, idx_ready = s.sem("c_small"), s.sem("c_idx")
    rows_in = [s.sem(f"c_rows{a}") for a in range(2)]
    prompt_in = [s.sem(f"c_prompt{a}") for a in range(2)]
    turned, mixed, made = s.sem("c_turned"), s.sem("c_mixed"), s.sem("c_made")
    evac_a, evac_v = s.sem("c_evac_a"), s.sem("c_evac_v")
    lift, summed, gelu, placed = s.sem("c_lift"), s.sem("c_summed"), s.sem("c_gelu"), s.sem("c_placed")
    pe_terms, pe_read = s.sem("c_pe_terms"), s.sem("c_pe_read")

    def pipeline(eng, first, second, third):
        first(0, 0, NSUB_P)
        first(0, 1, NSUB_P)
        second(0, 0, NSUB_P)
        first(1, 0, NSUB_S)
        second(0, 1, NSUB_P)
        third(0, 0, NSUB_P)
        first(1, 1, NSUB_S)
        second(1, 0, NSUB_S)
        third(0, 1, NSUB_P)
        with eng.Fori(2, NB + 1) as q:
            first(q, 0, NSUB_S)
            second(q - 1, 1, NSUB_S)
            third(q - 1, 0, NSUB_S)
            first(q, 1, NSUB_S)
            second(q, 0, NSUB_S)
            third(q - 1, 1, NSUB_S)
        second(NB, 1, NSUB_S)
        third(NB, 0, NSUB_S)
        third(NB, 1, NSUB_S)

    def nothing(q, a, n):
        pass

    with nc.Block() as block:
        @block.sync
        def _(sp):
            for a in range(2):
                for r in range(2):
                    sp.dma_start(w1[:, a, :, r * HD:(r + 1) * HD],
                                 T["cmp_w1"][0, a, r * 1024:(r + 1) * 1024].rearrange("(e q) h -> q e h", q=P)
                                 ).then_inc(small, 16)
                sp.dma_start(w2[0:HD, a, :], T["cmp_w2"][0, 0]).then_inc(small, 16)
            sp.dma_start(pe_rows[0:32, :], T["cmp_pe"][0].rearrange("a (r q) d -> (a r) (q d)", q=2)).then_inc(small, 16)
            sp.dma_start(w2[0:HD, 2, :], T["cmp_w2"][0, 1]).then_inc(small, 16)
            sp.dma_start(sub, T["c_sub"]).then_inc(small, 16)
            sp.dma_start(pages.bitcast(I32), T["page_rows"]).then_inc(small, 16)
            for a, src in enumerate((T["p_ck"], T["p_cv"])):
                sp.dma_start(rows[a][0:NSUB_P].rearrange("p t c -> p (t c)"),
                             src[0, 0].rearrange("(n t) g d -> n (t g d)", t=CMP_STRIDE)).then_inc(prompt_in[a], 16)

        @block.gpsimd
        def _(pool):
            pool.wait_ge(idx_ready, 1)
            for b in range(NB):
                for a, src in enumerate((T["cache_cmp_k"], T["cache_cmp_v"])):
                    pool.wait_ge(turned, 4 * (2 * b + a) + 4)
                    pool.indirect_dma_start(
                        out=rows[a].rearrange("p t c -> p (t c)"), out_offset=None,
                        in_=src[0].rearrange("n (j t) g d -> (n j) (t g d)", t=CMP_STRIDE),
                        in_offset=bass.IndirectOffsetOnAxis(ap=s.gidx[:, b:b + 1], axis=0)).then_inc(rows_in[a], 16)

        @block.tensor
        def _(pe):
            pe.wait_ge(small, 160)
            pe.transpose(s.ps[6][:, 0:32], pe_rows[0:32, :], s.ident[0:32, 0:32]).then_inc(pe_terms, 1)
            pe.wait_ge(pe_read, 1)
            for a in range(2):
                for r in range(2):
                    for e in range(8):
                        last = pe.matmul(s.ps[7][0:HD, a:a + 1], w1[:, a, e, r * HD:(r + 1) * HD],
                                         peT[:, a, r, e:e + 1], start=(r + e == 0), stop=(r * e == 7))
            last.then_inc(pe_terms, 1)
            pe.wait_ge(pe_read, 2)

            def turn(q, a, n):
                pe.wait_ge(*((prompt_in[a], 16) if isinstance(q, int) and q == 0 else (rows_in[a], 16 * q)))
                for bank in range(4):
                    wait(pe, evac_a if bank % 2 else evac_v, 2 * (2 * q + a - 1) + bank // 2 + 1)
                    for j in range(4):
                        last = pe.transpose(s.ps[bank][:, j * P:j * P + n], rows[a][0:n, 4 * bank + j, :],
                                            s.ident[0:n, 0:n])
                    last.then_inc(turned, 1)

            def mix(q, a, n):
                pe.wait_ge(evac_a, 2 * (2 * q + a) + 2)
                pe.wait_ge(evac_v, 2 * (2 * q + a) + 2)
                wait(pe, summed, 2 * q + a - 1)
                out = view(s.ps[4 + a], 0, NG, P)[:, :, 0:n]
                for e in range(8):
                    last = pe.matmul(out, w1[:, a, e, :], pairs[a][:, :, e, 0:n], start=(e == 0), stop=(e == 7))
                last.then_inc(mixed, 1)

            def make(q, a, n):
                m = n - 1
                pe.wait_ge(gelu, 2 * q + a + 1)
                wait(pe, placed, 2 * q + a - 1)
                for g in range(NG):
                    if a == 0:
                        last = pe.matmul(s.ps[6][:, g * P:g * P + m], w2[0:HD, 0:2, :].rearrange("p a d -> p (a d)"),
                                         act_h[0][0:HD, g, 0:m], start=True, stop=True)
                    else:
                        last = pe.matmul(s.ps[7][0:m, g * HD:(g + 1) * HD], act_h[1][0:HD, g, 0:m], w2[0:HD, 2, :],
                                         start=True, stop=True)
                last.then_inc(made, 1)

            pipeline(pe, turn, mix, make)

        def evacuate(eng, copy, done, banks):
            def run(q, a, n):
                wait(eng, mixed, 2 * q + a - 1)
                for bank in banks:
                    eng.wait_ge(turned, 4 * (2 * q + a) + bank + 1)
                    src = view(s.ps[bank], 0, 2, 2, P)
                    for s2 in range(2):
                        for g in range(NG):
                            last = copy(pairs[a][s2 * HD:(s2 + 1) * HD, g, 2 * bank:2 * bank + 2, 0:n],
                                        src[g * HD:(g + 1) * HD, :, s2, 0:n])
                    last.then_inc(done, 1)
            return run

        @block.scalar
        def _(act):
            act.wait_ge(pe_terms, 1)

            def lift_gelu(q, a, n):
                m = n - 1
                act.wait_ge(mixed, 2 * q + a + 1)
                wait(act, summed, 2 * q + a - 1)
                src = view(s.ps[4 + a], 0, NG, P)
                act.activation(lifted[a][0:HD, :, 0:m], src[HD:P, :, 1:n], ACT.Identity,
                               bias=pe_h[0:HD, a:a + 1]).then_inc(lift, 1)
                act.wait_ge(summed, 2 * q + a + 1)
                wait(act, made, 2 * q + a - 1)
                act.activation(act_h[a][0:HD, :, 0:m], hid[a][0:HD, :, 0:m], ACT.Gelu_apprx_tanh).then_inc(gelu, 1)

            act.wait_ge(pe_read, 2)
            pipeline(act, evacuate(act, lambda o, i: act.activation(o, i, ACT.Copy), evac_a, (1, 3)), lift_gelu, nothing)

        @block.vector
        def _(v):
            ch = s.dve_chain
            v.wait_ge(small, 160)
            ch.link(v, v.tensor_copy(pages_f, pages.bitcast(I32)))
            ch.link(v, v.tensor_scalar(pages_f, pages_f, float(SUB_PER_PAGE), sub[:, 0:1], ALU.mult, ALU.add))
            v.tensor_copy(s.gidx[:, :], pages_f).then_inc(idx_ready, 1)
            v.wait_ge(pe_terms, 1)
            v.tensor_copy(view(s.work, X3 + 256, 32), s.ps[6][:, 0:32]).then_inc(pe_read, 1)
            v.wait_ge(pe_terms, 2)
            v.tensor_copy(pe_h[0:HD, :], s.ps[7][0:HD, 0:2]).then_inc(pe_read, 1)

            def add(q, a, n):
                m = n - 1
                v.wait_ge(lift, 2 * q + a + 1)
                wait(v, gelu, 2 * q + a - 1)
                src = view(s.ps[4 + a], 0, NG, P)
                v.tensor_tensor(hid[a][0:HD, :, 0:m], src[0:HD, :, 0:m], lifted[a][0:HD, :, 0:m],
                                ALU.add).then_inc(summed, 1)

            def place(q, a, n):
                m = n - 1
                v.wait_ge(made, 2 * q + a + 1)
                if a == 0:
                    keys = s.kcT.rearrange("p q n -> p (q n)")
                    for g in range(NG):
                        half = slice(g * HD, (g + 1) * HD)
                        last = v.tensor_copy(keys[half, bass.ds(q * P, m)], s.ps[6][half, g * P:g * P + m])
                else:
                    values = s.vc.rearrange("p q n -> p (q n)")
                    last = v.tensor_copy(values[0:m, bass.ds(q * P, P)], s.ps[7][0:m, 0:P])
                last.then_inc(placed, 1)

            pipeline(v, evacuate(v, v.tensor_copy, evac_v, (0, 2)), add, place)


def stage_prompt_attention(nc, s, T):
    prob = [view(s.ring, 1024 * i, 1024) for i in range(2)]
    probT = [view(s.ring, 2048 + 1024 * i, 1024) for i in range(2)]
    o_tm = [view(s.ring, 4096 + 512 * i, 512) for i in range(2)]
    part = view(s.ring, 5120, 512)
    top = view(s.ring, 5632, 2, 8)
    total = view(s.ring, 5648, 4, 8)
    coef = view(s.ring, 5680, 8)
    cmp_add = view(s.work, 23880, 256).bitcast(BF16).rearrange("p (t n) -> p t n", t=TT)
    cmp_add_f = view(s.ring, 6144, TT, HD)
    cmp_mul = view(s.ring, 6656, TT, HD)
    score = [s.psall[:, 1024 * i:1024 * (i + 1)] for i in range(2)]
    turn_ps = [s.ps[4], s.ps[5]]
    out_ps = [s.ps[6], s.ps[7]]
    masks_in, mask_cast = s.sem("a_masks"), s.sem("a_mask_cast")
    scored, maxed, exped, masked = s.sem("a_scored"), s.sem("a_maxed"), s.sem("a_exped"), s.sem("a_masked")
    turned, pv, combined = s.sem("a_turned"), s.sem("a_pv"), s.sem("a_combined")
    moved = [s.sem("a_moved_v"), s.sem("a_moved_a")]

    units = []
    for t in range(TT):
        units.append(Unit(kind=0, t=t, h=0, lo=0, n=TT // 2, last=True))
        for kind in (1, 2):
            for h in range(NH):
                lo = 0 if kind == 1 else max(0, t - WIN // P)
                units.append(Unit(kind=kind, t=t, h=h, lo=lo, n=t + 1 - lo, last=h == NH - 1))
        if t:
            units.insert(len(units) - 8, Unit(kind=3, t=t - 1, h=0, lo=0, n=4, last=False))
    units.append(Unit(kind=3, t=TT - 1, h=0, lo=0, n=4, last=False))
    chunk = real = 0
    for u in units:
        u.chunks = []
        width = 8 if u.kind == 0 else u.n
        for c0 in range(0, width, 4):
            u.chunks.append((chunk, c0, min(4, width - c0)))
            chunk += 1
        u.branch = 3 * u.t + u.kind
        if u.kind < 3:
            u.i = real
            real += 1
    scored_units = [u for u in units if u.kind < 3]

    def done_chunks(c):
        return c // 2 + 1

    def steps():
        ahead = 2
        for u in units:
            nxt = None
            if u.kind < 3:
                nxt = scored_units[ahead] if ahead < len(scored_units) else None
                ahead += 1
            yield u, nxt

    with nc.Block() as block:
        @block.sync
        def _(sp):
            sp.dma_start(cmp_add_f, T["c_cmp_add"]).then_inc(masks_in, 16)
            sp.dma_start(cmp_mul, T["c_cmp_mul"]).then_inc(masks_in, 16)

        @block.tensor
        def _(pe):
            def scores(u):
                wait(pe, exped, u.i - 1)
                ps = score[u.i % 2]
                if u.kind == 0:
                    for g in range(NG):
                        pe.matmul(ps[:, 512 * g:512 * g + 256], s.identb[:, :],
                                  bc(cmp_add[:, u.t, :].unsqueeze(1), (P, HPG, HD)), start=True, stop=False)
                    for j in range(HPG):
                        for g in range(NG):
                            last = pe.matmul(ps[:, 512 * g + j * HD:512 * g + j * HD + NC_P],
                                             s.qT[g * HD:(g + 1) * HD, j, u.t * P:(u.t + 1) * P],
                                             s.kcT[g * HD:(g + 1) * HD, 0, 0:NC_P], start=False,
                                             stop=(j == HPG - 1))
                else:
                    g, j = u.h // HPG, u.h % HPG
                    keys = s.ksT if u.kind == 1 else s.kwT
                    for c0 in range(0, u.n, 4):
                        c1 = min(u.n, c0 + 4)
                        diag = c1 == u.n
                        far = u.kind == 2 and u.t >= WIN // P and c0 == 0
                        last = pe.matmul(ps[:, c0 * P:c1 * P], s.qT[g * HD:(g + 1) * HD, j, u.t * P:(u.t + 1) * P],
                                         keys[g * HD:(g + 1) * HD, (u.lo + c0) * P:(u.lo + c1) * P],
                                         start=True, stop=not (diag or far))
                        if far:
                            last = pe.matmul(ps[:, 0:P], s.identb[:, :], s.add[:, 1, :], start=False, stop=not diag)
                        if diag:
                            last = pe.matmul(ps[:, (u.n - 1) * P:u.n * P], s.identb[:, :], s.add[:, 0, :],
                                             start=False, stop=True)
                last.then_inc(scored, 1)

            pe.wait_ge(mask_cast, 1)
            scores(scored_units[0])
            scores(scored_units[1])
            for u, nxt in steps():
                if u.kind == 3:
                    pe.wait_ge(combined, 3 * u.t + 3)
                elif u.kind == 0:
                    pe.wait_ge(masked, u.t + 1)
                else:
                    pe.wait_ge(exped, u.i + 1)
                for c, c0, n in u.chunks:
                    wait(pe, moved[c % 2], done_chunks(c) - 1)
                    out = turn_ps[c % 2]
                    for k in range(n):
                        if u.kind == 0:
                            h = c0 + k
                            last = pe.transpose(out[0:NC_P, k * P:(k + 1) * P], prob[u.i % 2][:, h * HD:h * HD + NC_P],
                                                s.ident[:, :])
                        else:
                            src = o_tm[u.t % 2] if u.kind == 3 else prob[u.i % 2]
                            last = pe.transpose(out[:, k * P:(k + 1) * P], src[:, (c0 + k) * P:(c0 + k + 1) * P],
                                                s.ident[:, :])
                    last.then_inc(turned, 1)
                if nxt:
                    scores(nxt)
                if u.kind == 3:
                    continue
                for c, c0, n in u.chunks:
                    pe.wait_ge(moved[c % 2], done_chunks(c))
                out = out_ps[u.branch % 2]
                if u.h == 0:
                    wait(pe, combined, u.branch - 1)
                if u.kind == 0:
                    for h in range(NH):
                        g = h // HPG
                        last = pe.matmul(out[:, h * HD:(h + 1) * HD], probT[u.i % 2][0:NC_P, h * P:(h + 1) * P],
                                         s.vc[0:NC_P, 0, g * HD:(g + 1) * HD], start=True, stop=True)
                else:
                    g = u.h // HPG
                    for k in range(u.n):
                        last = pe.matmul(out[:, u.h * HD:(u.h + 1) * HD], probT[u.i % 2][:, k * P:(k + 1) * P],
                                         s.vkv[:, u.lo + k, u.kind - 1, g * HD:(g + 1) * HD],
                                         start=(k == 0), stop=(k == u.n - 1))
                last.then_inc(pv, 1)

        def copy_chunks(eng, copy, which, u):
            for c, c0, n in u.chunks:
                if c % 2 != which:
                    continue
                eng.wait_ge(turned, c + 1)
                if u.kind == 3:
                    copy(s.oN[:, :, u.t * P:(u.t + 1) * P], view(turn_ps[which], 0, 4, P)).then_inc(moved[which], 1)
                    continue
                wait(eng, pv, u.i - 1)
                rows = NC_P if u.kind == 0 else P
                copy(probT[u.i % 2][0:rows, c0 * P:(c0 + n) * P],
                     turn_ps[which][0:rows, 0:n * P]).then_inc(moved[which], 1)

        @block.scalar
        def _(act):
            def exps(u):
                act.wait_ge(maxed, u.i + 1)
                if u.kind == 0:
                    act.activation(prob[u.i % 2][:, 0:512], prob[u.i % 2][:, 0:512], ACT.Exp).then_inc(exped, 1)
                else:
                    before = [w for w in scored_units if w.i == u.i - 2]
                    if before:
                        act.wait_ge(turned, before[0].chunks[-1][0] + 1)
                    act.activation(prob[u.i % 2][:, 0:u.n * P], score[u.i % 2][:, 0:u.n * P], ACT.Exp,
                                   bias=top[:, u.i % 2, 0:1],
                                   accum_out=total[:, u.branch % 4, u.h:u.h + 1]).then_inc(exped, 1)

            exps(scored_units[0])
            exps(scored_units[1])
            for u, nxt in steps():
                copy_chunks(act, lambda o, i: act.activation(o, i, ACT.Copy), 1, u)
                if nxt:
                    exps(nxt)

        @block.vector
        def _(v):
            ch = s.dve_chain

            def maxima(u):
                v.wait_ge(scored, u.i + 1)
                ps, pr = score[u.i % 2], prob[u.i % 2]
                wait(v, exped, u.i - 1)
                if u.kind:
                    v.tensor_reduce(top[:, u.i % 2, 0:1], ps[:, 0:u.n * P], AX.X, ALU.max,
                                    negate=True).then_inc(maxed, 1)
                    return
                before = [w for w in scored_units if w.i == u.i - 2]
                if before:
                    v.wait_ge(turned, before[0].chunks[-1][0] + 1)
                by_group = lambda x: x.rearrange("p (g j n) -> p g j n", g=NG, n=HD)
                heads = ps.rearrange("p (g j n) -> p g j n", g=NG, n=HD)[:, :, 0:HPG]
                most = top[:, u.i % 2, :].rearrange("p (g j) -> p g j", g=NG)
                ch.link(v, v.tensor_reduce(most, heads, AX.X, ALU.max))
                v.tensor_tensor(by_group(pr[:, 0:512]), heads, bc(most.unsqueeze(3), (P, NG, HPG, HD)),
                                ALU.subtract).then_inc(maxed, 1)
                v.wait_ge(exped, u.i + 1)
                e = pr[:, 0:512].rearrange("p (h n) -> p h n", h=NH)
                ch.link(v, v.tensor_tensor(e, e, bc(cmp_mul[:, u.t, :].unsqueeze(1), (P, NH, HD)), ALU.mult))
                ch.link(v, v.tensor_reduce(total[:, u.branch % 4, :], e, AX.X, ALU.add))
                v.tensor_scalar(total[:, u.branch % 4, :], total[:, u.branch % 4, :], 1e-30, None,
                                ALU.max).then_inc(masked, 1)

            def combine(u):
                v.wait_ge(pv, u.i + 1)
                ch.link(v, v.reciprocal(coef, total[:, u.branch % 4, :]))
                gate = s.gates[:, u.t, :].rearrange("p (h c) -> p h c", c=3)[:, :, u.kind]
                ch.link(v, v.tensor_tensor(coef, coef, gate, ALU.mult))
                src = out_ps[u.branch % 2].rearrange("p (g j d) -> p g j d", g=NG, d=HD)
                pairs = lambda x: x.rearrange("p (j g d) -> p g j d", g=NG, d=HD)
                by = bc(coef.rearrange("p (g j) -> p g j", g=NG).unsqueeze(3), (P, NG, HPG, HD))
                if u.kind == 0:
                    if u.t >= 2:
                        old = [w for w in units if w.kind == 3 and w.t == u.t - 2][0]
                        v.wait_ge(turned, old.chunks[-1][0] + 1)
                    v.tensor_tensor(pairs(o_tm[u.t % 2]), src, by, ALU.mult).then_inc(combined, 1)
                else:
                    v.wait_ge(combined, u.branch)
                    ch.link(v, v.tensor_tensor(pairs(part), src, by, ALU.mult))
                    v.tensor_tensor(o_tm[u.t % 2], o_tm[u.t % 2], part, ALU.add).then_inc(combined, 1)

            v.wait_ge(masks_in, 32)
            v.tensor_copy(cmp_add, cmp_add_f).then_inc(mask_cast, 1)
            maxima(scored_units[0])
            maxima(scored_units[1])
            pending = None
            for u, nxt in steps():
                copy_chunks(v, v.tensor_copy, 0, u)
                if nxt:
                    maxima(nxt)
                if pending:
                    combine(pending)
                    pending = None
                if u.last:
                    pending = u
                    if u.kind == 2 and u.t == TT - 1:
                        combine(u)
                        pending = None


def stage_decode_attention(nc, s, T):
    ROWS = NB * NH
    key_rows = [view(s.ring, 2048 * i, 16, P) for i in range(2)]
    val_rows = [view(s.ring, 4096 + 2048 * i, 16, P) for i in range(2)]
    win_keys = [view(s.ring, 512 * b, 4, P) for b in range(NB)]
    win_vals = [view(s.ring, 4096 + 512 * b, 4, P) for b in range(NB)]
    keysT = [view(s.work, 8256 + 2048 * i, 16, P) for i in range(2)]
    win_keysT = [view(s.work, 8256 + 512 * b, 4, P) for b in range(NB)]
    scT = view(s.work, 12384, 16, ROWS)
    prT = view(s.work, 13408, 16, ROWS)
    rows = view(s.work, X3, 2048)[0:ROWS]
    Y = X3 + 2048
    qbd = view(s.work, Y, ROWS)
    knew = view(s.work, Y + 64, 2, NB)
    gate = view(s.work, Y + 80, 3)[0:ROWS]
    own = view(s.work, Y + 88, NB)[0:ROWS]
    over = view(s.work, Y + 96, NS_S)
    st = view(s.work, Y + 136, 16)[0:ROWS]
    cmp_rows = view(s.work, Y + 152, P)[0:ROWS]
    cmp_pT = view(s.work, Y + 280, ROWS)
    cmp_sc = view(s.work, Y + 344, ROWS)
    imp = view(s.work, Y + 408, NS_S)[0:ROWS]
    grp = view(s.work, Y + 448, NB * NG)
    grp_all = view(s.work, Y + 464, ROWS)
    pen = view(s.work, Y + 528, NS_S)[0:ROWS]
    new_d = view(s.work, Y + 568, NB)[0:ROWS]
    new_dT = view(s.work, Y + 576, 2, ROWS)
    gt = view(s.work, 23880, NS_S * NS_S)[0:ROWS]
    eq = view(s.work, Y + 704, NS_S * NS_S)[0:ROWS]
    lower = view(s.work, 14448, NS_S * NS_S)[0:ROWS]
    small, q_ready = s.sem("d_small"), s.sem("d_q_ready")
    k_in = [s.sem(f"d_k{i}") for i in range(2)]
    v_in = [s.sem(f"d_v{i}") for i in range(2)]
    wk_in, wv_in = s.sem("d_wk"), s.sem("d_wv")
    turned, evac_v, evac_a = s.sem("d_turned"), s.sem("d_evac_v"), s.sem("d_evac_a")
    dotted, dots_read = s.sem("d_dotted"), s.sem("d_dots_read")
    pe_to_v, v_to_pe = s.sem("d_pe_to_v"), s.sem("d_v_to_pe")
    v_to_a, a_to_v = s.sem("d_v_to_a"), s.sem("d_a_to_v")
    vals_used = s.sem("d_vals_used")
    O = s.ps[7]

    with nc.Block() as block:
        @block.sync
        def _(sp):
            sp.dma_start(gate, T["gate_rows"].rearrange("b (h c) -> (b h) c", c=3)).then_inc(small, 16)
            sp.dma_start(own, T["c_own"]).then_inc(small, 16)
            sp.dma_start(over[0:NC_S], T["c_over"]).then_inc(small, 16)
            sp.dma_start(lower, T["c_lower"]).then_inc(small, 16)
            sp.wait_ge(turned, 4 * NB)
            for b in range(NB):
                sp.dma_start(win_keys[b], T["cache_win_k"][0, b].rearrange("(p t) g d -> p t (g d)", t=4)).then_inc(wk_in, 16)
            sp.wait_ge(vals_used, NB)
            for b in range(NB):
                sp.dma_start(win_vals[b], T["cache_win_v"][0, b].rearrange("(p t) g d -> p t (g d)", t=4)).then_inc(wv_in, 16)

        @block.gpsimd
        def _(pool):
            def gather(dst, src, b, done):
                pool.indirect_dma_start(
                    out=dst.rearrange("p t c -> p (t c)"), out_offset=None,
                    in_=src[0].rearrange("n (j t) g d -> (n j) (t g d)", t=CMP_STRIDE),
                    in_offset=bass.IndirectOffsetOnAxis(ap=s.gidx[:, b:b + 1], axis=0)).then_inc(done, 16)

            for b in range(2):
                gather(key_rows[b], T["cache_slc_k"], b, k_in[b])
            for b in range(2):
                gather(val_rows[b], T["cache_slc_v"], b, v_in[b])
            for b in range(2, NB):
                pool.wait_ge(turned, 4 * (b - 1))
                gather(key_rows[b % 2], T["cache_slc_k"], b, k_in[b % 2])
            for b in range(2, NB):
                pool.wait_ge(vals_used, b - 1)
                gather(val_rows[b % 2], T["cache_slc_v"], b, v_in[b % 2])

        @block.tensor
        def _(pe):
            to_v = [0]

            def signal(ins):
                to_v[0] += 1
                ins.then_inc(pe_to_v, 1)

            pe.wait_ge(q_ready, 1)
            for b in range(NB):
                last = pe.matmul(s.ps[6][0:NC_S, b * NH:(b + 1) * NH], s.kcT[:, 1 + b, 0:NC_S],
                                 qbd[:, b * NH:(b + 1) * NH], start=True, stop=True)
            signal(last)
            pe.wait_ge(v_to_pe, 1)
            signal(pe.transpose(s.ps[5][0:ROWS, 0:NC_S], cmp_sc[0:NC_S, :], s.ident[0:NC_S, 0:NC_S]))
            for kind in range(2):
                last = pe.matmul(s.ps[4][0:ROWS, kind * NB:(kind + 1) * NB], qbd, knew[:, kind, :],
                                 start=True, stop=True)
            signal(last)

            def turn_keys(src, chunks, first):
                for c in range(chunks):
                    for k in range(4):
                        last = pe.transpose(s.ps[(first + c) % 4][:, k * P:(k + 1) * P], src[:, 4 * c + k, :], s.ident[:, :])
                    last.then_inc(turned, 1)

            def dots(keys, n, b, slot):
                for k in range(n):
                    last = pe.matmul(s.ps[5 + slot % 2][:, k * NH:(k + 1) * NH], keys[:, k, :],
                                     qbd[:, bass.ds(b * NH, NH)], start=True, stop=True)
                last.then_inc(dotted, 1)

            pe.wait_ge(v_to_pe, 2)
            signal(pe.transpose(s.ps[6][0:NC_S, 0:ROWS], cmp_rows[:, 0:NC_S], s.ident[0:ROWS, 0:ROWS]))
            pe.wait_ge(v_to_pe, 3)
            pe.matmul(s.ps[6][0:ROWS, 128:128 + NS_S], grp_all[0:NC_S, :], over[0:NC_S, :],
                      start=True, stop=True)
            signal(pe.transpose(s.ps[6][0:NC_S, 256:256 + ROWS], cmp_rows[:, 0:NC_S], s.ident[0:ROWS, 0:ROWS]))
            pe.wait_ge(v_to_pe, 4)
            with pe.Fori(0, NB // 2) as i:
                for h in range(2):
                    b = 2 * i + h
                    pe.wait_ge(k_in[h], 16 * i + 16)
                    turn_keys(key_rows[h], 4, 0)
                    pe.wait_ge(evac_v, 2 * b + 2)
                    pe.wait_ge(evac_a, 2 * b + 2)
                    pe.wait_ge(dots_read, b + 1)
                    dots(keysT[h], 16, b, h)

            def to_rows(n):
                for k in range(n):
                    last = pe.transpose(s.ps[k // 4][0:ROWS, (k % 4) * P:(k % 4 + 1) * P], scT[:, k, :], s.ident[:, :])
                signal(last)

            def to_keys(n):
                for k in range(n):
                    last = pe.transpose(s.ps[k // 8][:, (k % 8) * ROWS:(k % 8 + 1) * ROWS],
                                        rows[:, k * P:(k + 1) * P], s.ident[0:ROWS, 0:ROWS])
                last = pe.transpose(s.ps[4][0:NB, 0:ROWS], new_d, s.ident[0:ROWS, 0:ROWS])
                signal(last)

            pe.wait_ge(dots_read, NB + 1)
            to_rows(16)
            pe.wait_ge(v_to_pe, 5)
            to_keys(16)
            pe.wait_ge(v_to_pe, 6)
            pe.wait_ge(wk_in, 16 * NB)
            for b in range(NB):
                if b >= 4:
                    pe.wait_ge(evac_a if b % 2 else evac_v, 2 * NB + (b - 4) // 2 + 1)
                turn_keys(win_keys[b], 1, b)
            pe.matmul(O[:, 0:ROWS], s.vkv[0:NB, TT, 0, :], new_dT[0:NB, 0, :], start=True, stop=False,
                      skip_group_check=True)
            for b in range(NB):
                pe.matmul(O[:, b * NH:(b + 1) * NH], s.vc[0:NC_S, 1 + b, :], cmp_pT[0:NC_S, b * NH:(b + 1) * NH],
                          start=False, stop=False, skip_group_check=True)
            with pe.Fori(0, NB // 2) as i:
                for h in range(2):
                    b = 2 * i + h
                    pe.wait_ge(v_in[h], 16 * i + 16)
                    for k in range(16):
                        last = pe.matmul(O[:, bass.ds(b * NH, NH)], val_rows[h][:, k, :],
                                         prT[:, k, bass.ds(b * NH, NH)], start=False, stop=False,
                                         skip_group_check=True)
                    last.then_inc(vals_used, 1)
            pe.wait_ge(evac_v, 2 * NB + NB // 2)
            pe.wait_ge(evac_a, 2 * NB + NB // 2)
            for b in range(NB):
                pe.wait_ge(dots_read, NB + b + 1)
                dots(win_keysT[b], 4, b, b)
            pe.wait_ge(dots_read, 2 * NB + 1)
            to_rows(4)
            pe.wait_ge(v_to_pe, 7)
            to_keys(4)
            pe.wait_ge(v_to_pe, 8)
            pe.wait_ge(wv_in, 16 * NB)
            pe.matmul(O[:, 0:ROWS], s.vkv[0:NB, TT, 1, :], new_dT[0:NB, 1, :], start=False, stop=False,
                      skip_group_check=True)
            for b in range(NB):
                for k in range(4):
                    last = pe.matmul(O[:, b * NH:(b + 1) * NH], win_vals[b][:, k, :], prT[:, k, b * NH:(b + 1) * NH],
                                     start=False, stop=(b == NB - 1 and k == 3), skip_group_check=True)
            signal(last)

        def copy_keys(eng, copy, done, odd, then):
            with eng.Fori(0, NB // 2) as i:
                for h in range(2):
                    b = 2 * i + h
                    for c in (odd, odd + 2):
                        eng.wait_ge(turned, 4 * b + c + 1)
                        copy(keysT[h][:, 4 * c:4 * c + 4, :], view(s.ps[c], 0, 4, P)).then_inc(done, 1)
                    then(b, h)

        def copy_window(eng, copy, done, odd):
            for b in range(odd, NB, 2):
                eng.wait_ge(turned, 4 * NB + b + 1)
                copy(win_keysT[b], view(s.ps[b % 4], 0, 4, P)).then_inc(done, 1)

        @block.scalar
        def _(act):
            ch = s.act_chain
            exps = [0]

            def exp_rows(weights, bias, total, new):
                exps[0] += 1
                act.wait_ge(v_to_a, exps[0])
                ch.link(act, act.activation(weights, weights, ACT.Exp, bias=bias, accum_out=total))
                if new is not None:
                    ch.link(act, act.activation(new, new, ACT.Exp, bias=bias))
                act.nop().then_inc(a_to_v, 1)

            exp_rows(cmp_rows[:, 0:NC_S], st[:, 1:2], st[:, 2:3], None)
            copy_keys(act, lambda o, i: act.activation(o, i, ACT.Copy), evac_a, 1, lambda b, h: None)
            exp_rows(rows[:, 0:2048], st[:, 5:6], st[:, 6:7], st[:, 3:4])
            copy_window(act, lambda o, i: act.activation(o, i, ACT.Copy), evac_a, 1)
            exp_rows(rows[:, 0:512], st[:, 5:6], st[:, 6:7], st[:, 4:5])

        @block.vector
        def _(v):
            ch = s.dve_chain
            from_pe, from_a = [0], [0]

            def pe_done():
                from_pe[0] += 1
                v.wait_ge(pe_to_v, from_pe[0])

            def act_done():
                from_a[0] += 1
                v.wait_ge(a_to_v, from_a[0])

            v.sem_inc(dots_read, 1)
            ch.link(v, v.memset(qbd, 0.0))
            for g in range(NG):
                half = slice(g * HD, (g + 1) * HD)
                last = v.tensor_copy(qbd[half].rearrange("p (b g j) -> p b g j", g=NG, j=HPG)[:, :, g, :],
                                     s.qT[half, :, SEQ:TOK].rearrange("p j b -> p b j"))
            v.tensor_copy(knew[:, 0, :], s.ksT[:, SEQ:TOK])
            ch.link(v, v.tensor_copy(knew[:, 1, :], s.kwT[:, SEQ:TOK]))
            v.nop().then_inc(q_ready, 1)
            v.wait_ge(small, 64)
            pe_done()
            v.tensor_copy(cmp_sc[0:NC_S, :], s.ps[6][0:NC_S, 0:ROWS]).then_inc(v_to_pe, 1)
            pe_done()
            ch.link(v, v.tensor_reduce(st[:, 1:2], s.ps[5][0:ROWS, 0:NC_S], AX.X, ALU.max, negate=True))
            ch.link(v, v.tensor_copy(cmp_rows[:, 0:NC_S], s.ps[5][0:ROWS, 0:NC_S]))
            v.nop().then_inc(v_to_a, 1)
            pe_done()
            for kind in range(2):
                ch.link(v, v.tensor_tensor(new_d, s.ps[4][0:ROWS, kind * NB:(kind + 1) * NB], own, ALU.mult))
                ch.link(v, v.tensor_reduce(st[:, 3 + kind:4 + kind], new_d, AX.X, ALU.add))
            act_done()
            ch.link(v, v.tensor_scalar(st[:, 2:3], st[:, 2:3], 1e-30, None, ALU.max))
            ch.link(v, v.reciprocal(st[:, 2:3], st[:, 2:3]))
            ch.link(v, v.tensor_scalar(cmp_rows[:, 0:NC_S], cmp_rows[:, 0:NC_S], st[:, 2:3], None, ALU.mult))
            v.nop().then_inc(v_to_pe, 1)
            pe_done()
            ch.link(v, v.tensor_copy(cmp_pT[0:NC_S, :], s.ps[6][0:NC_S, 0:ROWS]))
            ch.link(v, v.tensor_reduce(grp[0:NC_S, :], cmp_pT[0:NC_S, :].rearrange("p (x j) -> p x j", j=HPG), AX.X,
                                       ALU.add))
            ch.link(v, v.tensor_copy(grp_all[0:NC_S, :].rearrange("p (x j) -> p x j", j=HPG),
                                     bc(grp[0:NC_S, :].unsqueeze(2), (NC_S, NB * NG, HPG))))
            ch.link(v, v.tensor_scalar(cmp_rows[:, 0:NC_S], cmp_rows[:, 0:NC_S], gate[:, 0:1], None, ALU.mult))
            v.nop().then_inc(v_to_pe, 1)
            pe_done()
            v.tensor_copy(cmp_pT[0:NC_S, :], s.ps[6][0:NC_S, 256:256 + ROWS])
            ch.link(v, v.tensor_copy(imp, s.ps[6][0:ROWS, 128:128 + NS_S]))
            v.memset(imp[:, 0:1], 1e9)
            ch.link(v, v.memset(imp[:, NS_S - 2:NS_S], 1e9))
            square = lambda x: x.rearrange("p (a b) -> p a b", a=NS_S)
            mine, other = bc(imp.unsqueeze(2), (ROWS, NS_S, NS_S)), bc(imp.unsqueeze(1), (ROWS, NS_S, NS_S))
            v.tensor_tensor(square(gt), other, mine, ALU.is_gt)
            ch.link(v, v.tensor_tensor(square(eq), other, mine, ALU.is_equal))
            ch.link(v, v.tensor_tensor(eq, eq, lower, ALU.mult))
            ch.link(v, v.tensor_tensor(gt, gt, eq, ALU.add))
            ch.link(v, v.tensor_reduce(pen, square(gt), AX.X, ALU.add))
            ch.link(v, v.tensor_scalar(pen, pen, NSEL - 0.5, NEG, ALU.is_gt, ALU.mult))
            v.nop().then_inc(v_to_pe, 1)

            def take_scores(b, h):
                v.wait_ge(dotted, b + 1)
                v.tensor_copy(scT[:, :, bass.ds(b * NH, NH)], view(s.ps[5 + h], 0, 16, NH)).then_inc(dots_read, 1)

            copy_keys(v, v.tensor_copy, evac_v, 0, take_scores)

            def softmax_rows(n, kind, mask):
                pe_done()
                mask()
                new = st[:, 2 + kind:3 + kind]
                ch.link(v, v.tensor_reduce(st[:, 5:6], rows[:, 0:n], AX.X, ALU.max))
                ch.link(v, v.tensor_tensor(st[:, 5:6], st[:, 5:6], new, ALU.max))
                ch.link(v, v.tensor_scalar(st[:, 5:6], st[:, 5:6], -1.0, None, ALU.mult))
                v.nop().then_inc(v_to_a, 1)
                act_done()
                ch.link(v, v.tensor_tensor(st[:, 6:7], st[:, 6:7], new, ALU.add))
                ch.link(v, v.reciprocal(st[:, 6:7], st[:, 6:7]))
                ch.link(v, v.tensor_tensor(st[:, 6:7], st[:, 6:7], gate[:, kind:kind + 1], ALU.mult))
                v.tensor_scalar(rows[:, 0:n], rows[:, 0:n], st[:, 6:7], None, ALU.mult)
                ch.link(v, v.tensor_tensor(new, new, st[:, 6:7], ALU.mult))
                ch.link(v, v.tensor_scalar(new_d, own, new, None, ALU.mult))
                v.nop().then_inc(v_to_pe, 1)
                pe_done()
                for half in range((n // P + 7) // 8):
                    k = min(8, n // P)
                    v.tensor_copy(prT[:, 8 * half:8 * half + k, :], view(s.ps[half], 0, 8, ROWS)[:, 0:k])
                ch.link(v, v.tensor_copy(new_dT[0:NB, kind - 1, :], s.ps[4][0:NB, 0:ROWS]))
                v.nop().then_inc(v_to_pe, 1)

            def select():
                blocks = lambda x: x.rearrange("p (t m e) -> p t m e", t=16, m=32)
                ch.link(v, v.tensor_tensor(blocks(rows), blocks(s.psall[0:ROWS, 0:2048]),
                                           bc(pen[:, 0:32].unsqueeze(1).unsqueeze(3), (ROWS, 16, 32, 4)), ALU.add))

            def window():
                ch.link(v, v.tensor_copy(rows[:, 0:512], s.psall[0:ROWS, 0:512]))
                ch.link(v, v.memset(rows[:, 0:1], NEG))

            softmax_rows(2048, 1, select)
            copy_window(v, v.tensor_copy, evac_v, 0)
            for b in range(NB):
                v.wait_ge(dotted, NB + b + 1)
                v.tensor_copy(scT[:, 0:4, b * NH:(b + 1) * NH], view(s.ps[5 + b % 2], 0, 4, NH)).then_inc(dots_read, 1)
            softmax_rows(512, 2, window)
            pe_done()
            for g in range(NG):
                half = slice(g * HD, (g + 1) * HD)
                last = v.tensor_copy(s.oN[half, :, SEQ:TOK].rearrange("p j b -> p b j"),
                                     O[half, 0:ROWS].rearrange("p (b g j) -> p b g j", g=NG, j=HPG)[:, :, g, :])
            ch.link(v, last)


def stage_hgrn(nc, s, T):
    kinds = (C_HQ, C_HF, C_HG)
    w_in = T["w_in"][0].rearrange("(k p) n -> p k n", p=P)
    weights = [view(s.ring, 1024 * i, KT, P) for i in range(3)]
    q, k, b, sg = ([view(s.work, 8256 + 4128 * par + 1032 * i, TOK) for par in range(2)] for i in range(4))
    E = view(s.ring, 3072, TOK)
    state = view(s.ring, 4104, NB, P)
    vb = view(s.ring, 5128, NB, P)
    S = view(s.ring, 6152, TT, P)
    X = [view(s.work, 21360 + 1024 * i, SEQ) for i in range(2)]
    AT = view(s.work, 23408, TT, P)
    kdT = view(s.work, 24432, TT, P)
    o_tm = view(s.work, 21360 + 1024, TT, P)
    masks = view(s.work, 25456, 256).bitcast(U8).rearrange("p (l n) -> p l n", l=8)
    st = view(s.work, 25712, 192)
    lb, om, e2, most = (st[:, 4 * i:4 * i + 4] for i in (0, 1, 2, 4))
    dec, dec_d, ssq, rstd, lnv = (st[:, 24 + 8 * i:32 + 8 * i] for i in range(5))
    od, sqd, lnd, rstd_d, part = (st[:, 64 + 8 * i:72 + 8 * i] for i in range(5))
    w_loaded = [s.sem(f"g_w{i}") for i in range(3)]
    masks_in, lb_sub, lb_exp = s.sem("g_masks"), s.sem("g_lb_sub"), s.sem("g_lb_exp")
    projected, evac = s.sem("g_projected"), s.sem("g_evac")
    f_ready, g_ready = s.sem("g_f"), s.sem("g_g")
    diff, exped, x_ready = s.sem("g_diff"), s.sem("g_exped"), s.sem("g_x_ready")
    level, picked = s.sem("g_level"), s.sem("g_picked")
    kd_ready, kd_turned, kd_copied = s.sem("g_kd"), s.sem("g_kd_turned"), s.sem("g_kd_copied")
    updates, states = s.sem("g_updates"), s.sem("g_states")
    new_state, dec_out, dec_sq, dec_sum = s.sem("g_new_state"), s.sem("g_dec_out"), s.sem("g_dec_sq"), s.sem("g_dec_sum")
    rstd_ready, o_ready, o_scaled, o_turned, o_read = (s.sem(f"g_{n}") for n in ("rstd", "o", "o_scaled", "o_turned", "o_read"))
    dec_in, states_out = s.sem("g_dec_in"), s.sem("g_states_out")
    SLOTS = 9
    JOBS = 9
    job = (0, 1, 3, 5, 6, 7, 8)

    with nc.Block() as block:
        @block.sync
        def _(sp):
            sp.dma_start(kdT.bitcast(I32), T["c_levels"]).then_inc(masks_in, 16)
            for h in range(HGH):
                for i, c in enumerate(kinds):
                    wait(sp, projected, SLOTS * (h - 1) + 3 * i + 3 if h else 0)
                    sp.dma_start(weights[i], w_in[:, :, c + h * P:c + (h + 1) * P]).then_inc(w_loaded[i], 16)

        @block.gpsimd
        def _(pool):
            for h in range(HGH):
                wait(pool, states_out, 32 * h)
                wait(pool, dec_out, h)
                pool.dma_start(state, T["state_hgrn"][0, :, h].rearrange("b f i -> f b i")).then_inc(dec_in, 16)
                pool.dma_start(vb, T["hi_rows"][:, h * P:(h + 1) * P].partition_broadcast(P)).then_inc(dec_in, 16)
                pool.wait_ge(states, h + 1)
                pool.dma_start(T["p_hg"][0, 0, h], S[:, TT - 1, :]).then_inc(states_out, 16)
                pool.wait_ge(new_state, h + 1)
                pool.dma_start(T["s_hg"][0, :, h].rearrange("b f i -> f b i"), state).then_inc(states_out, 16)
            pool.wait_ge(states_out, 32 * HGH)

        @block.tensor
        def _(pe):
            def project(r, u):
                kind, c = u // 3, u % 3
                n = SLOTS * r + u
                if c == 0:
                    pe.wait_ge(w_loaded[kind], 16 * (r + 1))
                wait(pe, evac, n - 2)
                for i in range(KT):
                    last = pe.matmul(s.ps[c][:, 0:CH], weights[kind][:, i, :], s.hT[:, i, c * CH:(c + 1) * CH],
                                     start=(i == 0), stop=(i == KT - 1))
                last.then_inc(projected, 1)

            def attend(h, u):
                p = h % 2
                if u < 8:
                    if u < 7:
                        pe.wait_ge(x_ready, 7 * h + u + 1)
                    for half in range(2):
                        wait(pe, picked, 2 * (8 * h + u - 1) + half + 1)
                        for c in range(4 * half, 4 * half + 4):
                            cols = slice(c * P, (c + 1) * P)
                            a, x = (X[u % 2], X[u % 2]) if u < 7 else (k[p], q[p])
                            last = pe.matmul(s.ps[3 + half][:, (c % 4) * P:(c % 4 + 1) * P], a[:, cols], x[:, cols],
                                             start=True, stop=True)
                        last.then_inc(level, 1)
                if u == 1:
                    pe.wait_ge(kd_ready, h + 1)
                    wait(pe, o_read, h)
                    for c in range(TT):
                        last = pe.transpose(s.ps[6 + c // 4][:, (c % 4) * P:(c % 4 + 1) * P],
                                            X[0][:, c * P:(c + 1) * P], s.ident[:, :])
                    last.then_inc(kd_turned, 1)
                if u == 2:
                    pe.wait_ge(kd_copied, h + 1)
                    for c in range(TT):
                        last = pe.matmul(s.ps[6 + c // 4][:, (c % 4) * P:(c % 4 + 1) * P], kdT[:, c, :],
                                         s.vhi[:, c, h * P:(h + 1) * P], start=True, stop=True)
                    last.then_inc(updates, 1)
                if u == 6:
                    pe.wait_ge(new_state, h + 1)
                    for n in range(NB):
                        last = pe.matmul(s.ps[5][:, n:n + 1], state[:, n, :], q[p][:, SEQ + n:SEQ + n + 1],
                                         start=True, stop=True)
                    last.then_inc(dec_out, 1)
                if u == 8:
                    pe.wait_ge(dec_sq, h + 1)
                    pe.matmul(s.ps[5][:, NB:2 * NB], s.ones[:, :], sqd, start=True, stop=True).then_inc(dec_sum, 1)
                    pe.wait_ge(states, h + 1)
                    pe.wait_ge(picked, 16 * (h + 1))
                    for c in range(TT):
                        out = s.ps[6 + c // 4][:, (c % 4) * P:(c % 4 + 1) * P]
                        last = pe.matmul(out, AT[:, c, :], s.vhi[:, c, h * P:(h + 1) * P], start=True, stop=(c == 0))
                        if c:
                            last = pe.matmul(out, s.oH[:, h, c * P:(c + 1) * P], S[:, c - 1, :], start=False, stop=True)
                    last.then_inc(o_ready, 1)

            def turn_output(h):
                pe.wait_ge(o_scaled, h + 1)
                for c in range(TT):
                    last = pe.transpose(s.ps[6 + c // 4][:, (c % 4) * P:(c % 4 + 1) * P], o_tm[:, c, :], s.ident[:, :])
                last.then_inc(o_turned, 1)

            for r in range(HGH + 1):
                for u in range(SLOTS):
                    if r < HGH:
                        project(r, u)
                    if u == 0 and r >= 2:
                        turn_output(r - 2)
                    if r >= 1:
                        attend(r - 1, u)
            turn_output(HGH - 1)

        @block.scalar
        def _(act):
            ch = s.act_chain
            func = (ACT.Copy, ACT.Sigmoid, ACT.Silu)

            def halves(u):
                m = 64 >> u
                return E[:, 0:SEQ].rearrange("p (b h m) -> p b h m", h=2, m=m)

            def evacuate(r, u):
                kind, c = u // 3, u % 3
                dst = (q, b, sg)[kind][r % 2]
                act.wait_ge(projected, SLOTS * r + u + 1)
                act.activation(dst[:, c * CH:(c + 1) * CH], s.ps[c][:, 0:CH], func[kind]).then_inc(evac, 1)

            def attend(h, u):
                p = h % 2
                if u < 7:
                    act.wait_ge(diff, JOBS * h + job[u] + 1)
                    e = halves(u)
                    act.activation(e[:, :, 0, :], e[:, :, 0, :], ACT.Exp, scale=-1.0)
                    act.activation(e[:, :, 1, :], e[:, :, 1, :], ACT.Exp).then_inc(exped, 1)
                if u == 1:
                    act.wait_ge(diff, JOBS * h + 3)
                    act.activation(E[:, 0:SEQ], E[:, 0:SEQ], ACT.Exp, scale=-1.0).then_inc(exped, 1)
                if u == 2:
                    act.wait_ge(kd_turned, h + 1)
                    act.activation(kdT.rearrange("p c n -> p (c n)"), s.psall[:, 6 * 512:8 * 512],
                                   ACT.Copy).then_inc(kd_copied, 1)
                    act.wait_ge(diff, JOBS * h + 5)
                    act.activation(E, b[p], ACT.Exp).then_inc(exped, 1)
                if u == 8:
                    act.wait_ge(dec_sum, h + 1)
                    ch.link(act, act.activation(lnd, s.ps[5][:, NB:2 * NB], ACT.Ln, bias=s.eps[:, 0:1], scale=1.0 / P))
                    act.activation(rstd_d, lnd, ACT.Exp, scale=-0.5).then_inc(rstd_ready, 1)
                    act.wait_ge(o_ready, h + 1)
                    for c in range(TT):
                        last = act.activation(kdT[:, c, :], s.ps[6 + c // 4][:, (c % 4) * P:(c % 4 + 1) * P], ACT.Square,
                                              accum_out=ssq[:, c:c + 1])
                    ch.link(act, last)
                    ch.link(act, act.activation(lnv, ssq, ACT.Ln, bias=s.eps[:, 0:1], scale=1.0 / P))
                    act.activation(rstd, lnv, ACT.Exp, scale=-0.5).then_inc(rstd_ready, 1)

            act.wait_ge(lb_sub, 1)
            act.activation(st[:, 8:16], st[:, 8:16], ACT.Exp).then_inc(lb_exp, 1)
            for r in range(HGH + 1):
                for u in range(SLOTS):
                    if r >= 1:
                        attend(r - 1, u)
                    if r < HGH:
                        evacuate(r, u)
                        if u == 6:
                            act.wait_ge(f_ready, r + 1)
                            act.activation(b[r % 2], b[r % 2], ACT.Ln).then_inc(g_ready, 1)

        @block.vector
        def _(v):
            ch = s.dve_chain
            rows = s.vec[:, 64:72].rearrange("p (a r) -> p a r", a=2)
            pair = st[:, 8:16].rearrange("p (a r) -> p a r", a=2)
            ch.link(v, v.tensor_tensor(most, rows[:, 0], rows[:, 1], ALU.max))
            v.tensor_tensor(pair, rows, bc(most.unsqueeze(1), (P, 2, 4)), ALU.subtract).then_inc(lb_sub, 1)
            v.memset(AT, 0.0)
            v.wait_ge(lb_exp, 1)
            ch.link(v, v.tensor_tensor(most, pair[:, 0], pair[:, 1], ALU.add))
            ch.link(v, v.reciprocal(most, most))
            ch.link(v, v.tensor_tensor(lb, pair[:, 0], most, ALU.mult))
            ch.link(v, v.tensor_scalar(om, lb, -1.0, 1.0, ALU.mult, ALU.add))
            v.wait_ge(masks_in, 16)
            ch.link(v, v.tensor_copy(masks, kdT.bitcast(I32)))

            def forget(r, u):
                p = r % 2
                if u == 6:
                    v.wait_ge(evac, SLOTS * r + 6)
                    ch.link(v, v.tensor_scalar(b[p], b[p], om[:, r:r + 1], lb[:, r:r + 1], ALU.mult, ALU.add))
                    v.tensor_scalar(k[p], b[p], -1.0, 1.0, ALU.mult, ALU.add).then_inc(f_ready, 1)
                if u == 7:
                    v.wait_ge(g_ready, r + 1)
                    for c in range(TT):
                        cols = b[p][:, c * P:(c + 1) * P]
                        last = v.tensor_tensor_scan(cols, s.ones[:, :], cols, 0.0, ALU.mult, ALU.add)
                    ch.link(v, last)

            def pick(h, u):
                for half in range(2):
                    v.wait_ge(level, 2 * (8 * h + u) + half + 1)
                    v.copy_predicated(AT[:, 4 * half:4 * half + 4, :], bc(masks[:, u, :].unsqueeze(1), (P, 4, P)),
                                      view(s.ps[3 + half], 0, 4, P)).then_inc(picked, 1)

            def attend(h, u):
                p = h % 2
                chunks = lambda x: x[:, 0:SEQ].rearrange("p (c n) -> p c n", n=P)
                if u < 7:
                    m = 64 >> u
                    halves = lambda x: x[:, 0:SEQ].rearrange("p (b h m) -> p b h m", h=2, m=m)
                    blocks = lambda x: x[:, 0:SEQ].rearrange("p (b m) -> p b m", m=2 * m)
                    v.tensor_tensor(blocks(E), blocks(b[p]), bc(blocks(b[p])[:, :, m - 1:m], (P, 512 // m, 2 * m)),
                                    ALU.subtract).then_inc(diff, 1)
                if 1 <= u:
                    if h or u:
                        pick(h, u - 1)
                if u < 7:
                    if u == 2:
                        v.wait_ge(kd_turned, h + 1)
                    if u == 1:
                        wait(v, o_turned, h)
                    if u >= 2:
                        v.wait_ge(level, 2 * (8 * h + u - 2) + 2)
                    v.wait_ge(exped, JOBS * h + job[u] + 1)
                    v.tensor_tensor(halves(X[u % 2])[:, :, 0], halves(k[p])[:, :, 0], halves(E)[:, :, 0], ALU.mult)
                    ch.link(v, v.tensor_tensor(halves(X[u % 2])[:, :, 1], halves(q[p])[:, :, 1], halves(E)[:, :, 1],
                                               ALU.mult))
                    v.nop().then_inc(x_ready, 1)
                if u == 0 and h >= 1:
                    finish(h - 1)
                if u == 1:
                    v.tensor_tensor(chunks(E), chunks(b[p]), bc(chunks(b[p])[:, :, P - 1:P], (P, TT, P)),
                                    ALU.subtract).then_inc(diff, 1)
                    v.wait_ge(exped, JOBS * h + 3)
                    v.wait_ge(level, 2 * 8 * h + 2)
                    ch.link(v, v.tensor_tensor(X[0], k[p][:, 0:SEQ], E[:, 0:SEQ], ALU.mult))
                    v.nop().then_inc(kd_ready, 1)
                if u == 2:
                    v.nop().then_inc(diff, 1)
                    v.wait_ge(exped, JOBS * h + 5)
                    v.tensor_copy(dec, chunks(E)[:, :, P - 1])
                    v.tensor_copy(dec_d, E[:, SEQ:TOK])
                    ch.link(v, v.tensor_tensor(s.oH[:, h, 0:SEQ], q[p][:, 0:SEQ], E[:, 0:SEQ], ALU.mult))
                if u == 3:
                    v.wait_ge(updates, h + 1)
                    wait(v, states_out, 32 * h)
                    src = view(s.psall, 6 * 512, TT, P)
                    ch.link(v, v.tensor_copy(S[:, 0, :], src[:, 0, :]))
                    for c in range(1, TT):
                        ch.link(v, v.scalar_tensor_tensor(out=S[:, c, :], in0=S[:, c - 1, :], scalar=dec[:, c:c + 1],
                                                          in1=src[:, c, :], op0=ALU.mult, op1=ALU.add))
                    v.nop().then_inc(states, 1)
                if u == 5:
                    v.wait_ge(dec_in, 32 * (h + 1))
                    v.tensor_tensor(vb, vb, bc(k[p][:, SEQ:TOK].unsqueeze(2), (P, NB, P)), ALU.mult)
                    ch.link(v, v.tensor_tensor(state, state, bc(dec_d.unsqueeze(2), (P, NB, P)), ALU.mult))
                    v.tensor_tensor(state, state, vb, ALU.add).then_inc(new_state, 1)
                if u == 7:
                    v.wait_ge(dec_out, h + 1)
                    ch.link(v, v.tensor_copy(od, s.ps[5][:, 0:NB]))
                    v.tensor_tensor(sqd, od, od, ALU.mult).then_inc(dec_sq, 1)
                if u == 8:
                    v.wait_ge(rstd_ready, 2 * h + 1)
                    ch.link(v, v.scalar_tensor_tensor(out=part, in0=od, scalar=s.vec[:, 72:73], in1=rstd_d,
                                                      op0=ALU.mult, op1=ALU.mult))
                    v.tensor_tensor(s.oH[:, h, SEQ:TOK], part, sg[p][:, SEQ:TOK], ALU.mult)
                    v.wait_ge(rstd_ready, 2 * h + 2)
                    v.tensor_tensor(o_tm, view(s.psall, 6 * 512, TT, P), bc(rstd.unsqueeze(2), (P, TT, P)),
                                    ALU.mult).then_inc(o_scaled, 1)

            def finish(h):
                v.wait_ge(o_turned, h + 1)
                v.scalar_tensor_tensor(out=s.oH[:, h, 0:SEQ], in0=s.psall[:, 6 * 512:8 * 512], scalar=s.vec[:, 72:73],
                                       in1=sg[h % 2][:, 0:SEQ], op0=ALU.mult, op1=ALU.mult).then_inc(o_read, 1)

            for r in range(HGH + 1):
                for u in range(SLOTS):
                    if r >= 1:
                        attend(r - 1, u)
                    if r < HGH:
                        forget(r, u)
            finish(HGH - 1)
            v.wait_ge(o_read, HGH)


def stage_mix(nc, s, T):
    w_in = T["w_in"][0].rearrange("(k p) n -> p k n", p=P)
    nsa = T["w_br_nsa"][0].rearrange("(g j d) n -> g d j n", g=NG, d=HD)
    hg = T["w_br_hg"][0].rearrange("(h p) n -> p h n", p=P)
    w_ga, w_gb = ([view(s.ring, 3072 * i + at, KT, P) for i in range(2)] for at in (0, 1024))
    w_nsa, w_hg = ([view(s.ring, 3072 * i + at, 4, P) for i in range(2)] for at in (2048, 2560))
    sig = [view(s.work, 16752 + 1032 * i, TOK) for i in range(2)]
    part = view(s.work, 16752 + 2064, TOK)
    mix = view(s.work, 8256, KT * TOK)
    loaded = [s.sem(f"x_loaded{i}") for i in range(2)]
    used = [s.sem(f"x_used{i}") for i in range(2)]
    free_a, free_v, product = s.sem("x_free_a"), s.sem("x_free_v"), s.sem("x_product")

    with nc.Block() as block:
        @block.sync
        def _(sp):
            with sp.Fori(0, KT // 2) as i:
                for h in range(2):
                    col = (2 * i + h) * P
                    sp.wait_ge(used[h], i + 1)
                    for dst, src in ((w_ga[h], w_in[:, :, bass.ds(C_GA + col, P)]), (w_gb[h], w_in[:, :, bass.ds(C_GB + col, P)]),
                                     (w_nsa[h][0:HD], nsa[0, :, :, bass.ds(col, P)]),
                                     (w_nsa[h][HD:P], nsa[1, :, :, bass.ds(col, P)]),
                                     (w_hg[h], hg[:, :, bass.ds(col, P)])):
                        sp.dma_start(dst, src).then_inc(loaded[h], 16)

        @block.tensor
        def _(pe):
            for h in range(2):
                pe.sem_inc(used[h], 1)
            with pe.Fori(0, KT // 2) as i:
                for h in range(2):
                    pe.wait_ge(loaded[h], 80 * i + 80)
                    n = 2 * i + h
                    for kind, (w, src) in enumerate(((w_ga, s.hT), (w_nsa, s.oN), (w_gb, s.hT), (w_hg, s.oH))):
                        tiles = KT if kind % 2 == 0 else 4
                        for c in range(3):
                            pe.wait_ge(free_v if kind % 2 else free_a, 6 * n + 3 * (kind // 2) + c + 1)
                            for k in range(tiles):
                                last = pe.matmul(s.ps[3 * (kind % 2) + c][:, 0:CH], w[h][:, k, :],
                                                 src[:, k, c * CH:(c + 1) * CH], start=(k == 0), stop=(k == tiles - 1))
                            if kind < 3 or c < 2:
                                last.then_inc(product, 1)
                            else:
                                last.then_inc(used[h], 1)
                                pe.wait_ge(used[h], i + 2)
                                pe.sem_inc(product, 1)

        @block.scalar
        def _(act):
            act.sem_inc(free_a, 3)
            with act.Fori(0, KT // 2) as i:
                for h in range(2):
                    n = 2 * i + h
                    for branch in range(2):
                        act.wait_ge(free_v, 6 * n + (3 if branch else 1))
                        for c in range(3):
                            act.wait_ge(product, 12 * n + 6 * branch + c + 1)
                            act.activation(sig[branch][:, c * CH:(c + 1) * CH], s.ps[c][:, 0:CH],
                                           ACT.Sigmoid).then_inc(free_a, 1)

        @block.vector
        def _(v):
            ch = s.dve_chain
            v.sem_inc(free_v, 3)
            with v.Fori(0, KT // 2) as i:
                ch.enter(i, 12)
                for h in range(2):
                    n = 2 * i + h
                    for branch in range(2):
                        for c in range(3):
                            v.wait_ge(free_a, 6 * n + 3 * branch + c + 4)
                            v.wait_ge(product, 12 * n + 6 * branch + c + 4)
                            cols = slice(c * CH, (c + 1) * CH)
                            at = mix[:, bass.ds(n * TOK + c * CH, CH)]
                            ch.link(v, v.tensor_tensor(part[:, cols] if branch else at, sig[branch][:, cols],
                                                       s.ps[3 + c][:, 0:CH], ALU.mult))
                            v.nop().then_inc(free_v, 1)
                            if branch:
                                v.tensor_tensor(at, at, part[:, cols], ALU.add)
            ch.leave(KT // 2)


def stage_residual(nc, s, name, w, src, tiles, gate):
    panel = [view(s.ring, tiles * P * i, tiles, P) for i in range(2)]
    w = w.rearrange("(k p) n -> p k n", p=P)
    part = view(s.ring, 2 * tiles * P, NB)
    x = s.xT[:, :, :].rearrange("p k n -> p (k n)")
    mod = s.mod[:, :, :].rearrange("p m n -> p (m n)")
    loaded = [s.sem(f"{name}_loaded{i}") for i in range(2)]
    product, used, added = s.sem(f"{name}_product"), [s.sem(f"{name}_used{i}") for i in range(2)], s.sem(f"{name}_added")

    with nc.Block() as block:
        @block.sync
        def _(sp):
            with sp.Fori(0, KT // 2) as i:
                for h in range(2):
                    sp.wait_ge(used[h], i + 1)
                    sp.dma_start(panel[h], w[:, :, bass.ds((2 * i + h) * P, P)]).then_inc(loaded[h], 16)

        @block.tensor
        def _(pe):
            for h in range(2):
                pe.sem_inc(used[h], 1)
            with pe.Fori(0, KT // 2) as i:
                for h in range(2):
                    pe.wait_ge(loaded[h], 16 * i + 16)
                    pe.wait_ge(added, 6 * i + 1)
                    for c in range(3):
                        for k in range(tiles):
                            last = pe.matmul(s.ps[3 * h + c][:, 0:CH], panel[h][:, k, :], src[:, k, c * CH:(c + 1) * CH],
                                             start=(k == 0), stop=(k == tiles - 1))
                        last.then_inc(product if c < 2 else used[h], 1)

        @block.vector
        def _(v):
            ch = s.dve_chain
            v.sem_inc(added, 1)
            with v.Fori(0, KT // 2) as i:
                ch.enter(i, 4)
                for h in range(2):
                    n = 2 * i + h
                    for c in range(3):
                        v.wait_ge(*((product, 4 * i + 2 * h + c + 1) if c < 2 else (used[h], i + 2)))
                        m = CH if c < 2 else CH - NB
                        at = x[:, bass.ds(n * TOK + c * CH, m)]
                        last = v.scalar_tensor_tensor(out=at, in0=s.ps[3 * h + c][:, 0:m],
                                                      scalar=mod[:, bass.ds((gate + n) * (NB + 1), 1)], in1=at,
                                                      op0=ALU.mult, op1=ALU.add)
                        if c < 2:
                            last.then_inc(added, 1)
                    ch.link(v, v.tensor_tensor(part, s.ps[3 * h + 2][:, m:CH],
                                               mod[:, bass.ds((gate + n) * (NB + 1) + 1, NB)], ALU.mult))
                    at = x[:, bass.ds(n * TOK + SEQ, NB)]
                    ch.link(v, v.tensor_tensor(at, at, part, ALU.add))
                    v.nop().then_inc(added, 1)
            ch.leave(KT // 2)


def stage_up(nc, s, T):
    w_up = T["w_up"].rearrange("(k p) n -> p k n", p=P)
    w_u, w_v = ([view(s.ring, 2048 * i + at, KT, P) for i in range(2)] for at in (0, 1024))
    a = view(s.work, 0, FT * TOK)
    Z = FT * TOK
    u = view(s.work, Z, SEQ + 2)
    y = view(s.work, Z + 1028, TOK)
    tails = view(s.work, Z + 2060, FT * (NB + 2))
    bufT = view(s.work, Z + 2280, FT * 2 * NB)
    part = view(s.work, Z + 2632, NB)
    rows = view(s.ring, 4096, DFF)
    loaded = [s.sem(f"u_loaded{i}") for i in range(2)]
    used_u, used_v = s.sem("u_used_u"), s.sem("u_used_v")
    buf_in, turned, copied, out = s.sem("u_buf_in"), s.sem("u_turned"), s.sem("u_copied"), s.sem("u_out")
    u_read, v_read, u_sent, conv_a, conv_v = (s.sem(f"u_{n}") for n in ("u_read", "v_read", "u_sent", "conv_a", "conv_v"))
    conv = s.conv[:, :, :].rearrange("p j f -> p (j f)")

    with nc.Block() as block:
        @block.sync
        def _(sp):
            with sp.Fori(0, FT // 2) as i:
                for h in range(2):
                    col = (2 * i + h) * P
                    sp.wait_ge(used_v, 6 * i + 1)
                    sp.dma_start(w_u[h], w_up[:, :, bass.ds(col, P)]).then_inc(loaded[h], 16)
                    sp.dma_start(w_v[h], w_up[:, :, bass.ds(DFF + col, P)]).then_inc(loaded[h], 16)
            sp.wait_ge(copied, 1 + (FT + 3) // 4)
            sp.dma_start(T["p_cf"][0, 0], rows[0:2, :]).then_inc(out, 16)
            sp.dma_start(T["s_cf"][0, :, 1], rows[2:2 + NB, :]).then_inc(out, 16)
            sp.wait_ge(out, 32)

        @block.gpsimd
        def _(pool):
            pool.dma_start(rows[0:2 * NB, :], T["state_ffn_conv"][0].rearrange("b j f -> (b j) f")).then_inc(buf_in, 16)
            pool.dma_start(T["s_cf"][0, :, 0], T["state_ffn_conv"][0, :, 1]).then_inc(buf_in, 16)
            pool.wait_ge(buf_in, 32)

        @block.tensor
        def _(pe):
            pe.wait_ge(buf_in, 32)
            for f in range(FT):
                last = pe.transpose(s.ps[6][:, f * 16:(f + 1) * 16], rows[0:2 * NB, f * P:(f + 1) * P],
                                    s.ident[0:2 * NB, 0:2 * NB])
            last.then_inc(turned, 1)
            pe.sem_inc(used_v, 1)
            with pe.Fori(0, FT // 2) as i:
                for h in range(2):
                    f = 2 * i + h
                    pe.wait_ge(loaded[h], 32 * i + 32)
                    for kind, (w, read, done) in enumerate(((w_u, u_read, used_u), (w_v, v_read, used_v))):
                        pe.wait_ge(read, 3 * f + 1)
                        for c in range(3):
                            for k in range(KT):
                                last = pe.matmul(s.ps[3 * kind + c][:, 0:CH], w[h][:, k, :],
                                                 s.hT[:, k, c * CH:(c + 1) * CH], start=(k == 0), stop=(k == KT - 1))
                            last.then_inc(done, 1)
            pe.wait_ge(conv_v, FT + 1)
            for f in range(FT):
                if f % 4 == 0 and f >= 8:
                    pe.wait_ge(copied, f // 4)
                last = pe.transpose(s.ps[6 + f // 4 % 2][0:NB + 2, (f % 4) * P:(f % 4 + 1) * P],
                                    tails[:, f * 10:(f + 1) * 10], s.ident[:, :])
                if f % 4 == 3 or f == FT - 1:
                    last.then_inc(turned, 1)

        @block.scalar
        def _(act):
            ch = s.act_chain
            act.wait_ge(copied, 1)
            act.sem_inc(u_read, 1)
            with act.Fori(0, FT // 2) as i:
                ch.enter(i, 4)
                for h in range(2):
                    f = 2 * i + h
                    act.wait_ge(conv_v, f + 1)
                    for c in range(3):
                        m = CH if c < 2 else CH - NB
                        act.wait_ge(used_u, 3 * f + c + 1)
                        last = act.activation(u[:, 2 + c * CH:2 + c * CH + m], s.ps[c][:, 0:m], ACT.Copy)
                        if c < 2:
                            last.then_inc(u_read, 1)
                    ch.link(act, last)
                    tail = tails[:, bass.ds(10 * f, 2)]
                    act.activation(tail, s.ps[2][:, m - 2:m], ACT.Copy)
                    ch.link(act, act.activation(tails[:, bass.ds(10 * f + 2, NB)], s.ps[2][:, m:CH], ACT.Copy))
                    act.nop().then_inc(u_read, 1)
                    tap, bias = conv[:, bass.ds(2 * FT + f, 1)], conv[:, bass.ds(3 * FT + f, 1)]
                    act.wait_ge(v_read, 3 * f + 1)
                    act.activation(y[:, 0:SEQ], u[:, 2:SEQ + 2], ACT.Identity, scale=tap, bias=bias)
                    act.activation(y[:, SEQ:TOK], tails[:, bass.ds(10 * f + 2, NB)], ACT.Identity, scale=tap,
                                   bias=bias).then_inc(conv_a, 1)
                    act.wait_ge(conv_v, f + 2)
                    act.activation(y, y, ACT.Silu).then_inc(u_sent, 1)
            ch.leave(FT // 2)

        @block.vector
        def _(v):
            ch = s.dve_chain
            ch.link(v, v.memset(u[:, 0:2], 0.0))
            v.wait_ge(turned, 1)
            v.tensor_copy(bufT.rearrange("p (f j b) -> p f j b", j=2, b=NB),
                          view(s.ps[6], 0, FT, NB, 2).rearrange("p f b j -> p f j b")).then_inc(copied, 1)
            v.wait_ge(copied, 1)
            v.sem_inc(v_read, 1)
            v.sem_inc(conv_v, 1)
            with v.Fori(0, FT // 2) as i:
                ch.enter(i, 4)
                for h in range(2):
                    f = 2 * i + h
                    v.wait_ge(conv_a, f + 1)
                    taps = [conv[:, bass.ds(j * FT + f, 1)] for j in range(2)]
                    ch.link(v, v.scalar_tensor_tensor(out=y[:, 0:SEQ], in0=u[:, 1:SEQ + 1], scalar=taps[1],
                                                      in1=y[:, 0:SEQ], op0=ALU.mult, op1=ALU.add))
                    v.scalar_tensor_tensor(out=y[:, 0:SEQ], in0=u[:, 0:SEQ], scalar=taps[0], in1=y[:, 0:SEQ],
                                           op0=ALU.mult, op1=ALU.add)
                    yd = y[:, SEQ:TOK]
                    ch.link(v, v.scalar_tensor_tensor(out=yd, in0=bufT[:, bass.ds(16 * f + NB, NB)], scalar=taps[1],
                                                      in1=yd, op0=ALU.mult, op1=ALU.add))
                    v.scalar_tensor_tensor(out=yd, in0=bufT[:, bass.ds(16 * f, NB)], scalar=taps[0], in1=yd,
                                           op0=ALU.mult, op1=ALU.add).then_inc(conv_v, 1)
                    v.wait_ge(u_sent, f + 1)
                    for c in range(3):
                        v.wait_ge(used_v, 3 * f + c + 2)
                        v.tensor_tensor(a[:, bass.ds(f * TOK + c * CH, CH)], y[:, c * CH:(c + 1) * CH],
                                        s.ps[3 + c][:, 0:CH], ALU.mult).then_inc(v_read, 1)
            ch.leave(FT // 2)
            for g in range((FT + 3) // 4):
                n = min(4, FT - 4 * g) * P
                v.wait_ge(turned, g + 2)
                v.tensor_copy(rows[0:NB + 2, 512 * g:512 * g + n], s.ps[6 + g % 2][0:NB + 2, 0:n]).then_inc(copied, 1)


def stage_output(nc, s, T):
    y = [view(s.ring, 1024 * i, D) for i in range(2)]
    turned, done = s.sem("o_turned"), [s.sem("o_done_v"), s.sem("o_done_a")]
    sent = [s.sem(f"o_sent{i}") for i in range(2)]

    with nc.Block() as block:
        @block.tensor
        def _(pe):
            for t in range(TT + 1):
                n = rows_of(t)
                for half in range(2):
                    g = 2 * t + half
                    wait(pe, done[half], t - 3)
                    for j in range(4):
                        last = pe.transpose(s.ps[g % 8][0:n, j * P:(j + 1) * P],
                                            s.xT[:, 4 * half + j, t * P:t * P + n], s.ident[:, :])
                    last.then_inc(turned, 1)

        def copy_half(eng, copy, half):
            for t in range(TT + 1):
                n = rows_of(t)
                eng.wait_ge(turned, 2 * t + half + 1)
                wait(eng, sent[t % 2], 16 * (t // 2))
                copy(y[t % 2][0:n, 512 * half:512 * (half + 1)], s.ps[(2 * t + half) % 8][0:n, :]).then_inc(done[half], 1)

        @block.vector
        def _(v):
            copy_half(v, v.tensor_copy, 0)

        @block.scalar
        def _(act):
            copy_half(act, lambda o, i: act.activation(o, i, ACT.Copy), 1)

        @block.sync
        def _(sp):
            for t in range(TT + 1):
                for half in range(2):
                    sp.wait_ge(done[half], t + 1)
                dst = T["y_prompt"][0, t * P:(t + 1) * P] if t < TT else T["y_sample"][:, 0]
                sp.dma_start(dst, y[t % 2][0:rows_of(t), :]).then_inc(sent[t % 2], 16)
            for b in range(2):
                sp.wait_ge(sent[b], 16 * len(range(b, TT + 1, 2)))


def program(nc, T):
    s = allocate(nc)
    stage_modulation(nc, s, T)
    stage_norm(nc, s, "n1", s.A1, SH1)
    stage_token_major(nc, s, T)
    stage_compress(nc, s, T)
    stage_prompt_attention(nc, s, T)
    stage_decode_attention(nc, s, T)
    stage_hgrn(nc, s, T)
    stage_mix(nc, s, T)
    stage_residual(nc, s, "w", T["w_out"], view(s.work, 8256, KT, TOK), KT, G1)
    stage_norm(nc, s, "n2", s.A2, SH2)
    stage_up(nc, s, T)
    stage_residual(nc, s, "r", T["w_down"], view(s.work, 0, FT, TOK), FT, G2)
    stage_output(nc, s, T)


_INS = ["x_prompt", "x_sample", "cache_cmp_k", "cache_cmp_v", "cache_slc_k", "cache_slc_v", "cache_win_k",
        "cache_win_v", "state_hgrn", "state_ffn_conv", "page_table", "c_prompt", "c_sample", "ada_w", "ada_b",
        "norm_attn", "norm_ffn", "w_in", "q_gain", "k_gain", "cmp_w1", "cmp_w2", "cmp_pe", "hg_lb", "hg_norm",
        "w_br_nsa", "w_br_hg", "w_out", "w_up", "conv_w", "conv_b", "w_down"]
_OUTS = [("y_prompt", (1, SEQ, D)), ("y_sample", (NB, 1, D)),
         ("p_ck", (1, 1, SEQ, NG, HD)), ("p_cv", (1, 1, SEQ, NG, HD)), ("p_sk", (1, 1, SEQ, NG, HD)),
         ("p_sv", (1, 1, SEQ, NG, HD)), ("p_wk", (1, 1, WIN, NG, HD)), ("p_wv", (1, 1, WIN, NG, HD)),
         ("p_hg", (1, 1, HGH, P, P)), ("p_cf", (1, 1, 2, DFF)),
         ("s_ck", (1, NB, 1, NG, HD)), ("s_cv", (1, NB, 1, NG, HD)), ("s_sk", (1, NB, 1, NG, HD)),
         ("s_sv", (1, NB, 1, NG, HD)), ("s_wk", (1, NB, WIN, NG, HD)), ("s_wv", (1, NB, WIN, NG, HD)),
         ("s_hg", (1, NB, HGH, P, P)), ("s_cf", (1, NB, 2, DFF))]


def kernel(**inputs):
    from concourse import bacc
    from concourse.bass_utils import run_bass_kernel_spmd

    nc = bacc.Bacc("TRN2", target_bir_lowering=False, num_devices=1)
    arrays, T = {}, {}
    given = {name: np.ascontiguousarray(inputs[name]) for name in _INS if name != "page_table"}
    given.update(constants())
    for name, a in given.items():
        arrays[f"in_{name}"] = a
        T[name] = nc.dram_tensor(f"in_{name}", a.shape, mybir.dt.from_np(a.dtype), kind="ExternalInput").ap()
    for name, shape in _OUTS:
        T[name] = nc.dram_tensor(f"out_{name}", shape, F32, kind="ExternalOutput").ap()
    T["hi_rows"] = nc.dram_tensor("hi_rows", (NB, 512), F32).ap()
    T["gate_rows"] = nc.dram_tensor("gate_rows", (NB, 24), F32).ap()
    pages = np.ascontiguousarray(np.repeat(inputs["page_table"].T, SUB_PER_PAGE, axis=0))
    arrays["in_page_rows"] = pages
    T["page_rows"] = nc.dram_tensor("in_page_rows", pages.shape, I32, kind="ExternalInput").ap()
    T["ada_w"], T["w_up"], T["w_down"], T["w_out"] = T["ada_w"][0], T["w_up"][0], T["w_down"][0], T["w_out"][0]
    program(nc, T)
    r = run_bass_kernel_spmd(nc, [arrays], core_ids=[0])
    return tuple(r.results[0][f"out_{name}"] for name, _ in _OUTS)
```

```python
import math

import numpy as np

import concourse.bass as bass
import concourse.mybir as mybir

F32 = mybir.dt.float32
F32R = mybir.dt.float32r
BF16 = mybir.dt.bfloat16
I32 = mybir.dt.int32
U32 = mybir.dt.uint32
U8 = mybir.dt.uint8
ALU = mybir.AluOpType
ACT = mybir.ActivationFunctionType
AX = mybir.AxisListType

P = 128
D = 1024
KT = D // P
SEQ = 1024
NB = 8
TOK = SEQ + NB
TT = SEQ // P
CH = TOK // 3
HD = 64
NH = 8
NG = 2
HPG = NH // NG
CMP_STRIDE = 16
NSUB_P = SEQ // CMP_STRIDE
NC_P = NSUB_P - 1
PAST = 2048
NSUB_S = PAST // CMP_STRIDE
NC_S = NSUB_S - 1
PAGE = 128
PAGES = PAST // PAGE
SUB_PER_PAGE = PAGE // CMP_STRIDE
SLC = 64
NSEL = 16
NS_S = PAST // SLC + 1
WIN = 512
HGH = 4
DFF = 2816
FT = DFF // P
EPS = 1e-6
X3 = 4128
NEG = -1e30
SCALE = HD ** -0.5

C_Q, C_KC, C_VS, C_GATE, C_HQ, C_HF, C_HI, C_HG, C_GA, C_GB = (
    0, 512, 896, 1280, 1304, 1816, 2328, 2840, 3352, 4376)
SH1, SC1, G1, SH2, SC2, G2 = (KT * i for i in range(6))


class Core:
    pass


class Unit:

    def __init__(self, kind, t, h, lo, n, last):
        self.kind, self.t, self.h, self.lo, self.n, self.last = kind, t, h, lo, n, last


def rows_of(t):
    return P if t < TT else NB


class Chain:

    def __init__(self, sem):
        self.sem, self.base, self.n, self.per = sem, 0, 0, None

    def link(self, eng, ins):
        self.n += 1
        ins.then_inc(self.sem, 1)
        eng.wait_ge(self.sem, self.base + self.n)

    def enter(self, i, per):
        self.before = self.base + self.n
        self.base, self.n, self.per = self.before + i * per, 0, per

    def leave(self, times):
        assert self.n == self.per, (self.n, self.per)
        self.base, self.n = self.before + self.per * times, 0


def constants():
    q = np.arange(P)[:, None]
    k = np.arange(P)[None, :]
    add = np.zeros((P, 2, P), np.float32)
    add[:, 0] = np.where(k <= q, 0.0, NEG)
    add[:, 1] = np.where(k > q, 0.0, NEG)
    cmp_ok = np.zeros((P, TT, HD), np.float32)
    for t in range(TT):
        cmp_ok[:, t, :NC_P] = (np.arange(NC_P)[None] * CMP_STRIDE + 31) <= (t * P + q)
    inv = (np.float32(500000.0) ** (-np.arange(0, 16, 2, dtype=np.float32) / np.float32(16))).astype(np.float32)
    pos = np.concatenate([np.arange(SEQ), np.full(NB, PAST)]).astype(np.float32)
    ang = (pos[:, None] * inv[None]).astype(np.float32)
    cos, sin = np.cos(ang), np.sin(ang)
    rope = np.concatenate([cos, cos, sin, sin], axis=1).astype(np.float32)
    start = np.arange(NC_S) * CMP_STRIDE
    s0 = np.arange(NS_S) * SLC
    over = ((start[:, None] <= s0[None] + SLC - 1) & (start[:, None] + 31 >= s0[None])).astype(np.float32)
    own = (np.arange(HD)[:, None] // NH == np.arange(NB)[None]).astype(np.float32)
    lower = (np.arange(NS_S)[None, :] < np.arange(NS_S)[:, None]).astype(np.float32)
    lower = np.broadcast_to(lower.reshape(1, -1), (HD, NS_S * NS_S))
    levels = np.zeros((P, 8, P), np.int32)
    s, t = q, k
    levels[:, 7] = s == t
    for n in range(7):
        m = 64 >> n
        levels[:, n] = (s // (2 * m) == t // (2 * m)) & (s % (2 * m) < m) & (t % (2 * m) >= m)
    return {
        "c_ident": np.eye(P, dtype=np.float32),
        "c_add": add,
        "c_cmp_add": np.where(cmp_ok > 0, 0.0, NEG).astype(np.float32),
        "c_cmp_mul": cmp_ok,
        "c_rope": rope,
        "c_over": over,
        "c_own": own,
        "c_lower": np.ascontiguousarray(lower),
        "c_sub": (np.arange(P)[:, None] % SUB_PER_PAGE).astype(np.float32),
        "c_levels": levels,
    }


def allocate(nc):
    sb = nc.alloc_sbuf_tensor
    s = Core()

    def region(name, size):
        base = -(-nc.sbuf_base // 32) * 32
        whole, parts = sb(name, [P, size], F32), {}

        def short(start, *shape):
            n = math.prod(shape)
            if (start, n) not in parts:
                parts[start, n] = nc.alloc_sbuf_tensor_at(f"{name}_short_{start}_{n}", [P, n], F32R,
                                                          offset=base + 4 * start)
            return view(parts[start, n], 0, *shape)
        return whole, short

    x, x_short = region("xT", KT * TOK)
    s.xT, s.xT_r = view(x, 0, KT, TOK), x_short(0, KT, TOK)
    s.hT = sb("hT", [P, KT, TOK], F32R)
    s.ring, s.ring_short = region("ring", 8192)
    s.work, s.work_short = region("work", 25904)
    s.ident = sb("ident", [P, P], F32)
    s.identb = sb("identb", [P, P], BF16)
    s.ones = sb("ones", [P, P], F32)
    s.add = sb("add", [P, 2, P], BF16)
    s.rope = sb("rope", [P, TT + 1, 32], F32)
    s.gain = sb("gain", [P, 4, HD], F32)
    s.vec = sb("vec", [P, 80], F32)
    s.conv = sb("conv", [P, 4, FT], F32)
    s.mod = sb("mod", [P, 6 * KT, NB + 1], F32)
    s.A1 = sb("A1", [P, KT, NB + 1], F32)
    s.A2 = sb("A2", [P, KT, NB + 1], F32)
    s.cT = sb("cT", [P, KT, NB + 1], F32)
    s.eps = sb("eps", [P, 1], F32)
    s.gidx = sb("gidx", [P, NB], U32)
    s.psall = nc.alloc_psum_tensor("psall", [P, 8 * 512], F32)
    s.ps = [s.psall[:, 512 * i:512 * (i + 1)] for i in range(8)]
    s.stage_sems = []

    def sem(name):
        s.stage_sems.append(nc.alloc_semaphore(name))
        return s.stage_sems[-1]

    s.sem = sem
    s.dve_chain = Chain(nc.alloc_semaphore("dve_chain"))
    s.act_chain = Chain(nc.alloc_semaphore("act_chain"))
    s.pool_chain = Chain(nc.alloc_semaphore("pool_chain"))
    s.oN = view(s.work, 0, 4, TOK)
    s.oH = view(s.work, 4128, 4, TOK)
    s.qT = view(s.work, 8256, 4, TOK)
    s.ksT = view(s.work, 12384, TOK)
    s.kwT = view(s.work, 13416, TOK)
    s.vkv = view(s.work, 14448, TT + 1, 2, P)
    s.vhi = view(s.work, 16752, TT + 1, 512)
    s.gates = view(s.work, 21360, TT + 1, 24)
    s.kcT = view(s.work, 21576, NB + 1, P)
    s.vc = view(s.work, 22728, NB + 1, P)
    return s


def wait(eng, sem, value):
    if not isinstance(value, int) or value > 0:
        eng.wait_ge(sem, value)


def recycle(nc, s):
    nc.clear_and_free_semaphores(s.stage_sems)
    nc.all_engine_barrier()
    s.stage_sems.clear()


def view(t, start, *shape):
    n = 1
    for x in shape:
        n *= x
    v = t[:, start:start + n]
    if len(shape) == 1:
        return v
    names = "abcd"[:len(shape)]
    return v.rearrange(f"p ({' '.join(names)}) -> p {' '.join(names)}", **dict(zip(names, shape)))


def bc(ap, shape):
    return ap.to_broadcast(list(shape))


def stage_modulation(nc, s, T):
    x_tm = view(s.work, 0, TT + 1, D)
    rows = view(s.work, 9216, P)
    crow = view(s.work, 9344, P)
    c_tm = view(s.work, 9472, D)
    add_f = view(s.work, 10496, 2, P)
    panel = [view(s.ring, 2048 * i, KT, 256) for i in range(4)]
    small, x_in, c_in = s.sem("m_small"), s.sem("m_x_in"), s.sem("m_c_in")
    loaded = [s.sem(f"m_loaded{i}") for i in range(4)]
    panel_used, tr_done = s.sem("m_panel_used"), s.sem("m_tr_done")
    evac_v, evac_a, ada_done = s.sem("m_evac_v"), s.sem("m_evac_a"), s.sem("m_ada_done")
    ready = s.sem("m_cT_ready")
    ada = T["ada_w"].rearrange("(k p) n -> p k n", p=P)
    NGRP = 2 * (TT + 1)
    PANELS = G1 * P // 256
    s.spilled = s.sem("m_spilled")

    with nc.Block() as block:
        @block.sync
        def _(sp):
            sp.dma_start(s.ident[:, :], T["c_ident"]).then_inc(c_in, 16)
            sp.dma_start(c_tm[0:1, :], T["c_prompt"]).then_inc(c_in, 16)
            sp.dma_start(c_tm[1:NB + 1, :], T["c_sample"]).then_inc(c_in, 16)
            for n in range(PANELS):
                wait(sp, panel_used, n - 3)
                sp.dma_start(panel[n % 4], ada[:, :, n * 256:(n + 1) * 256]).then_inc(loaded[n % 4], 16)
            sp.wait_ge(evac_v, 3 + TT + 1)
            sp.wait_ge(evac_a, TT + 1)
            sp.dma_start(T["x_spill"], s.xT[:, :, :]).then_inc(s.spilled, 16)

        @block.gpsimd
        def _(pool):
            for new, old in ((T["s_wk"], T["cache_win_k"]), (T["s_wv"], T["cache_win_v"])):
                pool.dma_start(new[0, :, 0:WIN - 1].rearrange("b t g d -> b (t g d)"),
                               old[0, :, 1:WIN].rearrange("b t g d -> b (t g d)")).then_inc(small, 16)
            pool.wait_ge(small, 32)

        @block.scalar
        def _(act):
            act.dma_start(rows[0:48, :], T["ada_b"][0].rearrange("(r p) -> r p", p=P)).then_inc(x_in, 16)
            act.dma_start(rows[48:56, :], T["norm_attn"][0].rearrange("(r p) -> r p", p=P)).then_inc(x_in, 16)
            act.dma_start(rows[56:64, :], T["norm_ffn"][0].rearrange("(r p) -> r p", p=P)).then_inc(x_in, 16)
            act.dma_start(rows[64:72, :], T["hg_lb"].rearrange("a (r p) -> (a r) p", p=P)).then_inc(x_in, 16)
            act.dma_start(rows[72:73, :], T["hg_norm"]).then_inc(x_in, 16)
            act.dma_start(crow[0:66, :], T["conv_w"][0].rearrange("j (r p) -> (j r) p", p=P)).then_inc(x_in, 16)
            act.dma_start(crow[66:88, :], T["conv_b"][0].rearrange("(r p) -> r p", p=P)).then_inc(x_in, 16)
            act.dma_start(x_tm[:, 0:TT, :], T["x_prompt"][0].rearrange("(t p) d -> p t d", p=P)).then_inc(x_in, 16)
            act.dma_start(x_tm[0:NB, TT, :], T["x_sample"].rearrange("b t d -> (b t) d")).then_inc(x_in, 16)
            act.dma_start(add_f, T["c_add"]).then_inc(x_in, 16)
            act.dma_start(s.rope[:, 0:TT, :], T["c_rope"][0:SEQ].rearrange("(t p) c -> p t c", p=P)).then_inc(x_in, 16)
            act.dma_start(s.rope[0:NB, TT, :], T["c_rope"][SEQ:TOK]).then_inc(x_in, 16)
            act.dma_start(s.gain[:, 0, :], T["q_gain"].partition_broadcast(P).rearrange("p a d -> p (a d)")).then_inc(x_in, 16)
            act.dma_start(s.gain[:, 1:4, :], T["k_gain"][0].partition_broadcast(P)).then_inc(x_in, 16)
            for g in range(1, NGRP, 2):
                t, half = g // 2, g % 2
                n = rows_of(t)
                act.wait_ge(tr_done, 4 + g)
                act.activation(s.xT[:, 4 * half:4 * half + 4, t * P:t * P + n],
                               view(s.ps[2 + g % 4], 0, 4, P)[:, :, 0:n], ACT.Copy).then_inc(evac_a, 1)
            act.wait_ge(x_in, 224)

        @block.tensor
        def _(pe):
            pe.wait_ge(c_in, 48)
            for k in range(KT):
                last = pe.transpose(s.ps[1][:, 9 * k:9 * k + 9], c_tm[0:9, k * P:(k + 1) * P], s.ident[0:9, 0:9])
            last.then_inc(tr_done, 1)
            pe.wait_ge(x_in, 224)
            pe.transpose(s.ps[2][:, 0:73], rows[0:73, :], s.ident[0:73, 0:73]).then_inc(tr_done, 1)
            pe.transpose(s.ps[3][:, 0:88], crow[0:88, :], s.ident[0:88, 0:88]).then_inc(tr_done, 1)
            for g in range(NGRP):
                t, half = g // 2, g % 2
                n = rows_of(t)
                if g < 2:
                    pe.wait_ge(evac_v, 3)
                elif g >= 4:
                    if g % 2:
                        pe.wait_ge(evac_a, (g - 4) // 2 + 1)
                    else:
                        pe.wait_ge(evac_v, 3 + (g - 4) // 2 + 1)
                for j in range(4):
                    k = 4 * half + j
                    last = pe.transpose(s.ps[2 + g % 4][:, j * P:j * P + n], x_tm[0:n, t, k * P:(k + 1) * P],
                                        s.ident[0:n, 0:n])
                last.then_inc(tr_done, 1)
            pe.wait_ge(ready, 1)
            for n in range(PANELS):
                pe.wait_ge(loaded[n % 4], 16 * (n // 4 + 1))
                for h in range(2):
                    for k in range(KT):
                        last = pe.matmul(s.ps[0][:, (2 * n + h) * 9:(2 * n + h + 1) * 9],
                                         panel[n % 4][:, k, h * P:(h + 1) * P], s.cT[:, k, :],
                                         start=(k == 0), stop=(k == KT - 1))
                last.then_inc(panel_used, 1)
            pe.wait_ge(panel_used, PANELS)
            pe.sem_inc(ada_done, 1)

        @block.vector
        def _(v):
            ch = s.dve_chain
            v.memset(s.ones[:, :], 1.0)
            ch.link(v, v.memset(s.eps[:, :], EPS))
            v.wait_ge(tr_done, 1)
            v.tensor_copy(s.cT[:, :, :], view(s.ps[1], 0, KT, 9)).then_inc(ready, 1)
            v.wait_ge(c_in, 48)
            v.tensor_copy(s.identb[:, :], s.ident[:, :])
            v.wait_ge(tr_done, 3)
            v.wait_ge(x_in, 224)
            v.tensor_copy(s.add[:, :, :], add_f)
            v.tensor_copy(s.vec[:, 0:73], s.ps[2][:, 0:73]).then_inc(evac_v, 1)
            v.tensor_copy(s.conv[:, :, :], view(s.ps[3], 0, 4, FT)).then_inc(evac_v, 1)
            v.wait_ge(evac_v, 2)
            v.nop().then_inc(evac_v, 1)
            for g in range(0, NGRP, 2):
                t, half = g // 2, g % 2
                n = rows_of(t)
                v.wait_ge(tr_done, 4 + g)
                v.tensor_copy(s.xT[:, 4 * half:4 * half + 4, t * P:t * P + n],
                              view(s.ps[2 + g % 4], 0, 4, P)[:, :, 0:n]).then_inc(evac_v, 1)
            v.wait_ge(ada_done, 1)
            finish_modulation(s, v, 0, G1, s.ps[0])
            scale_gain(s, v, s.A1, SC1, 48)


def finish_modulation(s, v, first, end, ps):
    n = end - first
    s.dve_chain.link(v, v.tensor_tensor(s.mod[:, first:end, :], view(ps, 0, n, 9),
                                        bc(s.vec[:, first:end].unsqueeze(2), (P, n, 9)), ALU.add))


def scale_gain(s, v, A, scale, gain):
    ch = s.dve_chain
    ch.link(v, v.tensor_scalar(A[:, :, :], s.mod[:, scale:scale + KT, :], 1.0, None, ALU.add))
    ch.link(v, v.tensor_tensor(A[:, :, :], A[:, :, :], bc(s.vec[:, gain:gain + KT].unsqueeze(2), (P, KT, 9)), ALU.mult))


def high(eng, hi, src):
    return eng.tensor_copy(hi, src)


def low(eng, lo, src, hi):
    return eng.tensor_tensor(lo, src, hi, ALU.subtract)


def product(pe, out, w, x, first, last):
    pe.matmul(out, w[0], x[0], start=first, stop=False)
    pe.matmul(out, w[0], x[1], start=False, stop=False)
    return pe.matmul(out, w[1], x[0], start=False, stop=last)


def stage_norm(nc, s, name, A, shift, hi, lo, lo_r, spilled=None):
    sq = [view(s.ring, 1032 * i, TOK) for i in range(2)]
    lnv = view(s.ring, 2064, TOK)
    rstd = view(s.ring, 3096, TOK)
    tmp = view(s.ring, 4128, KT, NB)
    squared, summed, used = s.sem(f"{name}_squared"), s.sem(f"{name}_summed"), s.sem(f"{name}_used")
    rstd_ready, scaled, shifted = s.sem(f"{name}_rstd"), s.sem(f"{name}_scaled"), s.sem(f"{name}_shifted")
    cut = s.sem(f"{name}_cut")
    h = lo

    with nc.Block() as block:
        @block.scalar
        def _(act):
            ch = s.act_chain
            for k in range(KT):
                if k >= 2:
                    act.wait_ge(used, k - 1)
                act.activation(sq[k % 2], s.xT[:, k, :], ACT.Square).then_inc(squared, 1)
            act.wait_ge(summed, 1)
            for c in range(3):
                last = act.activation(lnv[:, c * CH:(c + 1) * CH], s.ps[c][:, 0:CH], ACT.Ln,
                                      bias=s.eps[:, 0:1], scale=1.0 / D)
            ch.link(act, last)
            act.activation(rstd, lnv, ACT.Exp, scale=-0.5).then_inc(rstd_ready, 1)
            for k in range(KT):
                act.wait_ge(scaled, k + 1)
                act.activation(h[:, k, 0:SEQ], h[:, k, 0:SEQ], ACT.Identity,
                               bias=s.mod[:, shift + k, 0:1]).then_inc(shifted, 1)
            act.wait_ge(shifted, KT)

        @block.tensor
        def _(pe):
            for k in range(KT):
                pe.wait_ge(squared, k + 1)
                for c in range(3):
                    last = pe.matmul(s.ps[c][:, 0:CH], s.ones[:, :], sq[k % 2][:, c * CH:(c + 1) * CH],
                                     start=(k == 0), stop=(k == KT - 1))
                last.then_inc(used, 1)
            pe.wait_ge(used, KT)
            pe.sem_inc(summed, 1)

        @block.vector
        def _(v):
            ch = s.dve_chain

            def split(k):
                v.wait_ge(shifted, k + 1)
                high(v, hi[:, k, :], lo[:, k, :]).then_inc(cut, 1)
                v.wait_ge(cut, k + 1)
                if k % 3:
                    ch.link(v, low(v, lo_r[:, k, :], lo[:, k, :], hi[:, k, :]))

            v.wait_ge(rstd_ready, 1)
            if spilled:
                v.wait_ge(spilled, 16)
            ch.link(v, v.tensor_tensor(tmp, s.xT[:, :, SEQ:TOK], A[:, :, 1:NB + 1], ALU.mult))
            ch.link(v, v.tensor_tensor(tmp, tmp, bc(rstd[:, SEQ:TOK].unsqueeze(1), (P, KT, NB)), ALU.mult))
            ch.link(v, v.tensor_tensor(h[:, :, SEQ:TOK], tmp, s.mod[:, shift:shift + KT, 1:NB + 1], ALU.add))
            for k in range(KT):
                v.scalar_tensor_tensor(out=h[:, k, 0:SEQ], in0=s.xT[:, k, 0:SEQ], scalar=A[:, k, 0:1],
                                       in1=rstd[:, 0:SEQ], op0=ALU.mult, op1=ALU.mult).then_inc(scaled, 1)
                if k >= 1:
                    split(k - 1)
            split(KT - 1)

        @block.gpsimd
        def _(pool):
            ch = s.pool_chain
            for k in range(0, KT, 3):
                pool.wait_ge(cut, k + 1)
                ch.link(pool, low(pool, lo_r[:, k, :], lo[:, k, :], hi[:, k, :]))


def stage_token_major(nc, s, T):
    groups = ((C_Q, 512), (C_KC, 384), (C_VS, 408), (C_HI, 512))
    home, short = (s.ring, s.work), (s.ring_short, s.work_short)
    raw = [view(home[g % 2], 4096, KT, w) for g, (_, w) in enumerate(groups)]
    w_hi, w_lo = ([short[g % 2](at, KT, w) for g, (_, w) in enumerate(groups)] for at in (0, 4096))
    cut, split = s.sem("t_cut"), s.sem("t_split")
    w_in = T["w_in"][0].rearrange("(k p) n -> p k n", p=P)
    F = 21576
    sq = [view(s.work, F + 512 * i, 512) for i in range(2)]
    stat = [view(s.work, F + 1024 + 64 * i, 64) for i in range(2)]
    rot = [view(s.work, F + 1152 + 256 * i, 256) for i in range(2)]
    qn = [view(s.work, F + 1664 + 512 * i, 512) for i in range(2)]
    kn = [view(s.work, F + 2688 + 384 * i, 384) for i in range(2)]
    NT = TT + 1
    UNITS = 4 * NT
    n_psum = 3
    w_loaded = [s.sem(f"t_w{i}") for i in range(4)]
    mm, act_free, dve_free = s.sem("t_mm"), s.sem("t_act_free"), s.sem("t_dve_free")
    squared, summed, rstd_ready = s.sem("t_squared"), s.sem("t_summed"), s.sem("t_rstd")
    normed, turned, turn_read = s.sem("t_normed"), s.sem("t_turned"), s.sem("t_turn_read")
    copied = s.sem("t_copied")
    sent = [s.sem(f"t_sent{i}") for i in range(2)]
    sent_v = s.sem("t_sent_v")

    with nc.Block() as block:
        @block.gpsimd
        def _(pool):
            def take_low(g):
                pool.wait_ge(cut, g + 1)
                low(pool, w_lo[g], raw[g], w_hi[g]).then_inc(split, 1)

            for g, (c, w) in enumerate(groups):
                if g >= 2:
                    pool.wait_ge(mm, (g - 1) * NT)
                pool.dma_start(raw[g], w_in[:, :, c:c + w]).then_inc(w_loaded[g], 16)
                if g:
                    take_low(g - 1)
            take_low(3)

        @block.sync
        def _(sp):
            for u in range(NT, 3 * NT):
                g, t = u // NT, u % NT
                n = rows_of(t)
                st = kn[u % 2]
                sp.wait_ge(normed, u + 1)
                sp.wait_ge(copied, u + 1)
                rows = slice(t * P, t * P + P)
                flat = lambda a: a.rearrange("t g d -> t (g d)")
                if g == 1:
                    for j, (pr, sa) in enumerate(((T["p_ck"], T["s_ck"]), (T["p_cv"], T["s_cv"]), (T["p_sk"], T["s_sk"]))):
                        dst = flat(pr[0, 0, rows]) if t < TT else flat(sa[0, :, 0])
                        sp.dma_start(dst, st[0:n, j * P:(j + 1) * P]).then_inc(sent[u % 2], 16)
                else:
                    dst = flat(T["p_sv"][0, 0, rows]) if t < TT else flat(T["s_sv"][0, :, 0])
                    sp.dma_start(dst, s.vkv[0:n, t, 0, :]).then_inc(sent_v, 16)
                    if t >= TT - WIN // P:
                        rows = slice((t - TT + WIN // P) * P, (t - TT + WIN // P + 1) * P)
                        dst = flat(T["p_wk"][0, 0, rows]) if t < TT else flat(T["s_wk"][0, :, WIN - 1])
                        sp.dma_start(dst, st[0:n, 0:P]).then_inc(sent[u % 2], 16)
                        dst = flat(T["p_wv"][0, 0, rows]) if t < TT else flat(T["s_wv"][0, :, WIN - 1])
                        sp.dma_start(dst, s.vkv[0:n, t, 1, :]).then_inc(sent_v, 16)
            sp.wait_ge(copied, UNITS)
            sp.dma_start(T["hi_rows"], s.vhi[0:NB, TT, :]).then_inc(sent_v, 16)
            sp.dma_start(T["gate_rows"], s.gates[0:NB, TT, :]).then_inc(sent_v, 16)
            sp.wait_ge(sent_v, 16 * (NT + WIN // P + 1 + 2))
            for b in range(2):
                sp.wait_ge(sent[b], 16 * sum((3 if u < 2 * NT else u % NT >= TT - WIN // P)
                                             for u in range(NT, 3 * NT) if u % 2 == b))

        @block.tensor
        def _(pe):
            def turn(u):
                g, t = u // NT, u % NT
                if u < 0 or g > 2:
                    return
                n = rows_of(t)
                pe.wait_ge(normed, u + 1)
                if u >= 2:
                    pe.wait_ge(turn_read, u - 1)
                out = s.ps[6 + u % 2]
                if g == 0:
                    for j in range(HPG):
                        last = pe.transpose(out[:, j * P:j * P + n], qn[u % 2][0:n, j * P:(j + 1) * P],
                                            s.ident[0:n, 0:n])
                else:
                    at = 256 if g == 1 else 0
                    last = pe.transpose(out[:, 0:n], kn[u % 2][0:n, at:at + P], s.ident[0:n, 0:n])
                last.then_inc(turned, 1)

            for u in range(UNITS):
                g, t = u // NT, u % NT
                n, w = rows_of(t), groups[g][1]
                if t == 0:
                    pe.wait_ge(split, g + 1)
                if u >= n_psum:
                    pe.wait_ge(act_free, u - n_psum + 1)
                    pe.wait_ge(dve_free, u - n_psum + 1)
                cols = slice(t * P, t * P + n)
                for k in range(KT):
                    last = product(pe, s.ps[u % n_psum][0:n, 0:w], (s.hT[:, k, cols], s.xT_r[:, k, cols]),
                                   (w_hi[g][:, k, :], w_lo[g][:, k, :]), k == 0, k == KT - 1)
                last.then_inc(mm, 1)
                turn(u - 1)

        @block.scalar
        def _(act):
            ch = s.act_chain

            def evacuate(u):
                g, t = u // NT, u % NT
                n = rows_of(t)
                act.wait_ge(turned, u + 1)
                cols = slice(t * P, t * P + n)
                if g == 0:
                    src = view(s.ps[6 + u % 2], 0, HPG, P)[:, :, 0:n]
                    act.activation(s.qT[:, :, cols], src, ACT.Copy).then_inc(turn_read, 1)
                else:
                    dst = s.ksT if g == 1 else s.kwT
                    act.activation(dst[:, cols], s.ps[6 + u % 2][:, 0:n], ACT.Copy).then_inc(turn_read, 1)

            for u in range(UNITS):
                g, t = u // NT, u % NT
                n = rows_of(t)
                ps = s.ps[u % n_psum]
                act.wait_ge(mm, u + 1)
                if g == 3:
                    ch.link(act, act.activation(s.vhi[0:n, t, :], ps[0:n, :], ACT.Copy))
                    act.nop().then_inc(act_free, 1)
                    act.nop().then_inc(copied, 1)
                    if u == 3 * NT:
                        evacuate(u - 1)
                    continue
                if u >= 2:
                    act.wait_ge(summed, u - 1)
                if g == 0:
                    act.activation(sq[u % 2][0:n, :], ps[0:n, :], ACT.Square).then_inc(squared, 1)
                elif g == 1:
                    if u >= NT + 2:
                        act.wait_ge(sent[u % 2], 16 * 3 * ((u - NT) // 2))
                    act.activation(kn[u % 2][0:n, P:2 * P], ps[0:n, P:2 * P], ACT.Copy)
                    act.activation(sq[u % 2][0:n, 0:384], ps[0:n, 0:384], ACT.Square).then_inc(squared, 1)
                else:
                    act.activation(s.vkv[0:n, t, :, :], ps[0:n, 0:512].rearrange("p (a c) -> p a c", a=2)[:, :, 0:P],
                                   ACT.Copy)
                    act.activation(s.gates[0:n, t, :], ps[0:n, 384:408], ACT.Exp, scale=-1.0)
                    act.activation(sq[u % 2][0:n, 0:P], ps[0:n, P:2 * P], ACT.Square).then_inc(squared, 1)
                act.wait_ge(squared, u + 1)
                act.nop().then_inc(act_free, 1)
                act.nop().then_inc(copied, 1)
                if u >= 1:
                    evacuate(u - 1)
                act.wait_ge(summed, u + 1)
                st = stat[u % 2]
                ch.link(act, act.activation(st[0:n, 8:16], st[0:n, 0:8], ACT.Ln, bias=s.eps[0:n, 0:1],
                                            scale=1.0 / HD))
                act.activation(st[0:n, 16:24], st[0:n, 8:16], ACT.Exp, scale=-0.5).then_inc(rstd_ready, 1)

        @block.vector
        def _(v):
            ch = s.dve_chain
            for i in range(2):
                ch.link(v, v.memset(stat[i], 1.0))
            ch.link(v, v.tensor_scalar(s.gain[:, 0, :], s.gain[:, 0, :], SCALE, None, ALU.mult))
            def cut_weights(g):
                v.wait_ge(w_loaded[g], 16)
                high(v, w_hi[g], raw[g]).then_inc(cut, 1)

            cut_weights(0)
            cut_weights(1)
            for u in range(3 * NT):
                if u in (NT + 4, 2 * NT + 4):
                    v.wait_ge(mm, (u // NT) * NT)
                    cut_weights(u // NT + 1)
                g, t = u // NT, u % NT
                n = rows_of(t)
                ps, st, sqt = s.ps[u % n_psum], stat[u % 2], sq[u % 2]
                if g == 0:
                    kinds, heads, gain, out = NG, HPG, 0, qn[u % 2]
                elif g == 1:
                    kinds, heads, gain, out = 2, NG, 1, kn[u % 2]
                else:
                    kinds, heads, gain, out = 1, NG, 3, kn[u % 2]

                def parts(tile, at=0):
                    if g == 1:
                        return tile[0:n, 0:384].rearrange("p (k h d) -> p k h d", k=3, d=HD)[:, 0:3:2]
                    return tile[0:n, at:at + kinds * heads * HD].rearrange("p (k h d) -> p k h d", k=kinds, d=HD)
                v.wait_ge(squared, u + 1)
                sums = st[0:n, 0:kinds * heads].rearrange("p (k h) -> p k h", k=kinds)
                v.tensor_reduce(sums, parts(sqt), AX.X, ALU.add).then_inc(summed, 1)
                v.wait_ge(rstd_ready, u + 1)
                shape = (n, kinds, heads, HD)
                rstd = st[0:n, 16:16 + kinds * heads].rearrange("p (k h) -> p k h", k=kinds).unsqueeze(3)
                dst = parts(out) if g else out[0:n, :].rearrange("p (h k d) -> p k h d", k=NG, d=HD)
                if u >= 2:
                    v.wait_ge(turned, u - 1)
                if g >= 1 and u >= NT + 2:
                    done = sum((3 if w < 2 * NT else w % NT >= TT - WIN // P)
                               for w in range(NT, u - 1) if w % 2 == u % 2)
                    v.wait_ge(sent[u % 2], 16 * done)
                ch.link(v, v.tensor_tensor(dst, parts(ps, P if g == 2 else 0), bc(rstd, shape), ALU.mult))
                v.nop().then_inc(dve_free, 1)
                for kd in range(kinds):
                    row = s.gain[0:n, gain + (kd if g else 0), :].unsqueeze(1)
                    last = v.tensor_tensor(dst[:, kd], dst[:, kd], bc(row, (n, heads, HD)), ALU.mult)
                ch.link(v, last)
                for kd in range(kinds):
                    x = dst[:, kd, :, 0:16]
                    a, b = (r[0:n, kd * 128:kd * 128 + heads * 16].rearrange("p (h c) -> p h c", c=16) for r in rot)
                    v.tensor_tensor(a, x, bc(s.rope[0:n, t, 0:16].unsqueeze(1), (n, heads, 16)), ALU.mult)
                    ch.link(v, v.tensor_tensor(b, x, bc(s.rope[0:n, t, 16:32].unsqueeze(1), (n, heads, 16)), ALU.mult))
                    v.tensor_tensor(x[:, :, 0:8], a[:, :, 0:8], b[:, :, 8:16], ALU.subtract)
                    ch.link(v, v.tensor_tensor(x[:, :, 8:16], a[:, :, 8:16], b[:, :, 0:8], ALU.add))
                if g == 2:
                    ga = s.gates[0:n, t, :]
                    ch.link(v, v.tensor_scalar(ga, ga, 1.0, None, ALU.add))
                    ch.link(v, v.reciprocal(ga, ga))
                v.nop().then_inc(normed, 1)
            for u in range(3 * NT, UNITS):
                v.nop().then_inc(dve_free, 1)


def stage_compress(nc, s, T):
    rows = [view(s.ring, 2048 * a, CMP_STRIDE, P) for a in range(2)]
    pairs = [view(s.ring, 4096 + 2048 * a, NG, 8, P) for a in range(2)]
    w1 = view(s.work, X3 + 1888, 2, 8, 2 * HD)
    w2 = view(s.work, 24392, 3, HD)
    pe_rows = view(s.work, X3 + 128, P)
    peT = view(s.work, X3 + 256, 2, 2, 8)
    pe_h = view(s.work, X3 + 288, 2)
    lifted = [view(s.work, X3 + 320 + 256 * a, NG, P) for a in range(2)]
    hid = [view(s.work, X3 + 832 + 256 * a, NG, P) for a in range(2)]
    act_h = [view(s.work, X3 + 1344 + 256 * a, NG, P) for a in range(2)]
    pages = view(s.work, X3 + 1856, NB)
    pages_f = view(s.work, X3 + 1864, NB)
    sub = view(s.work, X3 + 1872, 1)
    small, idx_ready = s.sem("c_small"), s.sem("c_idx")
    rows_in = [s.sem(f"c_rows{a}") for a in range(2)]
    prompt_in = [s.sem(f"c_prompt{a}") for a in range(2)]
    turned, mixed, made = s.sem("c_turned"), s.sem("c_mixed"), s.sem("c_made")
    evac_a, evac_v = s.sem("c_evac_a"), s.sem("c_evac_v")
    lift, summed, gelu, placed = s.sem("c_lift"), s.sem("c_summed"), s.sem("c_gelu"), s.sem("c_placed")
    pe_terms, pe_read = s.sem("c_pe_terms"), s.sem("c_pe_read")

    def pipeline(eng, first, second, third):
        first(0, 0, NSUB_P)
        first(0, 1, NSUB_P)
        second(0, 0, NSUB_P)
        first(1, 0, NSUB_S)
        second(0, 1, NSUB_P)
        third(0, 0, NSUB_P)
        first(1, 1, NSUB_S)
        second(1, 0, NSUB_S)
        third(0, 1, NSUB_P)
        with eng.Fori(2, NB + 1) as q:
            first(q, 0, NSUB_S)
            second(q - 1, 1, NSUB_S)
            third(q - 1, 0, NSUB_S)
            first(q, 1, NSUB_S)
            second(q, 0, NSUB_S)
            third(q - 1, 1, NSUB_S)
        second(NB, 1, NSUB_S)
        third(NB, 0, NSUB_S)
        third(NB, 1, NSUB_S)

    def nothing(q, a, n):
        pass

    with nc.Block() as block:
        @block.sync
        def _(sp):
            for a in range(2):
                for r in range(2):
                    sp.dma_start(w1[:, a, :, r * HD:(r + 1) * HD],
                                 T["cmp_w1"][0, a, r * 1024:(r + 1) * 1024].rearrange("(e q) h -> q e h", q=P)
                                 ).then_inc(small, 16)
                sp.dma_start(w2[0:HD, a, :], T["cmp_w2"][0, 0]).then_inc(small, 16)
            sp.dma_start(pe_rows[0:32, :], T["cmp_pe"][0].rearrange("a (r q) d -> (a r) (q d)", q=2)).then_inc(small, 16)
            sp.dma_start(w2[0:HD, 2, :], T["cmp_w2"][0, 1]).then_inc(small, 16)
            sp.dma_start(sub, T["c_sub"]).then_inc(small, 16)
            sp.dma_start(pages.bitcast(I32), T["page_rows"]).then_inc(small, 16)
            for a, src in enumerate((T["p_ck"], T["p_cv"])):
                sp.dma_start(rows[a][0:NSUB_P].rearrange("p t c -> p (t c)"),
                             src[0, 0].rearrange("(n t) g d -> n (t g d)", t=CMP_STRIDE)).then_inc(prompt_in[a], 16)

        @block.gpsimd
        def _(pool):
            pool.wait_ge(idx_ready, 1)
            for b in range(NB):
                for a, src in enumerate((T["cache_cmp_k"], T["cache_cmp_v"])):
                    pool.wait_ge(turned, 4 * (2 * b + a) + 4)
                    pool.indirect_dma_start(
                        out=rows[a].rearrange("p t c -> p (t c)"), out_offset=None,
                        in_=src[0].rearrange("n (j t) g d -> (n j) (t g d)", t=CMP_STRIDE),
                        in_offset=bass.IndirectOffsetOnAxis(ap=s.gidx[:, b:b + 1], axis=0)).then_inc(rows_in[a], 16)

        @block.tensor
        def _(pe):
            pe.wait_ge(small, 160)
            pe.transpose(s.ps[6][:, 0:32], pe_rows[0:32, :], s.ident[0:32, 0:32]).then_inc(pe_terms, 1)
            pe.wait_ge(pe_read, 1)
            for a in range(2):
                for r in range(2):
                    for e in range(8):
                        last = pe.matmul(s.ps[7][0:HD, a:a + 1], w1[:, a, e, r * HD:(r + 1) * HD],
                                         peT[:, a, r, e:e + 1], start=(r + e == 0), stop=(r * e == 7))
            last.then_inc(pe_terms, 1)
            pe.wait_ge(pe_read, 2)

            def turn(q, a, n):
                pe.wait_ge(*((prompt_in[a], 16) if isinstance(q, int) and q == 0 else (rows_in[a], 16 * q)))
                for bank in range(4):
                    wait(pe, evac_a if bank % 2 else evac_v, 2 * (2 * q + a - 1) + bank // 2 + 1)
                    for j in range(4):
                        last = pe.transpose(s.ps[bank][:, j * P:j * P + n], rows[a][0:n, 4 * bank + j, :],
                                            s.ident[0:n, 0:n])
                    last.then_inc(turned, 1)

            def mix(q, a, n):
                pe.wait_ge(evac_a, 2 * (2 * q + a) + 2)
                pe.wait_ge(evac_v, 2 * (2 * q + a) + 2)
                wait(pe, summed, 2 * q + a - 1)
                out = view(s.ps[4 + a], 0, NG, P)[:, :, 0:n]
                for e in range(8):
                    last = pe.matmul(out, w1[:, a, e, :], pairs[a][:, :, e, 0:n], start=(e == 0), stop=(e == 7))
                last.then_inc(mixed, 1)

            def make(q, a, n):
                m = n - 1
                pe.wait_ge(gelu, 2 * q + a + 1)
                wait(pe, placed, 2 * q + a - 1)
                for g in range(NG):
                    if a == 0:
                        last = pe.matmul(s.ps[6][:, g * P:g * P + m], w2[0:HD, 0:2, :].rearrange("p a d -> p (a d)"),
                                         act_h[0][0:HD, g, 0:m], start=True, stop=True)
                    else:
                        last = pe.matmul(s.ps[7][0:m, g * HD:(g + 1) * HD], act_h[1][0:HD, g, 0:m], w2[0:HD, 2, :],
                                         start=True, stop=True)
                last.then_inc(made, 1)

            pipeline(pe, turn, mix, make)

        def evacuate(eng, copy, done, banks):
            def run(q, a, n):
                wait(eng, mixed, 2 * q + a - 1)
                for bank in banks:
                    eng.wait_ge(turned, 4 * (2 * q + a) + bank + 1)
                    src = view(s.ps[bank], 0, 2, 2, P)
                    for s2 in range(2):
                        for g in range(NG):
                            last = copy(pairs[a][s2 * HD:(s2 + 1) * HD, g, 2 * bank:2 * bank + 2, 0:n],
                                        src[g * HD:(g + 1) * HD, :, s2, 0:n])
                    last.then_inc(done, 1)
            return run

        @block.scalar
        def _(act):
            act.wait_ge(pe_terms, 1)

            def lift_gelu(q, a, n):
                m = n - 1
                act.wait_ge(mixed, 2 * q + a + 1)
                wait(act, summed, 2 * q + a - 1)
                src = view(s.ps[4 + a], 0, NG, P)
                act.activation(lifted[a][0:HD, :, 0:m], src[HD:P, :, 1:n], ACT.Identity,
                               bias=pe_h[0:HD, a:a + 1]).then_inc(lift, 1)
                act.wait_ge(summed, 2 * q + a + 1)
                wait(act, made, 2 * q + a - 1)
                act.activation(act_h[a][0:HD, :, 0:m], hid[a][0:HD, :, 0:m], ACT.Gelu_apprx_tanh).then_inc(gelu, 1)

            act.wait_ge(pe_read, 2)
            pipeline(act, evacuate(act, lambda o, i: act.activation(o, i, ACT.Copy), evac_a, (1, 3)), lift_gelu, nothing)

        @block.vector
        def _(v):
            ch = s.dve_chain
            v.wait_ge(small, 160)
            ch.link(v, v.tensor_copy(pages_f, pages.bitcast(I32)))
            ch.link(v, v.tensor_scalar(pages_f, pages_f, float(SUB_PER_PAGE), sub[:, 0:1], ALU.mult, ALU.add))
            v.tensor_copy(s.gidx[:, :], pages_f).then_inc(idx_ready, 1)
            v.wait_ge(pe_terms, 1)
            v.tensor_copy(view(s.work, X3 + 256, 32), s.ps[6][:, 0:32]).then_inc(pe_read, 1)
            v.wait_ge(pe_terms, 2)
            v.tensor_copy(pe_h[0:HD, :], s.ps[7][0:HD, 0:2]).then_inc(pe_read, 1)

            def add(q, a, n):
                m = n - 1
                v.wait_ge(lift, 2 * q + a + 1)
                wait(v, gelu, 2 * q + a - 1)
                src = view(s.ps[4 + a], 0, NG, P)
                v.tensor_tensor(hid[a][0:HD, :, 0:m], src[0:HD, :, 0:m], lifted[a][0:HD, :, 0:m],
                                ALU.add).then_inc(summed, 1)

            def place(q, a, n):
                m = n - 1
                v.wait_ge(made, 2 * q + a + 1)
                if a == 0:
                    keys = s.kcT.rearrange("p q n -> p (q n)")
                    for g in range(NG):
                        half = slice(g * HD, (g + 1) * HD)
                        last = v.tensor_copy(keys[half, bass.ds(q * P, m)], s.ps[6][half, g * P:g * P + m])
                else:
                    values = s.vc.rearrange("p q n -> p (q n)")
                    last = v.tensor_copy(values[0:m, bass.ds(q * P, P)], s.ps[7][0:m, 0:P])
                last.then_inc(placed, 1)

            pipeline(v, evacuate(v, v.tensor_copy, evac_v, (0, 2)), add, place)


def stage_prompt_attention(nc, s, T):
    prob = [view(s.ring, 1024 * i, 1024) for i in range(2)]
    probT = [view(s.ring, 2048 + 1024 * i, 1024) for i in range(2)]
    o_tm = [view(s.ring, 4096 + 512 * i, 512) for i in range(2)]
    part = view(s.ring, 5120, 512)
    top = view(s.ring, 5632, 2, 8)
    total = view(s.ring, 5648, 4, 8)
    coef = view(s.ring, 5680, 8)
    cmp_add = view(s.work, 23880, 256).bitcast(BF16).rearrange("p (t n) -> p t n", t=TT)
    cmp_add_f = view(s.ring, 6144, TT, HD)
    cmp_mul = view(s.ring, 6656, TT, HD)
    score = [s.psall[:, 1024 * i:1024 * (i + 1)] for i in range(2)]
    turn_ps = [s.ps[4], s.ps[5]]
    out_ps = [s.ps[6], s.ps[7]]
    masks_in, mask_cast = s.sem("a_masks"), s.sem("a_mask_cast")
    scored, maxed, exped, masked = s.sem("a_scored"), s.sem("a_maxed"), s.sem("a_exped"), s.sem("a_masked")
    turned, pv, combined = s.sem("a_turned"), s.sem("a_pv"), s.sem("a_combined")
    moved = [s.sem("a_moved_v"), s.sem("a_moved_a")]

    units = []
    for t in range(TT):
        units.append(Unit(kind=0, t=t, h=0, lo=0, n=TT // 2, last=True))
        for kind in (1, 2):
            for h in range(NH):
                lo = 0 if kind == 1 else max(0, t - WIN // P)
                units.append(Unit(kind=kind, t=t, h=h, lo=lo, n=t + 1 - lo, last=h == NH - 1))
        if t:
            units.insert(len(units) - 8, Unit(kind=3, t=t - 1, h=0, lo=0, n=4, last=False))
    units.append(Unit(kind=3, t=TT - 1, h=0, lo=0, n=4, last=False))
    chunk = real = 0
    for u in units:
        u.chunks = []
        width = 8 if u.kind == 0 else u.n
        for c0 in range(0, width, 4):
            u.chunks.append((chunk, c0, min(4, width - c0)))
            chunk += 1
        u.branch = 3 * u.t + u.kind
        if u.kind < 3:
            u.i = real
            real += 1
    scored_units = [u for u in units if u.kind < 3]

    def done_chunks(c):
        return c // 2 + 1

    def steps():
        ahead = 2
        for u in units:
            nxt = None
            if u.kind < 3:
                nxt = scored_units[ahead] if ahead < len(scored_units) else None
                ahead += 1
            yield u, nxt

    with nc.Block() as block:
        @block.sync
        def _(sp):
            sp.dma_start(cmp_add_f, T["c_cmp_add"]).then_inc(masks_in, 16)
            sp.dma_start(cmp_mul, T["c_cmp_mul"]).then_inc(masks_in, 16)

        @block.tensor
        def _(pe):
            def scores(u):
                wait(pe, exped, u.i - 1)
                ps = score[u.i % 2]
                if u.kind == 0:
                    for g in range(NG):
                        pe.matmul(ps[:, 512 * g:512 * g + 256], s.identb[:, :],
                                  bc(cmp_add[:, u.t, :].unsqueeze(1), (P, HPG, HD)), start=True, stop=False)
                    for j in range(HPG):
                        for g in range(NG):
                            last = pe.matmul(ps[:, 512 * g + j * HD:512 * g + j * HD + NC_P],
                                             s.qT[g * HD:(g + 1) * HD, j, u.t * P:(u.t + 1) * P],
                                             s.kcT[g * HD:(g + 1) * HD, 0, 0:NC_P], start=False,
                                             stop=(j == HPG - 1))
                else:
                    g, j = u.h // HPG, u.h % HPG
                    keys = s.ksT if u.kind == 1 else s.kwT
                    for c0 in range(0, u.n, 4):
                        c1 = min(u.n, c0 + 4)
                        diag = c1 == u.n
                        far = u.kind == 2 and u.t >= WIN // P and c0 == 0
                        last = pe.matmul(ps[:, c0 * P:c1 * P], s.qT[g * HD:(g + 1) * HD, j, u.t * P:(u.t + 1) * P],
                                         keys[g * HD:(g + 1) * HD, (u.lo + c0) * P:(u.lo + c1) * P],
                                         start=True, stop=not (diag or far))
                        if far:
                            last = pe.matmul(ps[:, 0:P], s.identb[:, :], s.add[:, 1, :], start=False, stop=not diag)
                        if diag:
                            last = pe.matmul(ps[:, (u.n - 1) * P:u.n * P], s.identb[:, :], s.add[:, 0, :],
                                             start=False, stop=True)
                last.then_inc(scored, 1)

            pe.wait_ge(mask_cast, 1)
            scores(scored_units[0])
            scores(scored_units[1])
            for u, nxt in steps():
                if u.kind == 3:
                    pe.wait_ge(combined, 3 * u.t + 3)
                elif u.kind == 0:
                    pe.wait_ge(masked, u.t + 1)
                else:
                    pe.wait_ge(exped, u.i + 1)
                for c, c0, n in u.chunks:
                    wait(pe, moved[c % 2], done_chunks(c) - 1)
                    out = turn_ps[c % 2]
                    for k in range(n):
                        if u.kind == 0:
                            h = c0 + k
                            last = pe.transpose(out[0:NC_P, k * P:(k + 1) * P], prob[u.i % 2][:, h * HD:h * HD + NC_P],
                                                s.ident[:, :])
                        else:
                            src = o_tm[u.t % 2] if u.kind == 3 else prob[u.i % 2]
                            last = pe.transpose(out[:, k * P:(k + 1) * P], src[:, (c0 + k) * P:(c0 + k + 1) * P],
                                                s.ident[:, :])
                    last.then_inc(turned, 1)
                if nxt:
                    scores(nxt)
                if u.kind == 3:
                    continue
                for c, c0, n in u.chunks:
                    pe.wait_ge(moved[c % 2], done_chunks(c))
                out = out_ps[u.branch % 2]
                if u.h == 0:
                    wait(pe, combined, u.branch - 1)
                if u.kind == 0:
                    for h in range(NH):
                        g = h // HPG
                        last = pe.matmul(out[:, h * HD:(h + 1) * HD], probT[u.i % 2][0:NC_P, h * P:(h + 1) * P],
                                         s.vc[0:NC_P, 0, g * HD:(g + 1) * HD], start=True, stop=True)
                else:
                    g = u.h // HPG
                    for k in range(u.n):
                        last = pe.matmul(out[:, u.h * HD:(u.h + 1) * HD], probT[u.i % 2][:, k * P:(k + 1) * P],
                                         s.vkv[:, u.lo + k, u.kind - 1, g * HD:(g + 1) * HD],
                                         start=(k == 0), stop=(k == u.n - 1))
                last.then_inc(pv, 1)

        def copy_chunks(eng, copy, which, u):
            for c, c0, n in u.chunks:
                if c % 2 != which:
                    continue
                eng.wait_ge(turned, c + 1)
                if u.kind == 3:
                    copy(s.oN[:, :, u.t * P:(u.t + 1) * P], view(turn_ps[which], 0, 4, P)).then_inc(moved[which], 1)
                    continue
                wait(eng, pv, u.i - 1)
                rows = NC_P if u.kind == 0 else P
                copy(probT[u.i % 2][0:rows, c0 * P:(c0 + n) * P],
                     turn_ps[which][0:rows, 0:n * P]).then_inc(moved[which], 1)

        @block.scalar
        def _(act):
            def exps(u):
                act.wait_ge(maxed, u.i + 1)
                if u.kind == 0:
                    act.activation(prob[u.i % 2][:, 0:512], prob[u.i % 2][:, 0:512], ACT.Exp).then_inc(exped, 1)
                else:
                    before = [w for w in scored_units if w.i == u.i - 2]
                    if before:
                        act.wait_ge(turned, before[0].chunks[-1][0] + 1)
                    act.activation(prob[u.i % 2][:, 0:u.n * P], score[u.i % 2][:, 0:u.n * P], ACT.Exp,
                                   bias=top[:, u.i % 2, 0:1],
                                   accum_out=total[:, u.branch % 4, u.h:u.h + 1]).then_inc(exped, 1)

            exps(scored_units[0])
            exps(scored_units[1])
            for u, nxt in steps():
                copy_chunks(act, lambda o, i: act.activation(o, i, ACT.Copy), 1, u)
                if nxt:
                    exps(nxt)

        @block.vector
        def _(v):
            ch = s.dve_chain

            def maxima(u):
                v.wait_ge(scored, u.i + 1)
                ps, pr = score[u.i % 2], prob[u.i % 2]
                wait(v, exped, u.i - 1)
                if u.kind:
                    v.tensor_reduce(top[:, u.i % 2, 0:1], ps[:, 0:u.n * P], AX.X, ALU.max,
                                    negate=True).then_inc(maxed, 1)
                    return
                before = [w for w in scored_units if w.i == u.i - 2]
                if before:
                    v.wait_ge(turned, before[0].chunks[-1][0] + 1)
                by_group = lambda x: x.rearrange("p (g j n) -> p g j n", g=NG, n=HD)
                heads = ps.rearrange("p (g j n) -> p g j n", g=NG, n=HD)[:, :, 0:HPG]
                most = top[:, u.i % 2, :].rearrange("p (g j) -> p g j", g=NG)
                ch.link(v, v.tensor_reduce(most, heads, AX.X, ALU.max))
                v.tensor_tensor(by_group(pr[:, 0:512]), heads, bc(most.unsqueeze(3), (P, NG, HPG, HD)),
                                ALU.subtract).then_inc(maxed, 1)
                v.wait_ge(exped, u.i + 1)
                e = pr[:, 0:512].rearrange("p (h n) -> p h n", h=NH)
                ch.link(v, v.tensor_tensor(e, e, bc(cmp_mul[:, u.t, :].unsqueeze(1), (P, NH, HD)), ALU.mult))
                ch.link(v, v.tensor_reduce(total[:, u.branch % 4, :], e, AX.X, ALU.add))
                v.tensor_scalar(total[:, u.branch % 4, :], total[:, u.branch % 4, :], 1e-30, None,
                                ALU.max).then_inc(masked, 1)

            def combine(u):
                v.wait_ge(pv, u.i + 1)
                ch.link(v, v.reciprocal(coef, total[:, u.branch % 4, :]))
                gate = s.gates[:, u.t, :].rearrange("p (h c) -> p h c", c=3)[:, :, u.kind]
                ch.link(v, v.tensor_tensor(coef, coef, gate, ALU.mult))
                src = out_ps[u.branch % 2].rearrange("p (g j d) -> p g j d", g=NG, d=HD)
                pairs = lambda x: x.rearrange("p (j g d) -> p g j d", g=NG, d=HD)
                by = bc(coef.rearrange("p (g j) -> p g j", g=NG).unsqueeze(3), (P, NG, HPG, HD))
                if u.kind == 0:
                    if u.t >= 2:
                        old = [w for w in units if w.kind == 3 and w.t == u.t - 2][0]
                        v.wait_ge(turned, old.chunks[-1][0] + 1)
                    v.tensor_tensor(pairs(o_tm[u.t % 2]), src, by, ALU.mult).then_inc(combined, 1)
                else:
                    v.wait_ge(combined, u.branch)
                    ch.link(v, v.tensor_tensor(pairs(part), src, by, ALU.mult))
                    v.tensor_tensor(o_tm[u.t % 2], o_tm[u.t % 2], part, ALU.add).then_inc(combined, 1)

            v.wait_ge(masks_in, 32)
            v.tensor_copy(cmp_add, cmp_add_f).then_inc(mask_cast, 1)
            maxima(scored_units[0])
            maxima(scored_units[1])
            pending = None
            for u, nxt in steps():
                copy_chunks(v, v.tensor_copy, 0, u)
                if nxt:
                    maxima(nxt)
                if pending:
                    combine(pending)
                    pending = None
                if u.last:
                    pending = u
                    if u.kind == 2 and u.t == TT - 1:
                        combine(u)
                        pending = None


def stage_decode_attention(nc, s, T):
    ROWS = NB * NH
    key_rows = [view(s.ring, 2048 * i, 16, P) for i in range(2)]
    val_rows = [view(s.ring, 4096 + 2048 * i, 16, P) for i in range(2)]
    win_keys = [view(s.ring, 512 * b, 4, P) for b in range(NB)]
    win_vals = [view(s.ring, 4096 + 512 * b, 4, P) for b in range(NB)]
    keysT = [view(s.work, 8256 + 2048 * i, 16, P) for i in range(2)]
    win_keysT = [view(s.work, 8256 + 512 * b, 4, P) for b in range(NB)]
    scT = view(s.work, 12384, 16, ROWS)
    prT = view(s.work, 13408, 16, ROWS)
    rows = view(s.work, X3, 2048)[0:ROWS]
    Y = X3 + 2048
    qbd = view(s.work, Y, ROWS)
    knew = view(s.work, Y + 64, 2, NB)
    gate = view(s.work, Y + 80, 3)[0:ROWS]
    own = view(s.work, Y + 88, NB)[0:ROWS]
    over = view(s.work, Y + 96, NS_S)
    st = view(s.work, Y + 136, 16)[0:ROWS]
    cmp_rows = view(s.work, Y + 152, P)[0:ROWS]
    cmp_pT = view(s.work, Y + 280, ROWS)
    cmp_sc = view(s.work, Y + 344, ROWS)
    imp = view(s.work, Y + 408, NS_S)[0:ROWS]
    grp = view(s.work, Y + 448, NB * NG)
    grp_all = view(s.work, Y + 464, ROWS)
    pen = view(s.work, Y + 528, NS_S)[0:ROWS]
    new_d = view(s.work, Y + 568, NB)[0:ROWS]
    new_dT = view(s.work, Y + 576, 2, ROWS)
    gt = view(s.work, 23880, NS_S * NS_S)[0:ROWS]
    eq = view(s.work, Y + 704, NS_S * NS_S)[0:ROWS]
    lower = view(s.work, 14448, NS_S * NS_S)[0:ROWS]
    small, q_ready = s.sem("d_small"), s.sem("d_q_ready")
    k_in = [s.sem(f"d_k{i}") for i in range(2)]
    v_in = [s.sem(f"d_v{i}") for i in range(2)]
    wk_in, wv_in = s.sem("d_wk"), s.sem("d_wv")
    turned, evac_v, evac_a = s.sem("d_turned"), s.sem("d_evac_v"), s.sem("d_evac_a")
    dotted, dots_read = s.sem("d_dotted"), s.sem("d_dots_read")
    pe_to_v, v_to_pe = s.sem("d_pe_to_v"), s.sem("d_v_to_pe")
    v_to_a, a_to_v = s.sem("d_v_to_a"), s.sem("d_a_to_v")
    vals_used = s.sem("d_vals_used")
    O = s.ps[7]

    with nc.Block() as block:
        @block.sync
        def _(sp):
            sp.dma_start(gate, T["gate_rows"].rearrange("b (h c) -> (b h) c", c=3)).then_inc(small, 16)
            sp.dma_start(own, T["c_own"]).then_inc(small, 16)
            sp.dma_start(over[0:NC_S], T["c_over"]).then_inc(small, 16)
            sp.dma_start(lower, T["c_lower"]).then_inc(small, 16)
            sp.wait_ge(turned, 4 * NB)
            for b in range(NB):
                sp.dma_start(win_keys[b], T["cache_win_k"][0, b].rearrange("(p t) g d -> p t (g d)", t=4)).then_inc(wk_in, 16)
            sp.wait_ge(vals_used, NB)
            for b in range(NB):
                sp.dma_start(win_vals[b], T["cache_win_v"][0, b].rearrange("(p t) g d -> p t (g d)", t=4)).then_inc(wv_in, 16)

        @block.gpsimd
        def _(pool):
            def gather(dst, src, b, done):
                pool.indirect_dma_start(
                    out=dst.rearrange("p t c -> p (t c)"), out_offset=None,
                    in_=src[0].rearrange("n (j t) g d -> (n j) (t g d)", t=CMP_STRIDE),
                    in_offset=bass.IndirectOffsetOnAxis(ap=s.gidx[:, b:b + 1], axis=0)).then_inc(done, 16)

            for b in range(2):
                gather(key_rows[b], T["cache_slc_k"], b, k_in[b])
            for b in range(2):
                gather(val_rows[b], T["cache_slc_v"], b, v_in[b])
            for b in range(2, NB):
                pool.wait_ge(turned, 4 * (b - 1))
                gather(key_rows[b % 2], T["cache_slc_k"], b, k_in[b % 2])
            for b in range(2, NB):
                pool.wait_ge(vals_used, b - 1)
                gather(val_rows[b % 2], T["cache_slc_v"], b, v_in[b % 2])

        @block.tensor
        def _(pe):
            to_v = [0]

            def signal(ins):
                to_v[0] += 1
                ins.then_inc(pe_to_v, 1)

            pe.wait_ge(q_ready, 1)
            for b in range(NB):
                last = pe.matmul(s.ps[6][0:NC_S, b * NH:(b + 1) * NH], s.kcT[:, 1 + b, 0:NC_S],
                                 qbd[:, b * NH:(b + 1) * NH], start=True, stop=True)
            signal(last)
            pe.wait_ge(v_to_pe, 1)
            signal(pe.transpose(s.ps[5][0:ROWS, 0:NC_S], cmp_sc[0:NC_S, :], s.ident[0:NC_S, 0:NC_S]))
            for kind in range(2):
                last = pe.matmul(s.ps[4][0:ROWS, kind * NB:(kind + 1) * NB], qbd, knew[:, kind, :],
                                 start=True, stop=True)
            signal(last)

            def turn_keys(src, chunks, first):
                for c in range(chunks):
                    for k in range(4):
                        last = pe.transpose(s.ps[(first + c) % 4][:, k * P:(k + 1) * P], src[:, 4 * c + k, :], s.ident[:, :])
                    last.then_inc(turned, 1)

            def dots(keys, n, b, slot):
                for k in range(n):
                    last = pe.matmul(s.ps[5 + slot % 2][:, k * NH:(k + 1) * NH], keys[:, k, :],
                                     qbd[:, bass.ds(b * NH, NH)], start=True, stop=True)
                last.then_inc(dotted, 1)

            pe.wait_ge(v_to_pe, 2)
            signal(pe.transpose(s.ps[6][0:NC_S, 0:ROWS], cmp_rows[:, 0:NC_S], s.ident[0:ROWS, 0:ROWS]))
            pe.wait_ge(v_to_pe, 3)
            pe.matmul(s.ps[6][0:ROWS, 128:128 + NS_S], grp_all[0:NC_S, :], over[0:NC_S, :],
                      start=True, stop=True)
            signal(pe.transpose(s.ps[6][0:NC_S, 256:256 + ROWS], cmp_rows[:, 0:NC_S], s.ident[0:ROWS, 0:ROWS]))
            pe.wait_ge(v_to_pe, 4)
            with pe.Fori(0, NB // 2) as i:
                for h in range(2):
                    b = 2 * i + h
                    pe.wait_ge(k_in[h], 16 * i + 16)
                    turn_keys(key_rows[h], 4, 0)
                    pe.wait_ge(evac_v, 2 * b + 2)
                    pe.wait_ge(evac_a, 2 * b + 2)
                    pe.wait_ge(dots_read, b + 1)
                    dots(keysT[h], 16, b, h)

            def to_rows(n):
                for k in range(n):
                    last = pe.transpose(s.ps[k // 4][0:ROWS, (k % 4) * P:(k % 4 + 1) * P], scT[:, k, :], s.ident[:, :])
                signal(last)

            def to_keys(n):
                for k in range(n):
                    last = pe.transpose(s.ps[k // 8][:, (k % 8) * ROWS:(k % 8 + 1) * ROWS],
                                        rows[:, k * P:(k + 1) * P], s.ident[0:ROWS, 0:ROWS])
                last = pe.transpose(s.ps[4][0:NB, 0:ROWS], new_d, s.ident[0:ROWS, 0:ROWS])
                signal(last)

            pe.wait_ge(dots_read, NB + 1)
            to_rows(16)
            pe.wait_ge(v_to_pe, 5)
            to_keys(16)
            pe.wait_ge(v_to_pe, 6)
            pe.wait_ge(wk_in, 16 * NB)
            for b in range(NB):
                if b >= 4:
                    pe.wait_ge(evac_a if b % 2 else evac_v, 2 * NB + (b - 4) // 2 + 1)
                turn_keys(win_keys[b], 1, b)
            pe.matmul(O[:, 0:ROWS], s.vkv[0:NB, TT, 0, :], new_dT[0:NB, 0, :], start=True, stop=False,
                      skip_group_check=True)
            for b in range(NB):
                pe.matmul(O[:, b * NH:(b + 1) * NH], s.vc[0:NC_S, 1 + b, :], cmp_pT[0:NC_S, b * NH:(b + 1) * NH],
                          start=False, stop=False, skip_group_check=True)
            with pe.Fori(0, NB // 2) as i:
                for h in range(2):
                    b = 2 * i + h
                    pe.wait_ge(v_in[h], 16 * i + 16)
                    for k in range(16):
                        last = pe.matmul(O[:, bass.ds(b * NH, NH)], val_rows[h][:, k, :],
                                         prT[:, k, bass.ds(b * NH, NH)], start=False, stop=False,
                                         skip_group_check=True)
                    last.then_inc(vals_used, 1)
            pe.wait_ge(evac_v, 2 * NB + NB // 2)
            pe.wait_ge(evac_a, 2 * NB + NB // 2)
            for b in range(NB):
                pe.wait_ge(dots_read, NB + b + 1)
                dots(win_keysT[b], 4, b, b)
            pe.wait_ge(dots_read, 2 * NB + 1)
            to_rows(4)
            pe.wait_ge(v_to_pe, 7)
            to_keys(4)
            pe.wait_ge(v_to_pe, 8)
            pe.wait_ge(wv_in, 16 * NB)
            pe.matmul(O[:, 0:ROWS], s.vkv[0:NB, TT, 1, :], new_dT[0:NB, 1, :], start=False, stop=False,
                      skip_group_check=True)
            for b in range(NB):
                for k in range(4):
                    last = pe.matmul(O[:, b * NH:(b + 1) * NH], win_vals[b][:, k, :], prT[:, k, b * NH:(b + 1) * NH],
                                     start=False, stop=(b == NB - 1 and k == 3), skip_group_check=True)
            signal(last)

        def copy_keys(eng, copy, done, odd, then):
            with eng.Fori(0, NB // 2) as i:
                for h in range(2):
                    b = 2 * i + h
                    for c in (odd, odd + 2):
                        eng.wait_ge(turned, 4 * b + c + 1)
                        copy(keysT[h][:, 4 * c:4 * c + 4, :], view(s.ps[c], 0, 4, P)).then_inc(done, 1)
                    then(b, h)

        def copy_window(eng, copy, done, odd):
            for b in range(odd, NB, 2):
                eng.wait_ge(turned, 4 * NB + b + 1)
                copy(win_keysT[b], view(s.ps[b % 4], 0, 4, P)).then_inc(done, 1)

        @block.scalar
        def _(act):
            ch = s.act_chain
            exps = [0]

            def exp_rows(weights, bias, total, new):
                exps[0] += 1
                act.wait_ge(v_to_a, exps[0])
                ch.link(act, act.activation(weights, weights, ACT.Exp, bias=bias, accum_out=total))
                if new is not None:
                    ch.link(act, act.activation(new, new, ACT.Exp, bias=bias))
                act.nop().then_inc(a_to_v, 1)

            exp_rows(cmp_rows[:, 0:NC_S], st[:, 1:2], st[:, 2:3], None)
            copy_keys(act, lambda o, i: act.activation(o, i, ACT.Copy), evac_a, 1, lambda b, h: None)
            exp_rows(rows[:, 0:2048], st[:, 5:6], st[:, 6:7], st[:, 3:4])
            copy_window(act, lambda o, i: act.activation(o, i, ACT.Copy), evac_a, 1)
            exp_rows(rows[:, 0:512], st[:, 5:6], st[:, 6:7], st[:, 4:5])

        @block.vector
        def _(v):
            ch = s.dve_chain
            from_pe, from_a = [0], [0]

            def pe_done():
                from_pe[0] += 1
                v.wait_ge(pe_to_v, from_pe[0])

            def act_done():
                from_a[0] += 1
                v.wait_ge(a_to_v, from_a[0])

            v.sem_inc(dots_read, 1)
            ch.link(v, v.memset(qbd, 0.0))
            for g in range(NG):
                half = slice(g * HD, (g + 1) * HD)
                last = v.tensor_copy(qbd[half].rearrange("p (b g j) -> p b g j", g=NG, j=HPG)[:, :, g, :],
                                     s.qT[half, :, SEQ:TOK].rearrange("p j b -> p b j"))
            v.tensor_copy(knew[:, 0, :], s.ksT[:, SEQ:TOK])
            ch.link(v, v.tensor_copy(knew[:, 1, :], s.kwT[:, SEQ:TOK]))
            v.nop().then_inc(q_ready, 1)
            v.wait_ge(small, 64)
            pe_done()
            v.tensor_copy(cmp_sc[0:NC_S, :], s.ps[6][0:NC_S, 0:ROWS]).then_inc(v_to_pe, 1)
            pe_done()
            ch.link(v, v.tensor_reduce(st[:, 1:2], s.ps[5][0:ROWS, 0:NC_S], AX.X, ALU.max, negate=True))
            ch.link(v, v.tensor_copy(cmp_rows[:, 0:NC_S], s.ps[5][0:ROWS, 0:NC_S]))
            v.nop().then_inc(v_to_a, 1)
            pe_done()
            for kind in range(2):
                ch.link(v, v.tensor_tensor(new_d, s.ps[4][0:ROWS, kind * NB:(kind + 1) * NB], own, ALU.mult))
                ch.link(v, v.tensor_reduce(st[:, 3 + kind:4 + kind], new_d, AX.X, ALU.add))
            act_done()
            ch.link(v, v.tensor_scalar(st[:, 2:3], st[:, 2:3], 1e-30, None, ALU.max))
            ch.link(v, v.reciprocal(st[:, 2:3], st[:, 2:3]))
            ch.link(v, v.tensor_scalar(cmp_rows[:, 0:NC_S], cmp_rows[:, 0:NC_S], st[:, 2:3], None, ALU.mult))
            v.nop().then_inc(v_to_pe, 1)
            pe_done()
            ch.link(v, v.tensor_copy(cmp_pT[0:NC_S, :], s.ps[6][0:NC_S, 0:ROWS]))
            ch.link(v, v.tensor_reduce(grp[0:NC_S, :], cmp_pT[0:NC_S, :].rearrange("p (x j) -> p x j", j=HPG), AX.X,
                                       ALU.add))
            ch.link(v, v.tensor_copy(grp_all[0:NC_S, :].rearrange("p (x j) -> p x j", j=HPG),
                                     bc(grp[0:NC_S, :].unsqueeze(2), (NC_S, NB * NG, HPG))))
            ch.link(v, v.tensor_scalar(cmp_rows[:, 0:NC_S], cmp_rows[:, 0:NC_S], gate[:, 0:1], None, ALU.mult))
            v.nop().then_inc(v_to_pe, 1)
            pe_done()
            v.tensor_copy(cmp_pT[0:NC_S, :], s.ps[6][0:NC_S, 256:256 + ROWS])
            ch.link(v, v.tensor_copy(imp, s.ps[6][0:ROWS, 128:128 + NS_S]))
            v.memset(imp[:, 0:1], 1e9)
            ch.link(v, v.memset(imp[:, NS_S - 2:NS_S], 1e9))
            square = lambda x: x.rearrange("p (a b) -> p a b", a=NS_S)
            mine, other = bc(imp.unsqueeze(2), (ROWS, NS_S, NS_S)), bc(imp.unsqueeze(1), (ROWS, NS_S, NS_S))
            v.tensor_tensor(square(gt), other, mine, ALU.is_gt)
            ch.link(v, v.tensor_tensor(square(eq), other, mine, ALU.is_equal))
            ch.link(v, v.tensor_tensor(eq, eq, lower, ALU.mult))
            ch.link(v, v.tensor_tensor(gt, gt, eq, ALU.add))
            ch.link(v, v.tensor_reduce(pen, square(gt), AX.X, ALU.add))
            ch.link(v, v.tensor_scalar(pen, pen, NSEL - 0.5, NEG, ALU.is_gt, ALU.mult))
            v.nop().then_inc(v_to_pe, 1)

            def take_scores(b, h):
                v.wait_ge(dotted, b + 1)
                v.tensor_copy(scT[:, :, bass.ds(b * NH, NH)], view(s.ps[5 + h], 0, 16, NH)).then_inc(dots_read, 1)

            copy_keys(v, v.tensor_copy, evac_v, 0, take_scores)

            def softmax_rows(n, kind, mask):
                pe_done()
                mask()
                new = st[:, 2 + kind:3 + kind]
                ch.link(v, v.tensor_reduce(st[:, 5:6], rows[:, 0:n], AX.X, ALU.max))
                ch.link(v, v.tensor_tensor(st[:, 5:6], st[:, 5:6], new, ALU.max))
                ch.link(v, v.tensor_scalar(st[:, 5:6], st[:, 5:6], -1.0, None, ALU.mult))
                v.nop().then_inc(v_to_a, 1)
                act_done()
                ch.link(v, v.tensor_tensor(st[:, 6:7], st[:, 6:7], new, ALU.add))
                ch.link(v, v.reciprocal(st[:, 6:7], st[:, 6:7]))
                ch.link(v, v.tensor_tensor(st[:, 6:7], st[:, 6:7], gate[:, kind:kind + 1], ALU.mult))
                v.tensor_scalar(rows[:, 0:n], rows[:, 0:n], st[:, 6:7], None, ALU.mult)
                ch.link(v, v.tensor_tensor(new, new, st[:, 6:7], ALU.mult))
                ch.link(v, v.tensor_scalar(new_d, own, new, None, ALU.mult))
                v.nop().then_inc(v_to_pe, 1)
                pe_done()
                for half in range((n // P + 7) // 8):
                    k = min(8, n // P)
                    v.tensor_copy(prT[:, 8 * half:8 * half + k, :], view(s.ps[half], 0, 8, ROWS)[:, 0:k])
                ch.link(v, v.tensor_copy(new_dT[0:NB, kind - 1, :], s.ps[4][0:NB, 0:ROWS]))
                v.nop().then_inc(v_to_pe, 1)

            def select():
                blocks = lambda x: x.rearrange("p (t m e) -> p t m e", t=16, m=32)
                ch.link(v, v.tensor_tensor(blocks(rows), blocks(s.psall[0:ROWS, 0:2048]),
                                           bc(pen[:, 0:32].unsqueeze(1).unsqueeze(3), (ROWS, 16, 32, 4)), ALU.add))

            def window():
                ch.link(v, v.tensor_copy(rows[:, 0:512], s.psall[0:ROWS, 0:512]))
                ch.link(v, v.memset(rows[:, 0:1], NEG))

            softmax_rows(2048, 1, select)
            copy_window(v, v.tensor_copy, evac_v, 0)
            for b in range(NB):
                v.wait_ge(dotted, NB + b + 1)
                v.tensor_copy(scT[:, 0:4, b * NH:(b + 1) * NH], view(s.ps[5 + b % 2], 0, 4, NH)).then_inc(dots_read, 1)
            softmax_rows(512, 2, window)
            pe_done()
            for g in range(NG):
                half = slice(g * HD, (g + 1) * HD)
                last = v.tensor_copy(s.oN[half, :, SEQ:TOK].rearrange("p j b -> p b j"),
                                     O[half, 0:ROWS].rearrange("p (b g j) -> p b g j", g=NG, j=HPG)[:, :, g, :])
            ch.link(v, last)


def stage_hgrn(nc, s, T):
    kinds = (C_HQ, C_HF, C_HG)
    w_in = T["w_in"][0].rearrange("(k p) n -> p k n", p=P)
    raw = [view(s.ring, 2048 * i + 1024, KT, P) for i in range(2)]
    w_hi, w_lo = ([s.ring_short(2048 * i + at, KT, P) for i in range(2)] for at in (0, 1024))
    q, k, b, sg = ([view(s.work, 8256 + 4128 * par + 1032 * i, TOK) for par in range(2)] for i in range(4))
    E = view(s.ring, 4096, SEQ)
    state = view(s.ring, 5120, NB, P)
    vb = view(s.ring, 6144, NB, P)
    S = view(s.ring, 7168, TT, P)
    X = [view(s.work, 21360 + 1024 * i, SEQ) for i in range(2)]
    AT = view(s.work, 23408, TT, P)
    kdT = view(s.work, 24432, TT, P)
    o_tm = view(s.work, 21360 + 1024, TT, P)
    masks = view(s.work, 25456, 256).bitcast(U8).rearrange("p (l n) -> p l n", l=8)
    st = view(s.work, 25712, 192)
    lb, om, e2, most = (st[:, 4 * i:4 * i + 4] for i in (0, 1, 2, 4))
    dec, dec_d, ssq, rstd, lnv = (st[:, 24 + 8 * i:32 + 8 * i] for i in range(5))
    od, sqd, lnd, rstd_d, part = (st[:, 64 + 8 * i:72 + 8 * i] for i in range(5))
    w_loaded = [s.sem(f"g_w{i}") for i in range(2)]
    cut, split = s.sem("g_cut"), s.sem("g_split")
    masks_in, lb_sub, lb_exp = s.sem("g_masks"), s.sem("g_lb_sub"), s.sem("g_lb_exp")
    projected, evac = s.sem("g_projected"), s.sem("g_evac")
    f_ready, g_ready = s.sem("g_f"), s.sem("g_g")
    diff, exped, x_ready = s.sem("g_diff"), s.sem("g_exped"), s.sem("g_x_ready")
    level, picked = s.sem("g_level"), s.sem("g_picked")
    kd_ready, kd_turned, kd_copied = s.sem("g_kd"), s.sem("g_kd_turned"), s.sem("g_kd_copied")
    updates, states = s.sem("g_updates"), s.sem("g_states")
    new_state, dec_out, dec_sq, dec_sum = s.sem("g_new_state"), s.sem("g_dec_out"), s.sem("g_dec_sq"), s.sem("g_dec_sum")
    rstd_ready, o_ready, o_scaled, o_turned, o_read = (s.sem(f"g_{n}") for n in ("rstd", "o", "o_scaled", "o_turned", "o_read"))
    dec_in, states_out = s.sem("g_dec_in"), s.sem("g_states_out")
    SLOTS = 9
    JOBS = 9
    job = (0, 1, 3, 5, 6, 7, 8)

    with nc.Block() as block:
        @block.sync
        def _(sp):
            sp.dma_start(kdT.bitcast(I32), T["c_levels"]).then_inc(masks_in, 16)
            for h in range(HGH):
                for i, c in enumerate(kinds):
                    j = 3 * h + i
                    wait(sp, projected, 3 * (j - 1))
                    sp.dma_start(raw[j % 2], w_in[:, :, c + h * P:c + (h + 1) * P]).then_inc(w_loaded[j % 2], 16)

        @block.gpsimd
        def _(pool):
            def load_states(h):
                wait(pool, states_out, 32 * h)
                wait(pool, dec_out, h)
                pool.dma_start(state, T["state_hgrn"][0, :, h].rearrange("b f i -> f b i")).then_inc(dec_in, 16)
                pool.dma_start(vb, T["hi_rows"][:, h * P:(h + 1) * P].partition_broadcast(P)).then_inc(dec_in, 16)

            def take_low(j):
                pool.wait_ge(cut, j + 1)
                low(pool, w_lo[j % 2], raw[j % 2], w_hi[j % 2]).then_inc(split, 1)

            load_states(0)
            take_low(0)
            take_low(1)
            for r in range(HGH + 1):
                h = r - 1
                if r < HGH:
                    take_low(3 * r + 2)
                if r >= 1:
                    pool.wait_ge(states, h + 1)
                    pool.dma_start(T["p_hg"][0, 0, h], S[:, TT - 1, :]).then_inc(states_out, 16)
                if r < HGH - 1:
                    take_low(3 * r + 3)
                if r >= 1:
                    pool.wait_ge(new_state, h + 1)
                    pool.dma_start(T["s_hg"][0, :, h].rearrange("b f i -> f b i"), state).then_inc(states_out, 16)
                if r < HGH - 1:
                    take_low(3 * r + 4)
                if 1 <= r < HGH:
                    load_states(r)
            pool.wait_ge(states_out, 32 * HGH)

        @block.tensor
        def _(pe):
            def project(r, u):
                kind, c = u // 3, u % 3
                n = SLOTS * r + u
                j = 3 * r + kind
                if c == 0:
                    pe.wait_ge(split, j + 1)
                wait(pe, evac, n - 2)
                cols = slice(c * CH, (c + 1) * CH)
                for i in range(KT):
                    last = product(pe, s.ps[c][:, 0:CH], (w_hi[j % 2][:, i, :], w_lo[j % 2][:, i, :]),
                                   (s.hT[:, i, cols], s.xT_r[:, i, cols]), i == 0, i == KT - 1)
                last.then_inc(projected, 1)

            def attend(h, u):
                p = h % 2
                if u < 8:
                    if u < 7:
                        pe.wait_ge(x_ready, 7 * h + u + 1)
                    for half in range(2):
                        wait(pe, picked, 2 * (8 * h + u - 1) + half + 1)
                        for c in range(4 * half, 4 * half + 4):
                            cols = slice(c * P, (c + 1) * P)
                            a, x = (X[u % 2], X[u % 2]) if u < 7 else (k[p], q[p])
                            last = pe.matmul(s.ps[3 + half][:, (c % 4) * P:(c % 4 + 1) * P], a[:, cols], x[:, cols],
                                             start=True, stop=True)
                        last.then_inc(level, 1)
                if u == 1:
                    pe.wait_ge(kd_ready, h + 1)
                    wait(pe, o_read, h)
                    for c in range(TT):
                        last = pe.transpose(s.ps[6 + c // 4][:, (c % 4) * P:(c % 4 + 1) * P],
                                            X[0][:, c * P:(c + 1) * P], s.ident[:, :])
                    last.then_inc(kd_turned, 1)
                if u == 2:
                    pe.wait_ge(kd_copied, h + 1)
                    for c in range(TT):
                        last = pe.matmul(s.ps[6 + c // 4][:, (c % 4) * P:(c % 4 + 1) * P], kdT[:, c, :],
                                         s.vhi[:, c, h * P:(h + 1) * P], start=True, stop=True)
                    last.then_inc(updates, 1)
                if u == 6:
                    pe.wait_ge(new_state, h + 1)
                    for n in range(NB):
                        last = pe.matmul(s.ps[5][:, n:n + 1], state[:, n, :], q[p][:, SEQ + n:SEQ + n + 1],
                                         start=True, stop=True)
                    last.then_inc(dec_out, 1)
                if u == 8:
                    pe.wait_ge(dec_sq, h + 1)
                    pe.matmul(s.ps[5][:, NB:2 * NB], s.ones[:, :], sqd, start=True, stop=True).then_inc(dec_sum, 1)
                    pe.wait_ge(states, h + 1)
                    pe.wait_ge(picked, 16 * (h + 1))
                    for c in range(TT):
                        out = s.ps[6 + c // 4][:, (c % 4) * P:(c % 4 + 1) * P]
                        last = pe.matmul(out, AT[:, c, :], s.vhi[:, c, h * P:(h + 1) * P], start=True, stop=(c == 0))
                        if c:
                            last = pe.matmul(out, s.oH[:, h, c * P:(c + 1) * P], S[:, c - 1, :], start=False, stop=True)
                    last.then_inc(o_ready, 1)

            def turn_output(h):
                pe.wait_ge(o_scaled, h + 1)
                for c in range(TT):
                    last = pe.transpose(s.ps[6 + c // 4][:, (c % 4) * P:(c % 4 + 1) * P], o_tm[:, c, :], s.ident[:, :])
                last.then_inc(o_turned, 1)

            for r in range(HGH + 1):
                for u in range(SLOTS):
                    if r < HGH:
                        project(r, u)
                    if u == 0 and r >= 2:
                        turn_output(r - 2)
                    if r >= 1:
                        attend(r - 1, u)
            turn_output(HGH - 1)

        @block.scalar
        def _(act):
            ch = s.act_chain
            func = (ACT.Copy, ACT.Sigmoid, ACT.Silu)

            def halves(u):
                m = 64 >> u
                return E[:, 0:SEQ].rearrange("p (b h m) -> p b h m", h=2, m=m)

            def evacuate(r, u):
                kind, c = u // 3, u % 3
                dst = (q, b, sg)[kind][r % 2]
                act.wait_ge(projected, SLOTS * r + u + 1)
                act.activation(dst[:, c * CH:(c + 1) * CH], s.ps[c][:, 0:CH], func[kind]).then_inc(evac, 1)

            def attend(h, u):
                p = h % 2
                if u < 7:
                    act.wait_ge(diff, JOBS * h + job[u] + 1)
                    e = halves(u)
                    act.activation(e[:, :, 0, :], e[:, :, 0, :], ACT.Exp, scale=-1.0)
                    act.activation(e[:, :, 1, :], e[:, :, 1, :], ACT.Exp).then_inc(exped, 1)
                if u == 1:
                    act.wait_ge(diff, JOBS * h + 3)
                    act.activation(E[:, 0:SEQ], E[:, 0:SEQ], ACT.Exp, scale=-1.0).then_inc(exped, 1)
                if u == 2:
                    act.wait_ge(kd_turned, h + 1)
                    act.activation(kdT.rearrange("p c n -> p (c n)"), s.psall[:, 6 * 512:8 * 512],
                                   ACT.Copy).then_inc(kd_copied, 1)
                    act.wait_ge(diff, JOBS * h + 5)
                    act.activation(dec_d, b[p][:, SEQ:TOK], ACT.Exp)
                    act.activation(E, b[p][:, 0:SEQ], ACT.Exp).then_inc(exped, 1)
                if u == 8:
                    act.wait_ge(dec_sum, h + 1)
                    ch.link(act, act.activation(lnd, s.ps[5][:, NB:2 * NB], ACT.Ln, bias=s.eps[:, 0:1], scale=1.0 / P))
                    act.activation(rstd_d, lnd, ACT.Exp, scale=-0.5).then_inc(rstd_ready, 1)
                    act.wait_ge(o_ready, h + 1)
                    for c in range(TT):
                        last = act.activation(kdT[:, c, :], s.ps[6 + c // 4][:, (c % 4) * P:(c % 4 + 1) * P], ACT.Square,
                                              accum_out=ssq[:, c:c + 1])
                    ch.link(act, last)
                    ch.link(act, act.activation(lnv, ssq, ACT.Ln, bias=s.eps[:, 0:1], scale=1.0 / P))
                    act.activation(rstd, lnv, ACT.Exp, scale=-0.5).then_inc(rstd_ready, 1)

            act.wait_ge(lb_sub, 1)
            act.activation(st[:, 8:16], st[:, 8:16], ACT.Exp).then_inc(lb_exp, 1)
            for r in range(HGH + 1):
                for u in range(SLOTS):
                    if r >= 1:
                        attend(r - 1, u)
                    if r < HGH:
                        evacuate(r, u)
                        if u == 6:
                            act.wait_ge(f_ready, r + 1)
                            act.activation(b[r % 2], b[r % 2], ACT.Ln).then_inc(g_ready, 1)

        @block.vector
        def _(v):
            ch = s.dve_chain
            rows = s.vec[:, 64:72].rearrange("p (a r) -> p a r", a=2)
            pair = st[:, 8:16].rearrange("p (a r) -> p a r", a=2)
            ch.link(v, v.tensor_tensor(most, rows[:, 0], rows[:, 1], ALU.max))
            v.tensor_tensor(pair, rows, bc(most.unsqueeze(1), (P, 2, 4)), ALU.subtract).then_inc(lb_sub, 1)
            v.memset(AT, 0.0)
            v.wait_ge(lb_exp, 1)
            ch.link(v, v.tensor_tensor(most, pair[:, 0], pair[:, 1], ALU.add))
            ch.link(v, v.reciprocal(most, most))
            ch.link(v, v.tensor_tensor(lb, pair[:, 0], most, ALU.mult))
            ch.link(v, v.tensor_scalar(om, lb, -1.0, 1.0, ALU.mult, ALU.add))
            v.wait_ge(masks_in, 16)
            ch.link(v, v.tensor_copy(masks, kdT.bitcast(I32)))

            def cut_weights(j):
                v.wait_ge(w_loaded[j % 2], 16 * (j // 2 + 1))
                wait(v, projected, 3 * (j - 1))
                high(v, w_hi[j % 2], raw[j % 2]).then_inc(cut, 1)

            cut_weights(0)
            cut_weights(1)

            def forget(r, u):
                p = r % 2
                j = 3 * r + u // 3 + 1
                if u % 3 == 2 and 2 <= j < 3 * HGH:
                    cut_weights(j)
                if u == 6:
                    v.wait_ge(evac, SLOTS * r + 6)
                    ch.link(v, v.tensor_scalar(b[p], b[p], om[:, r:r + 1], lb[:, r:r + 1], ALU.mult, ALU.add))
                    v.tensor_scalar(k[p], b[p], -1.0, 1.0, ALU.mult, ALU.add).then_inc(f_ready, 1)
                if u == 7:
                    v.wait_ge(g_ready, r + 1)
                    for c in range(TT):
                        cols = b[p][:, c * P:(c + 1) * P]
                        last = v.tensor_tensor_scan(cols, s.ones[:, :], cols, 0.0, ALU.mult, ALU.add)
                    ch.link(v, last)

            def pick(h, u):
                for half in range(2):
                    v.wait_ge(level, 2 * (8 * h + u) + half + 1)
                    v.copy_predicated(AT[:, 4 * half:4 * half + 4, :], bc(masks[:, u, :].unsqueeze(1), (P, 4, P)),
                                      view(s.ps[3 + half], 0, 4, P)).then_inc(picked, 1)

            def attend(h, u):
                p = h % 2
                chunks = lambda x: x[:, 0:SEQ].rearrange("p (c n) -> p c n", n=P)
                if u < 7:
                    m = 64 >> u
                    halves = lambda x: x[:, 0:SEQ].rearrange("p (b h m) -> p b h m", h=2, m=m)
                    blocks = lambda x: x[:, 0:SEQ].rearrange("p (b m) -> p b m", m=2 * m)
                    v.tensor_tensor(blocks(E), blocks(b[p]), bc(blocks(b[p])[:, :, m - 1:m], (P, 512 // m, 2 * m)),
                                    ALU.subtract).then_inc(diff, 1)
                if 1 <= u:
                    if h or u:
                        pick(h, u - 1)
                if u < 7:
                    if u == 2:
                        v.wait_ge(kd_turned, h + 1)
                    if u == 1:
                        wait(v, o_turned, h)
                    if u >= 2:
                        v.wait_ge(level, 2 * (8 * h + u - 2) + 2)
                    v.wait_ge(exped, JOBS * h + job[u] + 1)
                    v.tensor_tensor(halves(X[u % 2])[:, :, 0], halves(k[p])[:, :, 0], halves(E)[:, :, 0], ALU.mult)
                    ch.link(v, v.tensor_tensor(halves(X[u % 2])[:, :, 1], halves(q[p])[:, :, 1], halves(E)[:, :, 1],
                                               ALU.mult))
                    v.nop().then_inc(x_ready, 1)
                if u == 0 and h >= 1:
                    finish(h - 1)
                if u == 1:
                    v.tensor_tensor(chunks(E), chunks(b[p]), bc(chunks(b[p])[:, :, P - 1:P], (P, TT, P)),
                                    ALU.subtract).then_inc(diff, 1)
                    v.wait_ge(exped, JOBS * h + 3)
                    v.wait_ge(level, 2 * 8 * h + 2)
                    ch.link(v, v.tensor_tensor(X[0], k[p][:, 0:SEQ], E[:, 0:SEQ], ALU.mult))
                    v.nop().then_inc(kd_ready, 1)
                if u == 2:
                    v.nop().then_inc(diff, 1)
                    v.wait_ge(exped, JOBS * h + 5)
                    v.tensor_copy(dec, chunks(E)[:, :, P - 1])
                    ch.link(v, v.tensor_tensor(s.oH[:, h, 0:SEQ], q[p][:, 0:SEQ], E[:, 0:SEQ], ALU.mult))
                if u == 3:
                    v.wait_ge(updates, h + 1)
                    wait(v, states_out, 32 * h)
                    src = view(s.psall, 6 * 512, TT, P)
                    ch.link(v, v.tensor_copy(S[:, 0, :], src[:, 0, :]))
                    for c in range(1, TT):
                        ch.link(v, v.scalar_tensor_tensor(out=S[:, c, :], in0=S[:, c - 1, :], scalar=dec[:, c:c + 1],
                                                          in1=src[:, c, :], op0=ALU.mult, op1=ALU.add))
                    v.nop().then_inc(states, 1)
                if u == 5:
                    v.wait_ge(dec_in, 32 * (h + 1))
                    v.tensor_tensor(vb, vb, bc(k[p][:, SEQ:TOK].unsqueeze(2), (P, NB, P)), ALU.mult)
                    ch.link(v, v.tensor_tensor(state, state, bc(dec_d.unsqueeze(2), (P, NB, P)), ALU.mult))
                    v.tensor_tensor(state, state, vb, ALU.add).then_inc(new_state, 1)
                if u == 7:
                    v.wait_ge(dec_out, h + 1)
                    ch.link(v, v.tensor_copy(od, s.ps[5][:, 0:NB]))
                    v.tensor_tensor(sqd, od, od, ALU.mult).then_inc(dec_sq, 1)
                if u == 8:
                    v.wait_ge(rstd_ready, 2 * h + 1)
                    ch.link(v, v.scalar_tensor_tensor(out=part, in0=od, scalar=s.vec[:, 72:73], in1=rstd_d,
                                                      op0=ALU.mult, op1=ALU.mult))
                    v.tensor_tensor(s.oH[:, h, SEQ:TOK], part, sg[p][:, SEQ:TOK], ALU.mult)
                    v.wait_ge(rstd_ready, 2 * h + 2)
                    v.tensor_tensor(o_tm, view(s.psall, 6 * 512, TT, P), bc(rstd.unsqueeze(2), (P, TT, P)),
                                    ALU.mult).then_inc(o_scaled, 1)

            def finish(h):
                v.wait_ge(o_turned, h + 1)
                v.scalar_tensor_tensor(out=s.oH[:, h, 0:SEQ], in0=s.psall[:, 6 * 512:8 * 512], scalar=s.vec[:, 72:73],
                                       in1=sg[h % 2][:, 0:SEQ], op0=ALU.mult, op1=ALU.mult).then_inc(o_read, 1)

            for r in range(HGH + 1):
                for u in range(SLOTS):
                    if r >= 1:
                        attend(r - 1, u)
                    if r < HGH:
                        forget(r, u)
            finish(HGH - 1)
            v.wait_ge(o_read, HGH)


def stage_mix(nc, s, T):
    w_in = T["w_in"][0].rearrange("(k p) n -> p k n", p=P)
    nsa = T["w_br_nsa"][0].rearrange("(g j d) n -> g d j n", g=NG, d=HD)
    hg = T["w_br_hg"][0].rearrange("(h p) n -> p h n", p=P)
    ada = T["ada_w"].rearrange("(k p) n -> p k n", p=P)
    base = ((s.ring, 0), (s.work, 16512))
    raw = [view(t, at + 2048, 2, KT, P) for t, at in base]
    w_hi, w_lo = ([short(at + o, 2, KT, P) for short, at in ((s.ring_short, 0), (s.work_short, 16512))]
                  for o in (0, 2048))
    w_br = [view(t, at + 4096, 2, 4, P) for t, at in base]
    panel = [view(s.ring, 5120 + 1024 * i, KT, P) for i in range(2)]
    sig = [view(s.work, 21632 + 1032 * i, TOK) for i in range(2)]
    part = view(s.work, 23696, TOK)
    mix = view(s.work, 8256, KT * TOK)
    loaded = [s.sem(f"x_loaded{i}") for i in range(2)]
    panel_in = [s.sem(f"x_panel_in{i}") for i in range(2)]
    panel_used, ada_done, cut, split = s.sem("x_panel_used"), s.sem("x_ada_done"), s.sem("x_cut"), s.sem("x_split")
    free_a, free_v, product_done = s.sem("x_free_a"), s.sem("x_free_v"), s.sem("x_product")
    LATE = G1

    with nc.Block() as block:
        @block.sync
        def _(sp):
            def load(n, h):
                col = n * P
                for dst, src in ((raw[h][:, 0], w_in[:, :, bass.ds(C_GA + col, P)]),
                                 (raw[h][:, 1], w_in[:, :, bass.ds(C_GB + col, P)]),
                                 (w_br[h][0:HD, 0], nsa[0, :, :, bass.ds(col, P)]),
                                 (w_br[h][HD:P, 0], nsa[1, :, :, bass.ds(col, P)]),
                                 (w_br[h][:, 1], hg[:, :, bass.ds(col, P)])):
                    sp.dma_start(dst, src).then_inc(loaded[h], 16)

            def load_panels(n, start=False):
                for q in range(4):
                    if not (start and q < 2):
                        sp.wait_ge(panel_used, 4 * n + q - 1)
                    sp.dma_start(panel[q % 2], ada[:, :, bass.ds((LATE + 4 * n + q) * P, P)]).then_inc(panel_in[q % 2], 16)

            load(0, 0)
            load(1, 1)
            load_panels(0, True)
            with sp.Fori(0, KT // 2 - 1) as i:
                for h in range(2):
                    n = 2 * i + h
                    sp.wait_ge(product_done, 12 * n + 12)
                    load(n + 2, h)
                    load_panels(n + 1)
            load_panels(KT - 1)

        @block.gpsimd
        def _(pool):
            with pool.Fori(0, KT // 2) as i:
                for h in range(2):
                    pool.wait_ge(cut, 2 * i + h + 1)
                    low(pool, w_lo[h], raw[h], w_hi[h]).then_inc(split, 1)

        @block.tensor
        def _(pe):
            def modulate(n, q):
                pe.wait_ge(panel_in[q % 2], 32 * n + 16 * (q // 2) + 16)
                for k in range(KT):
                    last = pe.matmul(s.ps[6][:, bass.ds((4 * n + q) * 9, 9)], panel[q % 2][:, k, :], s.cT[:, k, :],
                                     start=(k == 0), stop=(k == KT - 1))
                last.then_inc(panel_used, 1)

            with pe.Fori(0, KT // 2) as i:
                for h in range(2):
                    n = 2 * i + h
                    pe.wait_ge(split, n + 1)
                    for kind in range(4):
                        branch = kind // 2
                        for c in range(3):
                            cols = slice(c * CH, (c + 1) * CH)
                            out = s.ps[3 * (kind % 2) + c][:, 0:CH]
                            pe.wait_ge(free_v if kind % 2 else free_a, 6 * n + 3 * branch + c + 1)
                            if kind % 2 == 0:
                                for k in range(KT):
                                    last = product(pe, out, (w_hi[h][:, branch, k, :], w_lo[h][:, branch, k, :]),
                                                   (s.hT[:, k, cols], s.xT_r[:, k, cols]), k == 0, k == KT - 1)
                            else:
                                src = s.oH if branch else s.oN
                                for k in range(4):
                                    last = pe.matmul(out, w_br[h][:, branch, k, :], src[:, k, cols], start=(k == 0), stop=(k == 3))
                            last.then_inc(product_done, 1)
                        modulate(n, kind)
            pe.wait_ge(panel_used, 4 * KT)
            pe.sem_inc(ada_done, 1)

        @block.scalar
        def _(act):
            act.sem_inc(free_a, 3)
            with act.Fori(0, KT // 2) as i:
                for h in range(2):
                    n = 2 * i + h
                    for branch in range(2):
                        act.wait_ge(free_v, 6 * n + (3 if branch else 1))
                        for c in range(3):
                            act.wait_ge(product_done, 12 * n + 6 * branch + c + 1)
                            act.activation(sig[branch][:, c * CH:(c + 1) * CH], s.ps[c][:, 0:CH],
                                           ACT.Sigmoid).then_inc(free_a, 1)

        @block.vector
        def _(v):
            ch = s.dve_chain
            v.sem_inc(free_v, 3)

            def cut_weights(h, times):
                v.wait_ge(loaded[h], 80 * times)
                high(v, w_hi[h], raw[h]).then_inc(cut, 1)

            def body(n, h, i, more):
                for branch in range(2):
                    for c in range(3):
                        v.wait_ge(free_a, 6 * n + 3 * branch + c + 4)
                        v.wait_ge(product_done, 12 * n + 6 * branch + c + 4)
                        cols = slice(c * CH, (c + 1) * CH)
                        at = mix[:, bass.ds(n * TOK + c * CH, CH)]
                        ch.link(v, v.tensor_tensor(part[:, cols] if branch else at, sig[branch][:, cols],
                                                   s.ps[3 + c][:, 0:CH], ALU.mult))
                        v.nop().then_inc(free_v, 1)
                        if branch:
                            v.tensor_tensor(at, at, part[:, cols], ALU.add)
                if more:
                    cut_weights(h, i + 2)

            cut_weights(0, 1)
            cut_weights(1, 1)
            with v.Fori(0, KT // 2 - 1) as i:
                ch.enter(i, 12)
                for h in range(2):
                    body(2 * i + h, h, i, True)
            ch.leave(KT // 2 - 1)
            for h in range(2):
                body(KT - 2 + h, h, 0, False)
            v.wait_ge(ada_done, 1)
            finish_modulation(s, v, LATE, 6 * KT, s.ps[6])
            scale_gain(s, v, s.A2, SC2, 56)


def stage_out_projection(nc, s, T):
    w = T["w_out"].rearrange("(k p) n -> p k n", p=P)
    mix, mix_hi, mix_lo = view(s.work, 8256, KT, TOK), s.work_short(16512, KT, TOK), s.work_short(8256, KT, TOK)
    raw = [view(s.ring, 2048 * i + 1024, KT, P) for i in range(2)]
    w_hi, w_lo = ([s.ring_short(2048 * i + at, KT, P) for i in range(2)] for at in (0, 1024))
    part = view(s.ring, 4096, NB)
    loaded = [s.sem(f"w_loaded{i}") for i in range(2)]
    x_in, cut, split = s.sem("w_x_in"), s.sem("w_cut"), s.sem("w_split")
    mix_ready, mix_cut, made, added = s.sem("w_mix_ready"), s.sem("w_mix_cut"), s.sem("w_made"), s.sem("w_added")

    with nc.Block() as block:
        @block.sync
        def _(sp):
            for n in range(2):
                sp.dma_start(raw[n], w[:, :, n * P:(n + 1) * P]).then_inc(loaded[n], 16)
            sp.dma_start(s.xT[:, :, :], T["x_spill"]).then_inc(x_in, 16)
            for n in range(2, KT):
                sp.wait_ge(made, 3 * (n - 1))
                sp.dma_start(raw[n % 2], w[:, :, n * P:(n + 1) * P]).then_inc(loaded[n % 2], 16)

        @block.gpsimd
        def _(pool):
            for n in range(KT):
                if n == 2:
                    for k in range(2, KT, 3):
                        pool.wait_ge(mix_cut, k + 1)
                        low(pool, mix_lo[:, k, :], mix[:, k, :], mix_hi[:, k, :]).then_inc(mix_ready, 1)
                pool.wait_ge(cut, n + 1)
                low(pool, w_lo[n % 2], raw[n % 2], w_hi[n % 2]).then_inc(split, 1)

        @block.tensor
        def _(pe):
            for n in range(KT):
                pe.wait_ge(split, n + 1)
                if n >= 2:
                    pe.wait_ge(added, 3 * (n - 1))
                if n == 0:
                    pe.wait_ge(mix_ready, KT)
                for c in range(3):
                    cols = slice(c * CH, (c + 1) * CH)
                    for k in range(KT):
                        last = product(pe, s.ps[3 * (n % 2) + c][:, 0:CH], (w_hi[n % 2][:, k, :], w_lo[n % 2][:, k, :]),
                                       (mix_hi[:, k, cols], mix_lo[:, k, cols]), k == 0, k == KT - 1)
                    last.then_inc(made, 1)

        @block.scalar
        def _(act):
            for k in range(KT):
                act.activation(mix_hi[:, k, :], mix[:, k, :], ACT.Copy).then_inc(mix_cut, 1)

        @block.vector
        def _(v):
            ch = s.dve_chain

            def cut_weights(n):
                v.wait_ge(loaded[n % 2], 16 * (n // 2 + 1))
                high(v, w_hi[n % 2], raw[n % 2]).then_inc(cut, 1)

            cut_weights(0)
            cut_weights(1)
            for k in range(KT):
                if k % 3 != 2:
                    v.wait_ge(mix_cut, k + 1)
                    low(v, mix_lo[:, k, :], mix[:, k, :], mix_hi[:, k, :]).then_inc(mix_ready, 1)
            v.wait_ge(x_in, 16)
            for n in range(KT):
                for c in range(3):
                    ps = s.ps[3 * (n % 2) + c]
                    v.wait_ge(made, 3 * n + c + 1)
                    m = CH if c < 2 else CH - NB
                    at = s.xT[:, n, c * CH:c * CH + m]
                    last = v.scalar_tensor_tensor(out=at, in0=ps[:, 0:m], scalar=s.mod[:, G1 + n, 0:1], in1=at,
                                                  op0=ALU.mult, op1=ALU.add)
                    if c < 2:
                        last.then_inc(added, 1)
                ch.link(v, v.tensor_tensor(part, ps[:, m:CH], s.mod[:, G1 + n, 1:NB + 1], ALU.mult))
                ch.link(v, v.tensor_tensor(s.xT[:, n, SEQ:TOK], s.xT[:, n, SEQ:TOK], part, ALU.add))
                v.nop().then_inc(added, 1)
                if n + 2 < KT:
                    cut_weights(n + 2)


def stage_ffn(nc, s, T):
    GR = FT // 2
    w_up = T["w_up"].rearrange("(k p) n -> p k n", p=P)
    w_dn = T["w_down"].rearrange("(g e p) n -> p (g e) n", e=2, p=P)
    hi, lo = s.hT, s.work_short(0, KT, TOK)
    a = [view(s.work, 12384 + 2064 * i, 2, TOK) for i in range(2)]
    aH, aL = ([s.work_short(at + 2064 * i, 2, TOK) for i in range(2)] for at in (8256, 12384))
    u = view(s.work, 16512, SEQ + 2)
    y = view(s.work, 17540, TOK)
    tails = view(s.work, 18572, FT * (NB + 2))
    bufT = view(s.work, 18792, FT * 2 * NB)
    dec = view(s.work, 19144, KT, NB)
    rows = view(s.work, 19208, DFF)
    raw_d = view(s.work, 19208 + 2048, 2, D)
    wd = [s.work_short(19208 + 2048 * i, 2, D) for i in range(2)]
    raw_u = [view(s.ring, 4096 * f + 2048, 2, KT, P) for f in range(2)]
    wu = [[s.ring_short(4096 * f + 2048 * i, 2, KT, P) for i in range(2)] for f in range(2)]
    up_in = [s.sem(f"f_up_in{i}") for i in range(2)]
    dn_in, up_cut, dn_cut = s.sem("f_dn_in"), s.sem("f_up_cut"), s.sem("f_dn_cut")
    up_split, dn_split, a_ready = s.sem("f_up_split"), s.sem("f_dn_split"), s.sem("f_a_ready")
    u_made, v_made, d_made, added = s.sem("f_u_made"), s.sem("f_v_made"), s.sem("f_d_made"), s.sem("f_added")
    buf_in, turned, copied, out = s.sem("f_buf_in"), s.sem("f_turned"), s.sem("f_copied"), s.sem("f_out")
    u_read, v_read, silu_done, conv_a, conv_v = (s.sem(f"f_{n}") for n in ("u_read", "v_read", "silu", "conv_a", "conv_v"))
    conv = s.conv[:, :, :].rearrange("p j f -> p (j f)")
    x = s.xT

    def groups(eng, body, per=None, ch=None):
        body(0, 0, True, False)
        with eng.Fori(0, GR // 2) as i:
            if ch:
                ch.enter(i, per)
            body(2 * i + 1, 1, True, True)
            body(2 * i + 2, 0, True, True)
        if ch:
            ch.leave(GR // 2)
        body(GR, 1, False, True)

    with nc.Block() as block:
        @block.sync
        def _(sp):
            def load_up(f, h):
                for part in range(2):
                    sp.dma_start(raw_u[h][:, part], w_up[:, :, bass.ds(part * DFF + f * P, P)]).then_inc(up_in[h], 16)

            def load_down(g):
                sp.wait_ge(d_made, 24 * g + 1)
                sp.dma_start(raw_d, w_dn[:, bass.ds(2 * g, 2), :]).then_inc(dn_in, 16)

            load_up(0, 0)
            load_up(1, 1)
            sp.wait_ge(copied, 1)
            with sp.Fori(0, GR - 1) as g:
                for h in range(2):
                    f = 2 * g + 2 + h
                    sp.wait_ge(v_made, 3 * (f - 1))
                    load_up(f, h)
                load_down(g)
            load_down(GR - 1)
            sp.wait_ge(copied, 1 + (FT + 3) // 4)
            sp.dma_start(T["p_cf"][0, 0], rows[0:2, :]).then_inc(out, 16)
            sp.dma_start(T["s_cf"][0, :, 1], rows[2:2 + NB, :]).then_inc(out, 16)
            sp.wait_ge(out, 32)

        @block.gpsimd
        def _(pool):
            pool.dma_start(rows[0:2 * NB, :], T["state_ffn_conv"][0].rearrange("b j f -> (b j) f")).then_inc(buf_in, 16)
            pool.dma_start(T["s_cf"][0, :, 0], T["state_ffn_conv"][0, :, 1]).then_inc(buf_in, 16)

            def low_up(f, h):
                pool.wait_ge(up_cut, f + 1)
                low(pool, wu[h][1], raw_u[h], wu[h][0]).then_inc(up_split, 1)

            def body(g, par, up, down):
                if up:
                    low_up(2 * g + 1, 1)
                if down:
                    pool.wait_ge(dn_cut, g)
                    low(pool, wd[1], raw_d, wd[0]).then_inc(dn_split, 1)
                if up:
                    if up != "last":
                        low_up(2 * g + 2, 0)

            low_up(0, 0)
            body(0, 0, True, False)
            with pool.Fori(0, GR // 2 - 1) as i:
                body(2 * i + 1, 1, True, True)
                body(2 * i + 2, 0, True, True)
            body(GR - 2, 1, True, True)
            body(GR - 1, 0, "last", True)
            body(GR, 1, False, True)
            pool.wait_ge(buf_in, 32)

        @block.tensor
        def _(pe):
            pe.sem_inc(d_made, 1)
            pe.wait_ge(buf_in, 32)
            for f in range(FT):
                last = pe.transpose(s.ps[6][:, f * 16:(f + 1) * 16], rows[0:2 * NB, f * P:(f + 1) * P],
                                    s.ident[0:2 * NB, 0:2 * NB])
            last.then_inc(turned, 1)
            pe.wait_ge(copied, 1)

            def body(g, par, up, down):
                for h in range(2 if up else 0):
                    f = 2 * g + h
                    pe.wait_ge(up_split, f + 1)
                    for part, (read, made) in enumerate(((u_read, u_made), (v_read, v_made))):
                        pe.wait_ge(read, 3 * f + 1)
                        for c in range(3):
                            cols = slice(c * CH, (c + 1) * CH)
                            for k in range(KT):
                                last = product(pe, s.ps[3 * part + c][:, 0:CH], [w[:, part, k, :] for w in wu[h]],
                                               (hi[:, k, cols], lo[:, k, cols]), k == 0, k == KT - 1)
                            last.then_inc(made, 1)
                if down:
                    pe.wait_ge(dn_split, g)
                    pe.wait_ge(a_ready, 2 * g)
                    for n in range(KT):
                        for c in range(3):
                            cols = slice(c * CH, (c + 1) * CH)
                            pe.wait_ge(added, 24 * (g - 1) + 3 * n + c + 1)
                            for e in range(2):
                                last = product(pe, s.ps[6 + (3 * n + c) % 2][:, 0:CH], [w[:, e, n * P:(n + 1) * P] for w in wd],
                                               (aH[1 - par][:, e, cols], aL[1 - par][:, e, cols]), e == 0, e == 1)
                            last.then_inc(d_made, 1)

            groups(pe, body)
            pe.wait_ge(added, 24 * GR + 2)
            for f in range(FT):
                if f % 4 == 0 and f >= 8:
                    pe.wait_ge(copied, f // 4)
                last = pe.transpose(s.ps[6 + f // 4 % 2][0:NB + 2, (f % 4) * P:(f % 4 + 1) * P],
                                    tails[:, f * 10:(f + 1) * 10], s.ident[:, :])
                if f % 4 == 3 or f == FT - 1:
                    last.then_inc(turned, 1)

        @block.scalar
        def _(act):
            ch = s.act_chain
            act.wait_ge(copied, 1)
            act.sem_inc(u_read, 1)

            def body(g, par, up, down):
                for h in range(2 if up else 0):
                    f = 2 * g + h
                    act.wait_ge(conv_v, f + 1)
                    for c in range(3):
                        m = CH if c < 2 else CH - NB
                        act.wait_ge(u_made, 3 * f + c + 1)
                        last = act.activation(u[:, 2 + c * CH:2 + c * CH + m], s.ps[c][:, 0:m], ACT.Copy)
                        if c < 2:
                            last.then_inc(u_read, 1)
                    ch.link(act, last)
                    act.activation(tails[:, bass.ds(10 * f, 2)], s.ps[2][:, m - 2:m], ACT.Copy)
                    ch.link(act, act.activation(tails[:, bass.ds(10 * f + 2, NB)], s.ps[2][:, m:CH], ACT.Copy))
                    act.nop().then_inc(u_read, 1)
                    tap, bias = conv[:, bass.ds(2 * FT + f, 1)], conv[:, bass.ds(3 * FT + f, 1)]
                    act.wait_ge(v_read, 3 * f + 1)
                    act.activation(y[:, 0:SEQ], u[:, 2:SEQ + 2], ACT.Identity, scale=tap, bias=bias)
                    act.activation(y[:, SEQ:TOK], tails[:, bass.ds(10 * f + 2, NB)], ACT.Identity, scale=tap,
                                   bias=bias).then_inc(conv_a, 1)
                    act.wait_ge(conv_v, f + 2)
                    act.activation(y, y, ACT.Silu).then_inc(silu_done, 1)

            groups(act, body, 8, ch)

        @block.vector
        def _(v):
            ch = s.dve_chain
            ch.link(v, v.memset(u[:, 0:2], 0.0))
            v.memset(dec, 0.0)
            v.wait_ge(turned, 1)
            v.tensor_copy(bufT.rearrange("p (f j b) -> p f j b", j=2, b=NB),
                          view(s.ps[6], 0, FT, NB, 2).rearrange("p f b j -> p f j b")).then_inc(copied, 1)
            v.wait_ge(copied, 1)
            v.sem_inc(v_read, 1)
            v.sem_inc(conv_v, 1)
            v.sem_inc(added, 2)

            def cut_up(f, h, times):
                v.wait_ge(up_in[h], 32 * times)
                if not (isinstance(f, int) and f < 2):
                    v.wait_ge(v_made, 3 * (f - 1))
                high(v, wu[h][0], raw_u[h]).then_inc(up_cut, 1)

            def convolve(f):
                v.wait_ge(conv_a, f + 1)
                taps = [conv[:, bass.ds(j * FT + f, 1)] for j in range(2)]
                ch.link(v, v.scalar_tensor_tensor(out=y[:, 0:SEQ], in0=u[:, 1:SEQ + 1], scalar=taps[1],
                                                  in1=y[:, 0:SEQ], op0=ALU.mult, op1=ALU.add))
                v.scalar_tensor_tensor(out=y[:, 0:SEQ], in0=u[:, 0:SEQ], scalar=taps[0], in1=y[:, 0:SEQ],
                                       op0=ALU.mult, op1=ALU.add)
                yd = y[:, SEQ:TOK]
                ch.link(v, v.scalar_tensor_tensor(out=yd, in0=bufT[:, bass.ds(16 * f + NB, NB)], scalar=taps[1],
                                                  in1=yd, op0=ALU.mult, op1=ALU.add))
                v.scalar_tensor_tensor(out=yd, in0=bufT[:, bass.ds(16 * f, NB)], scalar=taps[0], in1=yd,
                                       op0=ALU.mult, op1=ALU.add).then_inc(conv_v, 1)

            def hidden(f, h, par):
                whole, hi, lo = (t[par][:, h, :] for t in (a, aH, aL))
                v.wait_ge(silu_done, f + 1)
                for c in range(3):
                    cols = slice(c * CH, (c + 1) * CH)
                    v.wait_ge(v_made, 3 * f + c + 1)
                    last = v.tensor_tensor(whole[:, cols], y[:, cols], s.ps[3 + c][:, 0:CH], ALU.mult)
                    if c < 2:
                        last.then_inc(v_read, 1)
                ch.link(v, last)
                v.nop().then_inc(v_read, 1)
                ch.link(v, high(v, hi, whole))
                low(v, lo, whole, hi).then_inc(a_ready, 1)

            def body(g, par, up, down, more=True):
                if up:
                    cut_up(2 * g + 1, 1, g + 1)
                if down:
                    v.wait_ge(dn_in, 16 * g)
                    v.wait_ge(d_made, 24 * (g - 1) + 1)
                    high(v, wd[0], raw_d).then_inc(dn_cut, 1)
                if up:
                    convolve(2 * g)
                    hidden(2 * g, 0, par)
                    if more:
                        cut_up(2 * g + 2, 0, g + 2)
                    convolve(2 * g + 1)
                if down:
                    for n in range(KT):
                        for c in range(3):
                            m = CH if c < 2 else CH - NB
                            ps = s.ps[6 + (3 * n + c) % 2]
                            v.wait_ge(d_made, 24 * (g - 1) + 3 * n + c + 2)
                            if c == 2:
                                ch.link(v, v.tensor_tensor(dec[:, n, :], dec[:, n, :], ps[:, m:CH], ALU.add))
                            at = x[:, n, c * CH:c * CH + m]
                            v.scalar_tensor_tensor(out=at, in0=ps[:, 0:m], scalar=s.mod[:, G2 + n, 0:1], in1=at,
                                                   op0=ALU.mult, op1=ALU.add).then_inc(added, 1)
                if up:
                    hidden(2 * g + 1, 1, par)

            cut_up(0, 0, 1)
            body(0, 0, True, False)
            with v.Fori(0, GR // 2 - 1) as i:
                ch.enter(i, 2 * (8 + KT))
                body(2 * i + 1, 1, True, True)
                body(2 * i + 2, 0, True, True)
            ch.leave(GR // 2 - 1)
            body(GR - 2, 1, True, True)
            body(GR - 1, 0, True, True, more=False)
            body(GR, 1, False, True)
            v.wait_ge(added, 24 * GR + 2)
            ch.link(v, v.tensor_tensor(dec, dec, s.mod[:, G2:G2 + KT, 1:NB + 1], ALU.mult))
            ch.link(v, v.tensor_tensor(x[:, :, SEQ:TOK], x[:, :, SEQ:TOK], dec, ALU.add))
            for g in range((FT + 3) // 4):
                n = min(4, FT - 4 * g) * P
                v.wait_ge(turned, g + 2)
                v.tensor_copy(rows[0:NB + 2, 512 * g:512 * g + n], s.ps[6 + g % 2][0:NB + 2, 0:n]).then_inc(copied, 1)


def stage_output(nc, s, T):
    y = [view(s.ring, 1024 * i, D) for i in range(2)]
    turned, done = s.sem("o_turned"), [s.sem("o_done_v"), s.sem("o_done_a")]
    sent = [s.sem(f"o_sent{i}") for i in range(2)]

    with nc.Block() as block:
        @block.tensor
        def _(pe):
            for t in range(TT + 1):
                n = rows_of(t)
                for half in range(2):
                    g = 2 * t + half
                    wait(pe, done[half], t - 3)
                    for j in range(4):
                        last = pe.transpose(s.ps[g % 8][0:n, j * P:(j + 1) * P],
                                            s.xT[:, 4 * half + j, t * P:t * P + n], s.ident[:, :])
                    last.then_inc(turned, 1)

        def copy_half(eng, copy, half):
            for t in range(TT + 1):
                n = rows_of(t)
                eng.wait_ge(turned, 2 * t + half + 1)
                wait(eng, sent[t % 2], 16 * (t // 2))
                copy(y[t % 2][0:n, 512 * half:512 * (half + 1)], s.ps[(2 * t + half) % 8][0:n, :]).then_inc(done[half], 1)

        @block.vector
        def _(v):
            copy_half(v, v.tensor_copy, 0)

        @block.scalar
        def _(act):
            copy_half(act, lambda o, i: act.activation(o, i, ACT.Copy), 1)

        @block.sync
        def _(sp):
            for t in range(TT + 1):
                for half in range(2):
                    sp.wait_ge(done[half], t + 1)
                dst = T["y_prompt"][0, t * P:(t + 1) * P] if t < TT else T["y_sample"][:, 0]
                sp.dma_start(dst, y[t % 2][0:rows_of(t), :]).then_inc(sent[t % 2], 16)
            for b in range(2):
                sp.wait_ge(sent[b], 16 * len(range(b, TT + 1, 2)))


def program(nc, T):
    s = allocate(nc)
    stage_modulation(nc, s, T)
    stage_norm(nc, s, "n1", s.A1, SH1, s.hT, s.xT, s.xT_r, s.spilled)
    stage_token_major(nc, s, T)
    stage_compress(nc, s, T)
    stage_prompt_attention(nc, s, T)
    stage_decode_attention(nc, s, T)
    stage_hgrn(nc, s, T)
    recycle(nc, s)
    stage_mix(nc, s, T)
    stage_out_projection(nc, s, T)
    stage_norm(nc, s, "n2", s.A2, SH2, s.hT, view(s.work, 0, KT, TOK), s.work_short(0, KT, TOK))
    stage_ffn(nc, s, T)
    stage_output(nc, s, T)


_INS = ["x_prompt", "x_sample", "cache_cmp_k", "cache_cmp_v", "cache_slc_k", "cache_slc_v", "cache_win_k",
        "cache_win_v", "state_hgrn", "state_ffn_conv", "page_table", "c_prompt", "c_sample", "ada_w", "ada_b",
        "norm_attn", "norm_ffn", "w_in", "q_gain", "k_gain", "cmp_w1", "cmp_w2", "cmp_pe", "hg_lb", "hg_norm",
        "w_br_nsa", "w_br_hg", "w_out", "w_up", "conv_w", "conv_b", "w_down"]
_OUTS = [("y_prompt", (1, SEQ, D)), ("y_sample", (NB, 1, D)),
         ("p_ck", (1, 1, SEQ, NG, HD)), ("p_cv", (1, 1, SEQ, NG, HD)), ("p_sk", (1, 1, SEQ, NG, HD)),
         ("p_sv", (1, 1, SEQ, NG, HD)), ("p_wk", (1, 1, WIN, NG, HD)), ("p_wv", (1, 1, WIN, NG, HD)),
         ("p_hg", (1, 1, HGH, P, P)), ("p_cf", (1, 1, 2, DFF)),
         ("s_ck", (1, NB, 1, NG, HD)), ("s_cv", (1, NB, 1, NG, HD)), ("s_sk", (1, NB, 1, NG, HD)),
         ("s_sv", (1, NB, 1, NG, HD)), ("s_wk", (1, NB, WIN, NG, HD)), ("s_wv", (1, NB, WIN, NG, HD)),
         ("s_hg", (1, NB, HGH, P, P)), ("s_cf", (1, NB, 2, DFF))]


def kernel(**inputs):
    from concourse import bacc
    from concourse.bass_utils import run_bass_kernel_spmd

    nc = bacc.Bacc("TRN2", target_bir_lowering=False, num_devices=1)
    arrays, T = {}, {}
    given = {name: np.ascontiguousarray(inputs[name]) for name in _INS if name != "page_table"}
    given.update(constants())
    for name, a in given.items():
        arrays[f"in_{name}"] = a
        T[name] = nc.dram_tensor(f"in_{name}", a.shape, mybir.dt.from_np(a.dtype), kind="ExternalInput").ap()
    for name, shape in _OUTS:
        T[name] = nc.dram_tensor(f"out_{name}", shape, F32, kind="ExternalOutput").ap()
    T["x_spill"] = nc.dram_tensor("x_spill", (P, KT, TOK), F32).ap()
    T["hi_rows"] = nc.dram_tensor("hi_rows", (NB, 512), F32).ap()
    T["gate_rows"] = nc.dram_tensor("gate_rows", (NB, 24), F32).ap()
    pages = np.ascontiguousarray(np.repeat(inputs["page_table"].T, SUB_PER_PAGE, axis=0))
    arrays["in_page_rows"] = pages
    T["page_rows"] = nc.dram_tensor("in_page_rows", pages.shape, I32, kind="ExternalInput").ap()
    T["ada_w"], T["w_up"], T["w_down"], T["w_out"] = T["ada_w"][0], T["w_up"][0], T["w_down"][0], T["w_out"][0]
    program(nc, T)
    r = run_bass_kernel_spmd(nc, [arrays], core_ids=[0])
    return tuple(r.results[0][f"out_{name}"] for name, _ in _OUTS)
```

```python
import math

import numpy as np

import concourse.bass as bass
import concourse.mybir as mybir

F32 = mybir.dt.float32
F32R = mybir.dt.float32r
BF16 = mybir.dt.bfloat16
I32 = mybir.dt.int32
U32 = mybir.dt.uint32
U8 = mybir.dt.uint8
ALU = mybir.AluOpType
ACT = mybir.ActivationFunctionType
AX = mybir.AxisListType

P = 128
D = 1024
KT = D // P
SEQ = 1024
NB = 8
TOK = SEQ + NB
TT = SEQ // P
CH = TOK // 3
HD = 64
NH = 8
NG = 2
HPG = NH // NG
CMP_STRIDE = 16
NSUB_P = SEQ // CMP_STRIDE
NC_P = NSUB_P - 1
PAST = 2048
NSUB_S = PAST // CMP_STRIDE
NC_S = NSUB_S - 1
PAGE = 128
PAGES = PAST // PAGE
SUB_PER_PAGE = PAGE // CMP_STRIDE
SLC = 64
NSEL = 16
NS_S = PAST // SLC + 1
WIN = 512
HGH = 4
DFF = 2816
FT = DFF // P
EPS = 1e-6
X3 = 4128
NEG = -1e30
SCALE = HD ** -0.5

C_Q, C_KC, C_VS, C_GATE, C_HQ, C_HF, C_HI, C_HG, C_GA, C_GB = (
    0, 512, 896, 1280, 1304, 1816, 2328, 2840, 3352, 4376)
SH1, SC1, G1, SH2, SC2, G2 = (KT * i for i in range(6))


class Core:
    pass


class Unit:

    def __init__(self, kind, t, h, lo, n, last):
        self.kind, self.t, self.h, self.lo, self.n, self.last = kind, t, h, lo, n, last


def rows_of(t):
    return P if t < TT else NB


class Chain:

    def __init__(self, sem):
        self.sem, self.base, self.n, self.per = sem, 0, 0, None

    def link(self, eng, ins):
        self.n += 1
        ins.then_inc(self.sem, 1)
        eng.wait_ge(self.sem, self.base + self.n)

    def enter(self, i, per):
        self.before = self.base + self.n
        self.base, self.n, self.per = self.before + i * per, 0, per

    def leave(self, times):
        assert self.n == self.per, (self.n, self.per)
        self.base, self.n = self.before + self.per * times, 0


def constants():
    q = np.arange(P)[:, None]
    k = np.arange(P)[None, :]
    add = np.zeros((P, 2, P), np.float32)
    add[:, 0] = np.where(k <= q, 0.0, NEG)
    add[:, 1] = np.where(k > q, 0.0, NEG)
    cmp_ok = np.zeros((P, TT, HD), np.float32)
    for t in range(TT):
        cmp_ok[:, t, :NC_P] = (np.arange(NC_P)[None] * CMP_STRIDE + 31) <= (t * P + q)
    inv = (np.float32(500000.0) ** (-np.arange(0, 16, 2, dtype=np.float32) / np.float32(16))).astype(np.float32)
    pos = np.concatenate([np.arange(SEQ), np.full(NB, PAST)]).astype(np.float32)
    ang = (pos[:, None] * inv[None]).astype(np.float32)
    cos, sin = np.cos(ang), np.sin(ang)
    rope = np.concatenate([cos, cos, sin, sin], axis=1).astype(np.float32)
    start = np.arange(NC_S) * CMP_STRIDE
    s0 = np.arange(NS_S) * SLC
    over = ((start[:, None] <= s0[None] + SLC - 1) & (start[:, None] + 31 >= s0[None])).astype(np.float32)
    own = (np.arange(HD)[:, None] // NH == np.arange(NB)[None]).astype(np.float32)
    lower = (np.arange(NS_S)[None, :] < np.arange(NS_S)[:, None]).astype(np.float32)
    lower = np.broadcast_to(lower.reshape(1, -1), (HD, NS_S * NS_S))
    levels = np.zeros((P, 8, P), np.int32)
    s, t = q, k
    levels[:, 7] = s == t
    for n in range(7):
        m = 64 >> n
        levels[:, n] = (s // (2 * m) == t // (2 * m)) & (s % (2 * m) < m) & (t % (2 * m) >= m)
    return {
        "c_ident": np.eye(P, dtype=np.float32),
        "c_add": add,
        "c_cmp_add": np.where(cmp_ok > 0, 0.0, NEG).astype(np.float32),
        "c_cmp_mul": cmp_ok,
        "c_rope": rope,
        "c_over": over,
        "c_own": own,
        "c_lower": np.ascontiguousarray(lower),
        "c_sub": (np.arange(P)[:, None] % SUB_PER_PAGE).astype(np.float32),
        "c_levels": levels,
    }


def allocate(nc):
    sb = nc.alloc_sbuf_tensor
    s = Core()

    def region(name, size):
        base = -(-nc.sbuf_base // 32) * 32
        whole, parts = sb(name, [P, size], F32), {}

        def short(start, *shape):
            n = math.prod(shape)
            if (start, n) not in parts:
                parts[start, n] = nc.alloc_sbuf_tensor_at(f"{name}_short_{start}_{n}", [P, n], F32R,
                                                          offset=base + 4 * start)
            return view(parts[start, n], 0, *shape)
        return whole, short

    x, x_short = region("xT", KT * TOK)
    s.xT, s.xT_r = view(x, 0, KT, TOK), x_short(0, KT, TOK)
    s.hT = sb("hT", [P, KT, TOK], F32R)
    s.ring, s.ring_short = region("ring", 8192)
    s.work, s.work_short = region("work", 25904)
    s.ident = sb("ident", [P, P], F32)
    s.identb = sb("identb", [P, P], BF16)
    s.ones = sb("ones", [P, P], F32)
    s.add = sb("add", [P, 2, P], BF16)
    s.rope = sb("rope", [P, TT + 1, 32], F32)
    s.gain = sb("gain", [P, 4, HD], F32)
    s.vec = sb("vec", [P, 80], F32)
    s.conv = sb("conv", [P, 4, FT], F32)
    s.mod = sb("mod", [P, 6 * KT, NB + 1], F32)
    s.A1 = sb("A1", [P, KT, NB + 1], F32)
    s.A2 = sb("A2", [P, KT, NB + 1], F32)
    s.cT = sb("cT", [P, KT, NB + 1], F32)
    s.eps = sb("eps", [P, 1], F32)
    s.gidx = sb("gidx", [P, NB], U32)
    s.psall = nc.alloc_psum_tensor("psall", [P, 8 * 512], F32)
    s.ps = [s.psall[:, 512 * i:512 * (i + 1)] for i in range(8)]
    s.stage_sems = []

    def sem(name):
        s.stage_sems.append(nc.alloc_semaphore(name))
        return s.stage_sems[-1]

    s.sem = sem
    s.dve_chain = Chain(nc.alloc_semaphore("dve_chain"))
    s.act_chain = Chain(nc.alloc_semaphore("act_chain"))
    s.pool_chain = Chain(nc.alloc_semaphore("pool_chain"))
    s.oN = view(s.work, 0, 4, TOK)
    s.oH = view(s.work, 4128, 4, TOK)
    s.qT = view(s.work, 8256, 4, TOK)
    s.ksT = view(s.work, 12384, TOK)
    s.kwT = view(s.work, 13416, TOK)
    s.vkv = view(s.work, 14448, TT + 1, 2, P)
    s.vhi = view(s.work, 16752, TT + 1, 512)
    s.gates = view(s.work, 21360, TT + 1, 24)
    s.kcT = view(s.work, 21576, NB + 1, P)
    s.vc = view(s.work, 22728, NB + 1, P)
    return s


def wait(eng, sem, value):
    if not isinstance(value, int) or value > 0:
        eng.wait_ge(sem, value)


def recycle(nc, s):
    nc.clear_and_free_semaphores(s.stage_sems)
    nc.all_engine_barrier()
    s.stage_sems.clear()


def view(t, start, *shape):
    n = 1
    for x in shape:
        n *= x
    v = t[:, start:start + n]
    if len(shape) == 1:
        return v
    names = "abcd"[:len(shape)]
    return v.rearrange(f"p ({' '.join(names)}) -> p {' '.join(names)}", **dict(zip(names, shape)))


def bc(ap, shape):
    return ap.to_broadcast(list(shape))


def high(eng, hi, src):
    return eng.tensor_copy(hi, src)


def low(eng, lo, src, hi):
    return eng.tensor_tensor(lo, src, hi, ALU.subtract)


def product(pe, out, w, x, first, last):
    pe.matmul(out, w[0], x[0], start=first, stop=False)
    pe.matmul(out, w[0], x[1], start=False, stop=False)
    return pe.matmul(out, w[1], x[0], start=False, stop=last)


class Norm:

    def __init__(self, s, name, A, shift, t, lo, sq, logs, rstd, part, banks):
        self.s, self.A, self.shift, self.t, self.lo = s, A, shift, t, lo
        self.sq, self.logs, self.rstd, self.part, self.banks = sq, logs, rstd, part, banks
        self.squared, self.summed, self.rstd_ready = (s.sem(f"{name}_{x}") for x in ("squared", "summed", "rstd"))
        self.scaled, self.hi_ready, self.ready = (s.sem(f"{name}_{x}") for x in ("scaled", "hi", "ready"))

    def square(self, act, k):
        wait(act, self.summed, k - 1)
        act.activation(self.sq[k % 2], self.s.xT[:, k, :], ACT.Square).then_inc(self.squared, 1)

    def sum(self, pe, k):
        pe.wait_ge(self.squared, k + 1)
        for c in range(3):
            last = pe.matmul(self.s.ps[self.banks[c]][:, 0:CH], self.s.ones[:, :], self.sq[k % 2][:, c * CH:(c + 1) * CH],
                             start=(k == 0), stop=(k == KT - 1))
        last.then_inc(self.summed, 1)

    def root(self, act):
        s = self.s
        act.wait_ge(self.summed, KT)
        for c in range(3):
            last = act.activation(self.logs[:, c * CH:(c + 1) * CH], s.ps[self.banks[c]][:, 0:CH], ACT.Ln,
                                  bias=s.eps[:, 0:1], scale=1.0 / D)
        s.act_chain.link(act, last)
        act.activation(self.rstd, self.logs, ACT.Exp, scale=-0.5).then_inc(self.rstd_ready, 1)
        act.wait_ge(self.rstd_ready, 1)

    def take_high(self, act):
        s = self.s
        for k in range(KT):
            act.wait_ge(self.scaled, k + 1)
            act.activation(s.hT[:, k, 0:SEQ], self.t[:, k, 0:SEQ], ACT.Identity,
                           bias=s.mod[:, self.shift + k, 0:1]).then_inc(self.hi_ready, 1)

    def scale_and_take_low(self, v):
        s, ch, t = self.s, self.s.dve_chain, self.t
        dec = slice(SEQ, TOK)
        part = self.part
        ch.link(v, v.tensor_tensor(part, s.xT[:, :, dec], self.A[:, :, 1:NB + 1], ALU.mult))
        ch.link(v, v.tensor_tensor(part, part, bc(self.rstd[:, dec].unsqueeze(1), (P, KT, NB)), ALU.mult))
        ch.link(v, v.tensor_tensor(t[:, :, dec], part, s.mod[:, self.shift:self.shift + KT, 1:NB + 1], ALU.add))
        ch.link(v, high(v, s.hT[:, :, dec], t[:, :, dec]))
        ch.link(v, low(v, self.lo[:, :, dec], t[:, :, dec], s.hT[:, :, dec]))

        def take_low(k):
            v.wait_ge(self.hi_ready, k + 1)
            v.scalar_tensor_tensor(out=self.lo[:, k, 0:SEQ], in0=t[:, k, 0:SEQ], scalar=s.mod[:, self.shift + k, 0:1],
                                   in1=s.hT[:, k, 0:SEQ], op0=ALU.add, op1=ALU.subtract).then_inc(self.ready, 1)

        for k in range(KT):
            v.scalar_tensor_tensor(out=t[:, k, 0:SEQ], in0=s.xT[:, k, 0:SEQ], scalar=self.A[:, k, 0:1],
                                   in1=self.rstd[:, 0:SEQ], op0=ALU.mult, op1=ALU.mult).then_inc(self.scaled, 1)
            if k >= 1:
                take_low(k - 1)
        take_low(KT - 1)


def stage_modulation(nc, s, T, norm, projections):
    x_tm = view(s.work, 0, TT + 1, D)
    rows = view(s.work, 9216, P)
    crow = view(s.work, 9344, P)
    c_tm = view(s.work, 9472, D)
    add_f = view(s.work, 10496, 2, P)
    panel = [view(s.ring, 2048 * i, KT, 256) for i in range(4)]
    x_in, c_in = s.sem("m_x_in"), s.sem("m_c_in")
    loaded = [s.sem(f"m_loaded{i}") for i in range(4)]
    panel_used, tr_done = s.sem("m_panel_used"), s.sem("m_tr_done")
    evac_v, evac_a, ada_done = s.sem("m_evac_v"), s.sem("m_evac_a"), s.sem("m_ada_done")
    ready = s.sem("m_cT_ready")
    ada = T["ada_w"].rearrange("(k p) n -> p k n", p=P)
    NGRP = 2 * (TT + 1)
    PANELS = G1 * P // 256
    s.spilled = s.sem("m_spilled")

    with nc.Block() as block:
        @block.sync
        def _(sp):
            sp.dma_start(s.ident[:, :], T["c_ident"]).then_inc(c_in, 16)
            sp.dma_start(c_tm[0:1, :], T["c_prompt"]).then_inc(c_in, 16)
            sp.dma_start(c_tm[1:NB + 1, :], T["c_sample"]).then_inc(c_in, 16)
            for n in range(PANELS):
                wait(sp, panel_used, n - 3)
                sp.dma_start(panel[n % 4], ada[:, :, n * 256:(n + 1) * 256]).then_inc(loaded[n % 4], 16)
            sp.wait_ge(evac_v, 3 + TT + 1)
            sp.wait_ge(evac_a, TT + 1)
            sp.dma_start(T["x_spill"], s.xT[:, :, :]).then_inc(s.spilled, 16)
            projections.load(sp, 0)

        @block.gpsimd
        def _(pool):
            projections.take_low(pool, 0)

        @block.scalar
        def _(act):
            act.dma_start(rows[0:48, :], T["ada_b"][0].rearrange("(r p) -> r p", p=P)).then_inc(x_in, 16)
            act.dma_start(rows[48:56, :], T["norm_attn"][0].rearrange("(r p) -> r p", p=P)).then_inc(x_in, 16)
            act.dma_start(rows[56:64, :], T["norm_ffn"][0].rearrange("(r p) -> r p", p=P)).then_inc(x_in, 16)
            act.dma_start(rows[64:72, :], T["hg_lb"].rearrange("a (r p) -> (a r) p", p=P)).then_inc(x_in, 16)
            act.dma_start(rows[72:73, :], T["hg_norm"]).then_inc(x_in, 16)
            act.dma_start(crow[0:66, :], T["conv_w"][0].rearrange("j (r p) -> (j r) p", p=P)).then_inc(x_in, 16)
            act.dma_start(crow[66:88, :], T["conv_b"][0].rearrange("(r p) -> r p", p=P)).then_inc(x_in, 16)
            act.dma_start(x_tm[:, 0:TT, :], T["x_prompt"][0].rearrange("(t p) d -> p t d", p=P)).then_inc(x_in, 16)
            act.dma_start(x_tm[0:NB, TT, :], T["x_sample"].rearrange("b t d -> (b t) d")).then_inc(x_in, 16)
            act.dma_start(add_f, T["c_add"]).then_inc(x_in, 16)
            act.dma_start(s.rope[:, 0:TT, :], T["c_rope"][0:SEQ].rearrange("(t p) c -> p t c", p=P)).then_inc(x_in, 16)
            act.dma_start(s.rope[0:NB, TT, :], T["c_rope"][SEQ:TOK]).then_inc(x_in, 16)
            act.dma_start(s.gain[:, 0, :], T["q_gain"].partition_broadcast(P).rearrange("p a d -> p (a d)")).then_inc(x_in, 16)
            act.dma_start(s.gain[:, 1:4, :], T["k_gain"][0].partition_broadcast(P)).then_inc(x_in, 16)
            for g in range(1, NGRP, 2):
                t, half = g // 2, g % 2
                n = rows_of(t)
                act.wait_ge(tr_done, 4 + g)
                act.activation(s.xT[:, 4 * half:4 * half + 4, t * P:t * P + n],
                               view(s.ps[2 + g % 4], 0, 4, P)[:, :, 0:n], ACT.Copy).then_inc(evac_a, 1)
            act.wait_ge(x_in, 224)
            act.wait_ge(evac_v, 3 + TT + 1)
            act.wait_ge(evac_a, TT + 1)
            for k in range(KT):
                norm.square(act, k)
            norm.root(act)

        @block.tensor
        def _(pe):
            pe.wait_ge(c_in, 48)
            for k in range(KT):
                last = pe.transpose(s.ps[1][:, 9 * k:9 * k + 9], c_tm[0:9, k * P:(k + 1) * P], s.ident[0:9, 0:9])
            last.then_inc(tr_done, 1)

            def modulate(n):
                pe.wait_ge(loaded[n % 4], 16 * (n // 4 + 1))
                for h in range(2):
                    for k in range(KT):
                        last = pe.matmul(s.ps[0][:, (2 * n + h) * 9:(2 * n + h + 1) * 9],
                                         panel[n % 4][:, k, h * P:(h + 1) * P], s.cT[:, k, :],
                                         start=(k == 0), stop=(k == KT - 1))
                last.then_inc(panel_used, 1)

            pe.wait_ge(ready, 1)
            for n in range(2):
                modulate(n)
            pe.wait_ge(x_in, 224)
            pe.transpose(s.ps[2][:, 0:73], rows[0:73, :], s.ident[0:73, 0:73]).then_inc(tr_done, 1)
            pe.transpose(s.ps[3][:, 0:88], crow[0:88, :], s.ident[0:88, 0:88]).then_inc(tr_done, 1)
            for g in range(NGRP):
                t, half = g // 2, g % 2
                n = rows_of(t)
                if g < 2:
                    pe.wait_ge(evac_v, 3)
                elif g >= 4:
                    if g % 2:
                        pe.wait_ge(evac_a, (g - 4) // 2 + 1)
                    else:
                        pe.wait_ge(evac_v, 3 + (g - 4) // 2 + 1)
                for j in range(4):
                    k = 4 * half + j
                    last = pe.transpose(s.ps[2 + g % 4][:, j * P:j * P + n], x_tm[0:n, t, k * P:(k + 1) * P],
                                        s.ident[0:n, 0:n])
                last.then_inc(tr_done, 1)
            for n in range(2, 5):
                modulate(n)
            for k in range(KT):
                norm.sum(pe, k)
            for n in range(5, PANELS):
                modulate(n)
            pe.wait_ge(panel_used, PANELS)
            pe.sem_inc(ada_done, 1)

        @block.vector
        def _(v):
            ch = s.dve_chain
            v.memset(s.ones[:, :], 1.0)
            ch.link(v, v.memset(s.eps[:, :], EPS))
            v.wait_ge(tr_done, 1)
            v.tensor_copy(s.cT[:, :, :], view(s.ps[1], 0, KT, 9)).then_inc(ready, 1)
            v.wait_ge(c_in, 48)
            v.tensor_copy(s.identb[:, :], s.ident[:, :])
            v.wait_ge(tr_done, 3)
            v.wait_ge(x_in, 224)
            v.tensor_copy(s.add[:, :, :], add_f)
            v.tensor_copy(s.vec[:, 0:73], s.ps[2][:, 0:73]).then_inc(evac_v, 1)
            v.tensor_copy(s.conv[:, :, :], view(s.ps[3], 0, 4, FT)).then_inc(evac_v, 1)
            v.wait_ge(evac_v, 2)
            v.nop().then_inc(evac_v, 1)
            for g in range(0, NGRP, 2):
                t, half = g // 2, g % 2
                n = rows_of(t)
                v.wait_ge(tr_done, 4 + g)
                v.tensor_copy(s.xT[:, 4 * half:4 * half + 4, t * P:t * P + n],
                              view(s.ps[2 + g % 4], 0, 4, P)[:, :, 0:n]).then_inc(evac_v, 1)
            projections.take_high(v, 0)
            v.wait_ge(ada_done, 1)
            finish_modulation(s, v, 0, G1, s.ps[0])
            scale_gain(s, v, s.A1, SC1, 48)


def finish_modulation(s, v, first, end, ps):
    n = end - first
    s.dve_chain.link(v, v.tensor_tensor(s.mod[:, first:end, :], view(ps, 0, n, 9),
                                        bc(s.vec[:, first:end].unsqueeze(2), (P, n, 9)), ALU.add))


def scale_gain(s, v, A, scale, gain):
    ch = s.dve_chain
    ch.link(v, v.tensor_scalar(A[:, :, :], s.mod[:, scale:scale + KT, :], 1.0, None, ALU.add))
    ch.link(v, v.tensor_tensor(A[:, :, :], A[:, :, :], bc(s.vec[:, gain:gain + KT].unsqueeze(2), (P, KT, 9)), ALU.mult))


class TokenMajorWeights:

    def __init__(self, s, T):
        self.groups = ((C_Q, 512), (C_KC, 384), (C_VS, 408), (C_HI, 512))
        home, short = (s.work, s.ring), (s.work_short, s.ring_short)
        self.raw = [view(home[g % 2], 4096, KT, w) for g, (_, w) in enumerate(self.groups)]
        self.hi, self.lo = ([short[g % 2](at, KT, w) for g, (_, w) in enumerate(self.groups)] for at in (0, 4096))
        self.loaded = [s.sem(f"t_w{i}") for i in range(4)]
        self.cut, self.split = s.sem("t_cut"), s.sem("t_split")
        self.w_in = T["w_in"][0].rearrange("(k p) n -> p k n", p=P)

    def load(self, eng, g):
        c, w = self.groups[g]
        eng.dma_start(self.raw[g], self.w_in[:, :, c:c + w]).then_inc(self.loaded[g], 16)

    def take_high(self, v, g):
        v.wait_ge(self.loaded[g], 16)
        high(v, self.hi[g], self.raw[g]).then_inc(self.cut, 1)

    def take_low(self, pool, g):
        pool.wait_ge(self.cut, g + 1)
        low(pool, self.lo[g], self.raw[g], self.hi[g]).then_inc(self.split, 1)


def stage_token_major(nc, s, T, weights, norm):
    groups, raw, w_hi, w_lo, w_loaded = weights.groups, weights.raw, weights.hi, weights.lo, weights.loaded
    cut, split = weights.cut, weights.split
    w_in = T["w_in"][0].rearrange("(k p) n -> p k n", p=P)
    F = 21576
    sq = [view(s.work, F + 512 * i, 512) for i in range(2)]
    stat = [view(s.work, F + 1024 + 64 * i, 64) for i in range(2)]
    rot = [view(s.work, F + 1152 + 256 * i, 256) for i in range(2)]
    qn = [view(s.work, F + 1664 + 512 * i, 512) for i in range(3)]
    NT = TT + 1
    UNITS = 4 * NT
    n_psum = 3
    mm, act_free, dve_free = s.sem("t_mm"), s.sem("t_act_free"), s.sem("t_dve_free")
    squared, summed, rstd_ready = s.sem("t_squared"), s.sem("t_summed"), s.sem("t_rstd")
    normed, turned, turn_read = s.sem("t_normed"), s.sem("t_turned"), s.sem("t_turn_read")
    copied = s.sem("t_copied")
    sent = [s.sem(f"t_sent{i}") for i in range(3)]
    sent_v = s.sem("t_sent_v")

    with nc.Block() as block:
        @block.gpsimd
        def _(pool):
            weights.take_low(pool, 1)
            for g in (2, 3):
                pool.wait_ge(mm, (g - 1) * NT)
                weights.load(pool, g)
                weights.take_low(pool, g)

        @block.sync
        def _(sp):
            weights.load(sp, 1)
            for u in range(NT, 3 * NT):
                g, t = u // NT, u % NT
                n = rows_of(t)
                st = qn[u % 3]
                sp.wait_ge(normed, u + 1)
                sp.wait_ge(copied, u + 1)
                rows = slice(t * P, t * P + P)
                flat = lambda a: a.rearrange("t g d -> t (g d)")
                if g == 1:
                    for j, (pr, sa) in enumerate(((T["p_ck"], T["s_ck"]), (T["p_cv"], T["s_cv"]), (T["p_sk"], T["s_sk"]))):
                        dst = flat(pr[0, 0, rows]) if t < TT else flat(sa[0, :, 0])
                        sp.dma_start(dst, st[0:n, j * P:(j + 1) * P]).then_inc(sent[u % 3], 16)
                else:
                    dst = flat(T["p_sv"][0, 0, rows]) if t < TT else flat(T["s_sv"][0, :, 0])
                    sp.dma_start(dst, s.vkv[0:n, t, 0, :]).then_inc(sent_v, 16)
                    if t >= TT - WIN // P:
                        rows = slice((t - TT + WIN // P) * P, (t - TT + WIN // P + 1) * P)
                        dst = flat(T["p_wk"][0, 0, rows]) if t < TT else flat(T["s_wk"][0, :, WIN - 1])
                        sp.dma_start(dst, st[0:n, 0:P]).then_inc(sent[u % 3], 16)
                        dst = flat(T["p_wv"][0, 0, rows]) if t < TT else flat(T["s_wv"][0, :, WIN - 1])
                        sp.dma_start(dst, s.vkv[0:n, t, 1, :]).then_inc(sent_v, 16)
            sp.wait_ge(copied, UNITS)
            sp.dma_start(T["hi_rows"], s.vhi[0:NB, TT, :]).then_inc(sent_v, 16)
            sp.dma_start(T["gate_rows"], s.gates[0:NB, TT, :]).then_inc(sent_v, 16)
            sp.wait_ge(sent_v, 16 * (NT + WIN // P + 1 + 2))
            for b in range(3):
                sp.wait_ge(sent[b], 16 * sum((3 if u < 2 * NT else u % NT >= TT - WIN // P)
                                             for u in range(NT, 3 * NT) if u % 3 == b))

        @block.tensor
        def _(pe):
            def turn(u):
                g, t = u // NT, u % NT
                if u < 0 or g > 2:
                    return
                n = rows_of(t)
                pe.wait_ge(normed, u + 1)
                if u >= 2:
                    pe.wait_ge(turn_read, u - 1)
                out = s.ps[6 + u % 2]
                if g == 0:
                    for j in range(HPG):
                        last = pe.transpose(out[:, j * P:j * P + n], qn[u % 3][0:n, j * P:(j + 1) * P],
                                            s.ident[0:n, 0:n])
                else:
                    at = 256 if g == 1 else 0
                    last = pe.transpose(out[:, 0:n], qn[u % 3][0:n, at:at + P], s.ident[0:n, 0:n])
                last.then_inc(turned, 1)

            for u in range(UNITS):
                g, t = u // NT, u % NT
                n, w = rows_of(t), groups[g][1]
                if t == 0:
                    pe.wait_ge(split, g + 1)
                if u >= n_psum:
                    pe.wait_ge(act_free, u - n_psum + 1)
                    pe.wait_ge(dve_free, u - n_psum + 1)
                if u == 0:
                    for k in range(KT):
                        pe.wait_ge(norm.ready, k + 1)
                        for first in range(n_psum):
                            cols = slice(first * P, (first + 1) * P)
                            last = product(pe, s.ps[first][:, 0:w], (s.hT[:, k, cols], s.xT_r[:, k, cols]),
                                           (w_hi[0][:, k, :], w_lo[0][:, k, :]), k == 0, k == KT - 1)
                            if k == KT - 1:
                                last.then_inc(mm, 1)
                if u < n_psum:
                    turn(u - 2)
                    continue
                cols = slice(t * P, t * P + n)
                for k in range(KT):
                    last = product(pe, s.ps[u % n_psum][0:n, 0:w], (s.hT[:, k, cols], s.xT_r[:, k, cols]),
                                   (w_hi[g][:, k, :], w_lo[g][:, k, :]), k == 0, k == KT - 1)
                last.then_inc(mm, 1)
                turn(u - 2)

        @block.scalar
        def _(act):
            ch = s.act_chain

            def evacuate(u):
                g, t = u // NT, u % NT
                n = rows_of(t)
                act.wait_ge(turned, u + 1)
                cols = slice(t * P, t * P + n)
                if g == 0:
                    src = view(s.ps[6 + u % 2], 0, HPG, P)[:, :, 0:n]
                    act.activation(s.qT[:, :, cols], src, ACT.Copy).then_inc(turn_read, 1)
                else:
                    dst = s.ksT if g == 1 else s.kwT
                    act.activation(dst[:, cols], s.ps[6 + u % 2][:, 0:n], ACT.Copy).then_inc(turn_read, 1)

            norm.take_high(act)
            for u in range(UNITS):
                g, t = u // NT, u % NT
                n = rows_of(t)
                ps = s.ps[u % n_psum]
                act.wait_ge(mm, u + 1)
                if g == 3:
                    ch.link(act, act.activation(s.vhi[0:n, t, :], ps[0:n, :], ACT.Copy))
                    act.nop().then_inc(act_free, 1)
                    act.nop().then_inc(copied, 1)
                    if u <= 3 * NT + 1:
                        evacuate(u - 2)
                    continue
                if u >= 2:
                    act.wait_ge(summed, u - 1)
                if g == 0:
                    act.activation(sq[u % 2][0:n, :], ps[0:n, :], ACT.Square).then_inc(squared, 1)
                elif g == 1:
                    if u >= NT + 3:
                        act.wait_ge(sent[u % 3], 16 * 3 * ((u - NT) // 3))
                    act.activation(qn[u % 3][0:n, P:2 * P], ps[0:n, P:2 * P], ACT.Copy)
                    act.activation(sq[u % 2][0:n, 0:384], ps[0:n, 0:384], ACT.Square).then_inc(squared, 1)
                else:
                    act.activation(s.vkv[0:n, t, :, :], ps[0:n, 0:512].rearrange("p (a c) -> p a c", a=2)[:, :, 0:P],
                                   ACT.Copy)
                    act.activation(s.gates[0:n, t, :], ps[0:n, 384:408], ACT.Exp, scale=-1.0)
                    act.activation(sq[u % 2][0:n, 0:P], ps[0:n, P:2 * P], ACT.Square).then_inc(squared, 1)
                act.wait_ge(squared, u + 1)
                act.nop().then_inc(act_free, 1)
                act.nop().then_inc(copied, 1)
                if u >= 2:
                    evacuate(u - 2)
                act.wait_ge(summed, u + 1)
                st = stat[u % 2]
                ch.link(act, act.activation(st[0:n, 8:16], st[0:n, 0:8], ACT.Ln, bias=s.eps[0:n, 0:1],
                                            scale=1.0 / HD))
                act.activation(st[0:n, 16:24], st[0:n, 8:16], ACT.Exp, scale=-0.5).then_inc(rstd_ready, 1)

        @block.vector
        def _(v):
            ch = s.dve_chain
            for i in range(2):
                ch.link(v, v.memset(stat[i], 1.0))
            ch.link(v, v.tensor_scalar(s.gain[:, 0, :], s.gain[:, 0, :], SCALE, None, ALU.mult))
            v.wait_ge(s.spilled, 16)
            norm.scale_and_take_low(v)
            weights.take_high(v, 1)
            for u in range(3 * NT):
                if u in (NT + 6, 2 * NT + 6):
                    v.wait_ge(mm, (u // NT) * NT)
                    weights.take_high(v, u // NT + 1)
                g, t = u // NT, u % NT
                n = rows_of(t)
                ps, st, sqt = s.ps[u % n_psum], stat[u % 2], sq[u % 2]
                if g == 0:
                    kinds, heads, gain, out = NG, HPG, 0, qn[u % 3]
                elif g == 1:
                    kinds, heads, gain, out = 2, NG, 1, qn[u % 3]
                else:
                    kinds, heads, gain, out = 1, NG, 3, qn[u % 3]

                def parts(tile, at=0):
                    if g == 1:
                        return tile[0:n, 0:384].rearrange("p (k h d) -> p k h d", k=3, d=HD)[:, 0:3:2]
                    return tile[0:n, at:at + kinds * heads * HD].rearrange("p (k h d) -> p k h d", k=kinds, d=HD)
                v.wait_ge(squared, u + 1)
                sums = st[0:n, 0:kinds * heads].rearrange("p (k h) -> p k h", k=kinds)
                v.tensor_reduce(sums, parts(sqt), AX.X, ALU.add).then_inc(summed, 1)
                v.wait_ge(rstd_ready, u + 1)
                shape = (n, kinds, heads, HD)
                rstd = st[0:n, 16:16 + kinds * heads].rearrange("p (k h) -> p k h", k=kinds).unsqueeze(3)
                dst = parts(out) if g else out[0:n, :].rearrange("p (h k d) -> p k h d", k=NG, d=HD)
                if u >= 3:
                    v.wait_ge(turned, u - 2)
                if g >= 1 and u >= NT + 3:
                    done = sum((3 if w < 2 * NT else w % NT >= TT - WIN // P)
                               for w in range(NT, u - 2) if w % 3 == u % 3)
                    v.wait_ge(sent[u % 3], 16 * done)
                ch.link(v, v.tensor_tensor(dst, parts(ps, P if g == 2 else 0), bc(rstd, shape), ALU.mult))
                v.nop().then_inc(dve_free, 1)
                for kd in range(kinds):
                    row = s.gain[0:n, gain + (kd if g else 0), :].unsqueeze(1)
                    last = v.tensor_tensor(dst[:, kd], dst[:, kd], bc(row, (n, heads, HD)), ALU.mult)
                ch.link(v, last)
                for kd in range(kinds):
                    x = dst[:, kd, :, 0:16]
                    a, b = (r[0:n, kd * 128:kd * 128 + heads * 16].rearrange("p (h c) -> p h c", c=16) for r in rot)
                    v.tensor_tensor(a, x, bc(s.rope[0:n, t, 0:16].unsqueeze(1), (n, heads, 16)), ALU.mult)
                    ch.link(v, v.tensor_tensor(b, x, bc(s.rope[0:n, t, 16:32].unsqueeze(1), (n, heads, 16)), ALU.mult))
                    v.tensor_tensor(x[:, :, 0:8], a[:, :, 0:8], b[:, :, 8:16], ALU.subtract)
                    ch.link(v, v.tensor_tensor(x[:, :, 8:16], a[:, :, 8:16], b[:, :, 0:8], ALU.add))
                if g == 2:
                    ga = s.gates[0:n, t, :]
                    ch.link(v, v.tensor_scalar(ga, ga, 1.0, None, ALU.add))
                    ch.link(v, v.reciprocal(ga, ga))
                v.nop().then_inc(normed, 1)
            for u in range(3 * NT, UNITS):
                v.nop().then_inc(dve_free, 1)


def stage_compress(nc, s, T):
    rows = [view(s.ring, 2048 * a, CMP_STRIDE, P) for a in range(2)]
    pairs = [view(s.ring, 4096 + 2048 * a, NG, 8, P) for a in range(2)]
    w1 = view(s.work, X3 + 1888, 2, 8, 2 * HD)
    w2 = view(s.work, 24392, 3, HD)
    pe_rows = view(s.work, X3 + 128, P)
    peT = view(s.work, X3 + 256, 2, 2, 8)
    pe_h = view(s.work, X3 + 288, 2)
    lifted = [view(s.work, X3 + 320 + 256 * a, NG, P) for a in range(2)]
    hid = [view(s.work, X3 + 832 + 256 * a, NG, P) for a in range(2)]
    act_h = [view(s.work, X3 + 1344 + 256 * a, NG, P) for a in range(2)]
    pages = view(s.work, X3 + 1856, NB)
    pages_f = view(s.work, X3 + 1864, NB)
    sub = view(s.work, X3 + 1872, 1)
    small, idx_ready = s.sem("c_small"), s.sem("c_idx")
    rows_in = [s.sem(f"c_rows{a}") for a in range(2)]
    prompt_in = [s.sem(f"c_prompt{a}") for a in range(2)]
    turned, mixed, made = s.sem("c_turned"), s.sem("c_mixed"), s.sem("c_made")
    evac_a, evac_v = s.sem("c_evac_a"), s.sem("c_evac_v")
    lift, summed, gelu, placed = s.sem("c_lift"), s.sem("c_summed"), s.sem("c_gelu"), s.sem("c_placed")
    pe_terms, pe_read = s.sem("c_pe_terms"), s.sem("c_pe_read")

    def pipeline(eng, first, second, third):
        first(0, 0, NSUB_P)
        first(0, 1, NSUB_P)
        second(0, 0, NSUB_P)
        first(1, 0, NSUB_S)
        second(0, 1, NSUB_P)
        third(0, 0, NSUB_P)
        first(1, 1, NSUB_S)
        second(1, 0, NSUB_S)
        third(0, 1, NSUB_P)
        with eng.Fori(2, NB + 1) as q:
            first(q, 0, NSUB_S)
            second(q - 1, 1, NSUB_S)
            third(q - 1, 0, NSUB_S)
            first(q, 1, NSUB_S)
            second(q, 0, NSUB_S)
            third(q - 1, 1, NSUB_S)
        second(NB, 1, NSUB_S)
        third(NB, 0, NSUB_S)
        third(NB, 1, NSUB_S)

    def nothing(q, a, n):
        pass

    with nc.Block() as block:
        @block.sync
        def _(sp):
            for a in range(2):
                for r in range(2):
                    sp.dma_start(w1[:, a, :, r * HD:(r + 1) * HD],
                                 T["cmp_w1"][0, a, r * 1024:(r + 1) * 1024].rearrange("(e q) h -> q e h", q=P)
                                 ).then_inc(small, 16)
                sp.dma_start(w2[0:HD, a, :], T["cmp_w2"][0, 0]).then_inc(small, 16)
            sp.dma_start(pe_rows[0:32, :], T["cmp_pe"][0].rearrange("a (r q) d -> (a r) (q d)", q=2)).then_inc(small, 16)
            sp.dma_start(w2[0:HD, 2, :], T["cmp_w2"][0, 1]).then_inc(small, 16)
            sp.dma_start(sub, T["c_sub"]).then_inc(small, 16)
            sp.dma_start(pages.bitcast(I32), T["page_rows"]).then_inc(small, 16)
            for a, src in enumerate((T["p_ck"], T["p_cv"])):
                sp.dma_start(rows[a][0:NSUB_P].rearrange("p t c -> p (t c)"),
                             src[0, 0].rearrange("(n t) g d -> n (t g d)", t=CMP_STRIDE)).then_inc(prompt_in[a], 16)

        @block.gpsimd
        def _(pool):
            pool.wait_ge(idx_ready, 1)
            for b in range(NB):
                for a, src in enumerate((T["cache_cmp_k"], T["cache_cmp_v"])):
                    pool.wait_ge(turned, 4 * (2 * b + a) + 4)
                    pool.indirect_dma_start(
                        out=rows[a].rearrange("p t c -> p (t c)"), out_offset=None,
                        in_=src[0].rearrange("n (j t) g d -> (n j) (t g d)", t=CMP_STRIDE),
                        in_offset=bass.IndirectOffsetOnAxis(ap=s.gidx[:, b:b + 1], axis=0)).then_inc(rows_in[a], 16)

        @block.tensor
        def _(pe):
            pe.wait_ge(small, 160)
            pe.transpose(s.ps[6][:, 0:32], pe_rows[0:32, :], s.ident[0:32, 0:32]).then_inc(pe_terms, 1)
            pe.wait_ge(pe_read, 1)
            for a in range(2):
                for r in range(2):
                    for e in range(8):
                        last = pe.matmul(s.ps[7][0:HD, a:a + 1], w1[:, a, e, r * HD:(r + 1) * HD],
                                         peT[:, a, r, e:e + 1], start=(r + e == 0), stop=(r * e == 7))
            last.then_inc(pe_terms, 1)
            pe.wait_ge(pe_read, 2)

            def turn(q, a, n):
                pe.wait_ge(*((prompt_in[a], 16) if isinstance(q, int) and q == 0 else (rows_in[a], 16 * q)))
                for bank in range(4):
                    wait(pe, evac_a if bank % 2 else evac_v, 2 * (2 * q + a - 1) + bank // 2 + 1)
                    for j in range(4):
                        last = pe.transpose(s.ps[bank][:, j * P:j * P + n], rows[a][0:n, 4 * bank + j, :],
                                            s.ident[0:n, 0:n])
                    last.then_inc(turned, 1)

            def mix(q, a, n):
                pe.wait_ge(evac_a, 2 * (2 * q + a) + 2)
                pe.wait_ge(evac_v, 2 * (2 * q + a) + 2)
                wait(pe, summed, 2 * q + a - 1)
                out = view(s.ps[4 + a], 0, NG, P)[:, :, 0:n]
                for e in range(8):
                    last = pe.matmul(out, w1[:, a, e, :], pairs[a][:, :, e, 0:n], start=(e == 0), stop=(e == 7))
                last.then_inc(mixed, 1)

            def make(q, a, n):
                m = n - 1
                pe.wait_ge(gelu, 2 * q + a + 1)
                wait(pe, placed, 2 * q + a - 1)
                for g in range(NG):
                    if a == 0:
                        last = pe.matmul(s.ps[6][:, g * P:g * P + m], w2[0:HD, 0:2, :].rearrange("p a d -> p (a d)"),
                                         act_h[0][0:HD, g, 0:m], start=True, stop=True)
                    else:
                        last = pe.matmul(s.ps[7][0:m, g * HD:(g + 1) * HD], act_h[1][0:HD, g, 0:m], w2[0:HD, 2, :],
                                         start=True, stop=True)
                last.then_inc(made, 1)

            pipeline(pe, turn, mix, make)

        def evacuate(eng, copy, done, banks):
            def run(q, a, n):
                wait(eng, mixed, 2 * q + a - 1)
                for bank in banks:
                    eng.wait_ge(turned, 4 * (2 * q + a) + bank + 1)
                    src = view(s.ps[bank], 0, 2, 2, P)
                    for s2 in range(2):
                        for g in range(NG):
                            last = copy(pairs[a][s2 * HD:(s2 + 1) * HD, g, 2 * bank:2 * bank + 2, 0:n],
                                        src[g * HD:(g + 1) * HD, :, s2, 0:n])
                    last.then_inc(done, 1)
            return run

        @block.scalar
        def _(act):
            act.wait_ge(pe_terms, 1)

            def lift_gelu(q, a, n):
                m = n - 1
                act.wait_ge(mixed, 2 * q + a + 1)
                wait(act, summed, 2 * q + a - 1)
                src = view(s.ps[4 + a], 0, NG, P)
                act.activation(lifted[a][0:HD, :, 0:m], src[HD:P, :, 1:n], ACT.Identity,
                               bias=pe_h[0:HD, a:a + 1]).then_inc(lift, 1)
                act.wait_ge(summed, 2 * q + a + 1)
                wait(act, made, 2 * q + a - 1)
                act.activation(act_h[a][0:HD, :, 0:m], hid[a][0:HD, :, 0:m], ACT.Gelu_apprx_tanh).then_inc(gelu, 1)

            act.wait_ge(pe_read, 2)
            pipeline(act, evacuate(act, lambda o, i: act.activation(o, i, ACT.Copy), evac_a, (1, 3)), lift_gelu, nothing)

        @block.vector
        def _(v):
            ch = s.dve_chain
            v.wait_ge(small, 160)
            ch.link(v, v.tensor_copy(pages_f, pages.bitcast(I32)))
            ch.link(v, v.tensor_scalar(pages_f, pages_f, float(SUB_PER_PAGE), sub[:, 0:1], ALU.mult, ALU.add))
            v.tensor_copy(s.gidx[:, :], pages_f).then_inc(idx_ready, 1)
            v.wait_ge(pe_terms, 1)
            v.tensor_copy(view(s.work, X3 + 256, 32), s.ps[6][:, 0:32]).then_inc(pe_read, 1)
            v.wait_ge(pe_terms, 2)
            v.tensor_copy(pe_h[0:HD, :], s.ps[7][0:HD, 0:2]).then_inc(pe_read, 1)

            def add(q, a, n):
                m = n - 1
                v.wait_ge(lift, 2 * q + a + 1)
                wait(v, gelu, 2 * q + a - 1)
                src = view(s.ps[4 + a], 0, NG, P)
                v.tensor_tensor(hid[a][0:HD, :, 0:m], src[0:HD, :, 0:m], lifted[a][0:HD, :, 0:m],
                                ALU.add).then_inc(summed, 1)

            def place(q, a, n):
                m = n - 1
                v.wait_ge(made, 2 * q + a + 1)
                if a == 0:
                    keys = s.kcT.rearrange("p q n -> p (q n)")
                    for g in range(NG):
                        half = slice(g * HD, (g + 1) * HD)
                        last = v.tensor_copy(keys[half, bass.ds(q * P, m)], s.ps[6][half, g * P:g * P + m])
                else:
                    values = s.vc.rearrange("p q n -> p (q n)")
                    last = v.tensor_copy(values[0:m, bass.ds(q * P, P)], s.ps[7][0:m, 0:P])
                last.then_inc(placed, 1)

            pipeline(v, evacuate(v, v.tensor_copy, evac_v, (0, 2)), add, place)


def stage_prompt_attention(nc, s, T):
    prob = [view(s.ring, 1024 * i, 1024) for i in range(2)]
    probT = [view(s.ring, 2048 + 1024 * i, 1024) for i in range(2)]
    o_tm = [view(s.ring, 4096 + 512 * i, 512) for i in range(2)]
    part = view(s.ring, 5120, 512)
    top = view(s.ring, 5632, 2, 8)
    total = view(s.ring, 5648, 4, 8)
    coef = view(s.ring, 5680, 8)
    cmp_add = view(s.work, 23880, 256).bitcast(BF16).rearrange("p (t n) -> p t n", t=TT)
    cmp_add_f = view(s.ring, 6144, TT, HD)
    cmp_mul = view(s.ring, 6656, TT, HD)
    score = [s.psall[:, 1024 * i:1024 * (i + 1)] for i in range(2)]
    turn_ps = [s.ps[4], s.ps[5]]
    out_ps = [s.ps[6], s.ps[7]]
    masks_in, mask_cast, window_out = s.sem("a_masks"), s.sem("a_mask_cast"), s.sem("a_window_out")
    scored, maxed, exped, masked = s.sem("a_scored"), s.sem("a_maxed"), s.sem("a_exped"), s.sem("a_masked")
    turned, pv, combined = s.sem("a_turned"), s.sem("a_pv"), s.sem("a_combined")
    moved = [s.sem("a_moved_v"), s.sem("a_moved_a")]

    units = []
    for t in range(TT):
        units.append(Unit(kind=0, t=t, h=0, lo=0, n=TT // 2, last=True))
        for kind in (1, 2):
            for h in range(NH):
                lo = 0 if kind == 1 else max(0, t - WIN // P)
                units.append(Unit(kind=kind, t=t, h=h, lo=lo, n=t + 1 - lo, last=h == NH - 1))
        if t:
            units.insert(len(units) - 8, Unit(kind=3, t=t - 1, h=0, lo=0, n=4, last=False))
    units.append(Unit(kind=3, t=TT - 1, h=0, lo=0, n=4, last=False))
    chunk = real = 0
    for u in units:
        u.chunks = []
        width = 8 if u.kind == 0 else u.n
        for c0 in range(0, width, 4):
            u.chunks.append((chunk, c0, min(4, width - c0)))
            chunk += 1
        u.branch = 3 * u.t + u.kind
        if u.kind < 3:
            u.i = real
            real += 1
    scored_units = [u for u in units if u.kind < 3]

    def done_chunks(c):
        return c // 2 + 1

    def steps():
        ahead = 2
        for u in units:
            nxt = None
            if u.kind < 3:
                nxt = scored_units[ahead] if ahead < len(scored_units) else None
                ahead += 1
            yield u, nxt

    with nc.Block() as block:
        @block.sync
        def _(sp):
            sp.dma_start(cmp_add_f, T["c_cmp_add"]).then_inc(masks_in, 16)
            sp.dma_start(cmp_mul, T["c_cmp_mul"]).then_inc(masks_in, 16)

        @block.gpsimd
        def _(pool):
            for new, old in ((T["s_wk"], T["cache_win_k"]), (T["s_wv"], T["cache_win_v"])):
                pool.dma_start(new[0, :, 0:WIN - 1].rearrange("b t g d -> b (t g d)"),
                               old[0, :, 1:WIN].rearrange("b t g d -> b (t g d)")).then_inc(window_out, 16)
            pool.wait_ge(window_out, 32)

        @block.tensor
        def _(pe):
            def scores(u):
                wait(pe, exped, u.i - 1)
                ps = score[u.i % 2]
                if u.kind == 0:
                    for g in range(NG):
                        pe.matmul(ps[:, 512 * g:512 * g + 256], s.identb[:, :],
                                  bc(cmp_add[:, u.t, :].unsqueeze(1), (P, HPG, HD)), start=True, stop=False)
                    for j in range(HPG):
                        for g in range(NG):
                            last = pe.matmul(ps[:, 512 * g + j * HD:512 * g + j * HD + NC_P],
                                             s.qT[g * HD:(g + 1) * HD, j, u.t * P:(u.t + 1) * P],
                                             s.kcT[g * HD:(g + 1) * HD, 0, 0:NC_P], start=False,
                                             stop=(j == HPG - 1))
                else:
                    g, j = u.h // HPG, u.h % HPG
                    keys = s.ksT if u.kind == 1 else s.kwT
                    for c0 in range(0, u.n, 4):
                        c1 = min(u.n, c0 + 4)
                        diag = c1 == u.n
                        far = u.kind == 2 and u.t >= WIN // P and c0 == 0
                        last = pe.matmul(ps[:, c0 * P:c1 * P], s.qT[g * HD:(g + 1) * HD, j, u.t * P:(u.t + 1) * P],
                                         keys[g * HD:(g + 1) * HD, (u.lo + c0) * P:(u.lo + c1) * P],
                                         start=True, stop=not (diag or far))
                        if far:
                            last = pe.matmul(ps[:, 0:P], s.identb[:, :], s.add[:, 1, :], start=False, stop=not diag)
                        if diag:
                            last = pe.matmul(ps[:, (u.n - 1) * P:u.n * P], s.identb[:, :], s.add[:, 0, :],
                                             start=False, stop=True)
                last.then_inc(scored, 1)

            pe.wait_ge(mask_cast, 1)
            scores(scored_units[0])
            scores(scored_units[1])
            for u, nxt in steps():
                if u.kind == 3:
                    pe.wait_ge(combined, 3 * u.t + 3)
                elif u.kind == 0:
                    pe.wait_ge(masked, u.t + 1)
                else:
                    pe.wait_ge(exped, u.i + 1)
                for c, c0, n in u.chunks:
                    wait(pe, moved[c % 2], done_chunks(c) - 1)
                    out = turn_ps[c % 2]
                    for k in range(n):
                        if u.kind == 0:
                            h = c0 + k
                            last = pe.transpose(out[0:NC_P, k * P:(k + 1) * P], prob[u.i % 2][:, h * HD:h * HD + NC_P],
                                                s.ident[:, :])
                        else:
                            src = o_tm[u.t % 2] if u.kind == 3 else prob[u.i % 2]
                            last = pe.transpose(out[:, k * P:(k + 1) * P], src[:, (c0 + k) * P:(c0 + k + 1) * P],
                                                s.ident[:, :])
                    last.then_inc(turned, 1)
                if nxt:
                    scores(nxt)
                if u.kind == 3:
                    continue
                for c, c0, n in u.chunks:
                    pe.wait_ge(moved[c % 2], done_chunks(c))
                out = out_ps[u.branch % 2]
                if u.h == 0:
                    wait(pe, combined, u.branch - 1)
                if u.kind == 0:
                    for h in range(NH):
                        g = h // HPG
                        last = pe.matmul(out[:, h * HD:(h + 1) * HD], probT[u.i % 2][0:NC_P, h * P:(h + 1) * P],
                                         s.vc[0:NC_P, 0, g * HD:(g + 1) * HD], start=True, stop=True)
                else:
                    g = u.h // HPG
                    for k in range(u.n):
                        last = pe.matmul(out[:, u.h * HD:(u.h + 1) * HD], probT[u.i % 2][:, k * P:(k + 1) * P],
                                         s.vkv[:, u.lo + k, u.kind - 1, g * HD:(g + 1) * HD],
                                         start=(k == 0), stop=(k == u.n - 1))
                last.then_inc(pv, 1)

        def copy_chunks(eng, copy, which, u):
            for c, c0, n in u.chunks:
                if c % 2 != which:
                    continue
                eng.wait_ge(turned, c + 1)
                if u.kind == 3:
                    copy(s.oN[:, :, u.t * P:(u.t + 1) * P], view(turn_ps[which], 0, 4, P)).then_inc(moved[which], 1)
                    continue
                wait(eng, pv, u.i - 1)
                rows = NC_P if u.kind == 0 else P
                copy(probT[u.i % 2][0:rows, c0 * P:(c0 + n) * P],
                     turn_ps[which][0:rows, 0:n * P]).then_inc(moved[which], 1)

        @block.scalar
        def _(act):
            def exps(u):
                act.wait_ge(maxed, u.i + 1)
                if u.kind == 0:
                    act.activation(prob[u.i % 2][:, 0:512], prob[u.i % 2][:, 0:512], ACT.Exp).then_inc(exped, 1)
                else:
                    before = [w for w in scored_units if w.i == u.i - 2]
                    if before:
                        act.wait_ge(turned, before[0].chunks[-1][0] + 1)
                    act.activation(prob[u.i % 2][:, 0:u.n * P], score[u.i % 2][:, 0:u.n * P], ACT.Exp,
                                   bias=top[:, u.i % 2, 0:1],
                                   accum_out=total[:, u.branch % 4, u.h:u.h + 1]).then_inc(exped, 1)

            exps(scored_units[0])
            exps(scored_units[1])
            for u, nxt in steps():
                copy_chunks(act, lambda o, i: act.activation(o, i, ACT.Copy), 1, u)
                if nxt:
                    exps(nxt)

        @block.vector
        def _(v):
            ch = s.dve_chain

            def maxima(u):
                v.wait_ge(scored, u.i + 1)
                ps, pr = score[u.i % 2], prob[u.i % 2]
                wait(v, exped, u.i - 1)
                if u.kind:
                    v.tensor_reduce(top[:, u.i % 2, 0:1], ps[:, 0:u.n * P], AX.X, ALU.max,
                                    negate=True).then_inc(maxed, 1)
                    return
                before = [w for w in scored_units if w.i == u.i - 2]
                if before:
                    v.wait_ge(turned, before[0].chunks[-1][0] + 1)
                by_group = lambda x: x.rearrange("p (g j n) -> p g j n", g=NG, n=HD)
                heads = ps.rearrange("p (g j n) -> p g j n", g=NG, n=HD)[:, :, 0:HPG]
                most = top[:, u.i % 2, :].rearrange("p (g j) -> p g j", g=NG)
                ch.link(v, v.tensor_reduce(most, heads, AX.X, ALU.max))
                v.tensor_tensor(by_group(pr[:, 0:512]), heads, bc(most.unsqueeze(3), (P, NG, HPG, HD)),
                                ALU.subtract).then_inc(maxed, 1)
                v.wait_ge(exped, u.i + 1)
                e = pr[:, 0:512].rearrange("p (h n) -> p h n", h=NH)
                ch.link(v, v.tensor_tensor(e, e, bc(cmp_mul[:, u.t, :].unsqueeze(1), (P, NH, HD)), ALU.mult))
                ch.link(v, v.tensor_reduce(total[:, u.branch % 4, :], e, AX.X, ALU.add))
                v.tensor_scalar(total[:, u.branch % 4, :], total[:, u.branch % 4, :], 1e-30, None,
                                ALU.max).then_inc(masked, 1)

            def combine(u):
                v.wait_ge(pv, u.i + 1)
                ch.link(v, v.reciprocal(coef, total[:, u.branch % 4, :]))
                gate = s.gates[:, u.t, :].rearrange("p (h c) -> p h c", c=3)[:, :, u.kind]
                ch.link(v, v.tensor_tensor(coef, coef, gate, ALU.mult))
                src = out_ps[u.branch % 2].rearrange("p (g j d) -> p g j d", g=NG, d=HD)
                pairs = lambda x: x.rearrange("p (j g d) -> p g j d", g=NG, d=HD)
                by = bc(coef.rearrange("p (g j) -> p g j", g=NG).unsqueeze(3), (P, NG, HPG, HD))
                if u.kind == 0:
                    if u.t >= 2:
                        old = [w for w in units if w.kind == 3 and w.t == u.t - 2][0]
                        v.wait_ge(turned, old.chunks[-1][0] + 1)
                    v.tensor_tensor(pairs(o_tm[u.t % 2]), src, by, ALU.mult).then_inc(combined, 1)
                else:
                    v.wait_ge(combined, u.branch)
                    ch.link(v, v.tensor_tensor(pairs(part), src, by, ALU.mult))
                    v.tensor_tensor(o_tm[u.t % 2], o_tm[u.t % 2], part, ALU.add).then_inc(combined, 1)

            v.wait_ge(masks_in, 32)
            v.tensor_copy(cmp_add, cmp_add_f).then_inc(mask_cast, 1)
            maxima(scored_units[0])
            maxima(scored_units[1])
            pending = None
            for u, nxt in steps():
                copy_chunks(v, v.tensor_copy, 0, u)
                if nxt:
                    maxima(nxt)
                if pending:
                    combine(pending)
                    pending = None
                if u.last:
                    pending = u
                    if u.kind == 2 and u.t == TT - 1:
                        combine(u)
                        pending = None


def stage_decode_attention(nc, s, T):
    ROWS = NB * NH
    BUFS = 4
    buf = [view(s.ring, 2048 * i, 16, P) for i in range(BUFS)]
    of = [(b + 2) % BUFS for b in range(NB)]
    win_keys = [view(s.ring, 512 * b, 4, P) for b in range(NB)]
    win_vals = [view(s.ring, 4096 + 512 * b, 4, P) for b in range(NB)]
    keysT = [view(s.work, 8256 + 2048 * i, 16, P) for i in range(2)]
    win_keysT = [view(s.work, 8256 + 512 * b, 4, P) for b in range(NB)]
    scT = view(s.work, 12384, 16, ROWS)
    prT = view(s.work, 13408, 16, ROWS)
    win_scT, win_prT = view(s.work, 15544, 4, ROWS), view(s.work, 15800, 4, ROWS)
    rows = view(s.work, X3, 2048)[0:ROWS]
    Y = X3 + 2048
    qbd = view(s.work, Y, ROWS)
    knew = view(s.work, Y + 64, 2, NB)
    gate = view(s.work, Y + 80, 3)[0:ROWS]
    own = view(s.work, Y + 88, NB)[0:ROWS]
    over = view(s.work, Y + 96, NS_S)
    st = view(s.work, Y + 136, 16)[0:ROWS]
    cmp_rows = view(s.work, Y + 152, P)[0:ROWS]
    cmp_pT = view(s.work, Y + 280, ROWS)
    cmp_sc = view(s.work, Y + 344, ROWS)
    imp = view(s.work, Y + 408, NS_S)[0:ROWS]
    grp = view(s.work, Y + 448, NB * NG)
    grp_all = view(s.work, Y + 464, ROWS)
    pen = view(s.work, Y + 528, NS_S)[0:ROWS]
    new_d = view(s.work, Y + 568, NB)[0:ROWS]
    new_dT = view(s.work, Y + 576, 2, ROWS)
    eq = view(s.work, Y + 704, NS_S * NS_S)[0:ROWS]
    gt = view(s.work, 23880, NS_S * NS_S)[0:ROWS]
    lower = view(s.work, 14448, NS_S * NS_S)[0:ROWS]
    small, q_ready = s.sem("d_small"), s.sem("d_q_ready")
    buf_in = [s.sem(f"d_buf_in{i}") for i in range(BUFS)]
    wk_in, wv_in = s.sem("d_wk"), s.sem("d_wv")
    turned, evac_v, evac_a = s.sem("d_turned"), s.sem("d_evac_v"), s.sem("d_evac_a")
    dotted, dots_read = s.sem("d_dotted"), s.sem("d_dots_read")
    pe_to_v, v_to_pe = s.sem("d_pe_to_v"), s.sem("d_v_to_pe")
    v_to_a, a_to_v = s.sem("d_v_to_a"), s.sem("d_a_to_v")
    vals_used = s.sem("d_vals_used")
    o_rows = view(s.work, X3, NB, P)[0:NH]
    O = s.psall[0:NH, 6 * 512:8 * 512].rearrange("p (b c) -> p b c", c=P)

    with nc.Block() as block:
        @block.sync
        def _(sp):
            for b in range(NB):
                sp.dma_start(win_keys[b], T["cache_win_k"][0, b].rearrange("(p t) g d -> p t (g d)", t=4)).then_inc(wk_in, 16)
            sp.dma_start(gate, T["gate_rows"].rearrange("b (h c) -> (b h) c", c=3)).then_inc(small, 16)
            sp.dma_start(own, T["c_own"]).then_inc(small, 16)
            sp.dma_start(over[0:NC_S], T["c_over"]).then_inc(small, 16)
            sp.dma_start(lower, T["c_lower"]).then_inc(small, 16)
            sp.wait_ge(vals_used, 6)
            for b in range(NB):
                sp.dma_start(win_vals[b], T["cache_win_v"][0, b].rearrange("(p t) g d -> p t (g d)", t=4)).then_inc(wv_in, 16)

        @block.gpsimd
        def _(pool):
            def gather(src, b):
                pool.indirect_dma_start(
                    out=buf[of[b]].rearrange("p t c -> p (t c)"), out_offset=None,
                    in_=src[0].rearrange("n (j t) g d -> (n j) (t g d)", t=CMP_STRIDE),
                    in_offset=bass.IndirectOffsetOnAxis(ap=s.gidx[:, b:b + 1], axis=0)).then_inc(buf_in[of[b]], 16)

            for b in range(NB):
                if b >= 2:
                    pool.wait_ge(turned, 4 * (b - 1))
                gather(T["cache_slc_k"], b)
            for b in range(NB):
                if b < BUFS:
                    pool.wait_ge(turned, NB + 4 * (b + BUFS + 1))
                else:
                    pool.wait_ge(vals_used, b - BUFS + 1)
                gather(T["cache_slc_v"], b)

        @block.tensor
        def _(pe):
            to_v, from_v = [0], [0]

            def signal(ins):
                to_v[0] += 1
                ins.then_inc(pe_to_v, 1)

            def v_done():
                from_v[0] += 1
                pe.wait_ge(v_to_pe, from_v[0])

            def turn_keys(src, chunks, first):
                for c in range(chunks):
                    for k in range(4):
                        last = pe.transpose(s.ps[(first + c) % 4][:, k * P:(k + 1) * P], src[:, 4 * c + k, :], s.ident[:, :])
                    last.then_inc(turned, 1)

            def dots(keys, n, b, slot):
                for k in range(n):
                    last = pe.matmul(s.ps[5 + slot % 2][:, k * NH:(k + 1) * NH], keys[:, k, :],
                                     qbd[:, b * NH:(b + 1) * NH], start=True, stop=True)
                last.then_inc(dotted, 1)

            def to_rows(src, n, banks):
                for k in range(n):
                    last = pe.transpose(banks[k // 4][0:ROWS, (k % 4) * P:(k % 4 + 1) * P], src[:, k, :], s.ident[:, :])
                signal(last)

            def to_keys(n, banks, small_at):
                for k in range(n):
                    last = pe.transpose(banks[k // 8][:, (k % 8) * ROWS:(k % 8 + 1) * ROWS],
                                        rows[:, k * P:(k + 1) * P], s.ident[0:ROWS, 0:ROWS])
                signal(pe.transpose(s.ps[4][0:NB, small_at:small_at + ROWS], new_d, s.ident[0:ROWS, 0:ROWS]))

            def compressed_scores():
                for b in range(NB):
                    last = pe.matmul(s.ps[7][0:NC_S, b * NH:(b + 1) * NH], s.kcT[:, 1 + b, 0:NC_S],
                                     qbd[:, b * NH:(b + 1) * NH], start=True, stop=True)
                signal(last)

            def compressed_rows():
                v_done()
                pe.transpose(s.ps[4][0:ROWS, 0:NC_S], cmp_sc[0:NC_S, :], s.ident[0:NC_S, 0:NC_S])
                for kind in range(2):
                    last = pe.matmul(s.ps[4][0:ROWS, 128 + kind * NB:128 + (kind + 1) * NB], qbd, knew[:, kind, :],
                                     start=True, stop=True)
                signal(last)

            def compressed_weights():
                v_done()
                signal(pe.transpose(s.ps[7][0:NC_S, 0:ROWS], cmp_rows[:, 0:NC_S], s.ident[0:ROWS, 0:ROWS]))

            def importance():
                v_done()
                pe.matmul(s.ps[4][0:ROWS, 0:NS_S], grp_all[0:NC_S, :], over[0:NC_S, :], start=True, stop=True)
                signal(pe.transpose(s.ps[7][0:NC_S, 0:ROWS], cmp_rows[:, 0:NC_S], s.ident[0:ROWS, 0:ROWS]))

            def window_rows():
                v_done()
                to_rows(win_scT, 4, [s.ps[7]])

            def window_weights():
                v_done()
                to_keys(4, [s.ps[7]], 0)

            steps = (compressed_rows, compressed_weights, importance, window_rows, window_weights)
            pe.wait_ge(q_ready, 1)
            compressed_scores()
            pe.wait_ge(wk_in, 16 * NB)
            for b in range(NB):
                if b >= 4:
                    pe.wait_ge(evac_a if b % 2 else evac_v, (b - 4) // 2 + 1)
                turn_keys(win_keys[b], 1, b)
            pe.wait_ge(evac_v, NB // 2)
            pe.wait_ge(evac_a, NB // 2)
            for b in range(NB):
                wait(pe, dots_read, b - 1)
                dots(win_keysT[b], 4, b, b)
            pe.wait_ge(buf_in[of[0]], 16)
            turn_keys(buf[of[0]], 4, 0)
            for b in range(NB):
                if b + 1 < NB:
                    pe.wait_ge(buf_in[of[b + 1]], 16 * ((b + 1) // BUFS + 1))
                    for c in range(4):
                        pe.wait_ge(evac_a if c % 2 else evac_v, NB // 2 + 2 * b + c // 2 + 1)
                        for k in range(4):
                            last = pe.transpose(s.ps[c][:, k * P:(k + 1) * P], buf[of[b + 1]][:, 4 * c + k, :], s.ident[:, :])
                        last.then_inc(turned, 1)
                pe.wait_ge(evac_v, NB // 2 + 2 * b + 2)
                pe.wait_ge(evac_a, NB // 2 + 2 * b + 2)
                pe.wait_ge(dots_read, NB + b - 1)
                dots(keysT[b % 2], 16, b, b)
                if b < len(steps):
                    steps[b]()
            pe.wait_ge(dots_read, 2 * NB)
            v_done()
            to_rows(scT, 16, s.ps[0:4])
            v_done()
            to_keys(16, s.ps[0:2], 0)
            v_done()
            head = lambda w, b: w[:, b * NH:(b + 1) * NH]
            for b in range(NB):
                pe.matmul(O[:, b, :], head(cmp_pT[0:NC_S], b), s.vc[0:NC_S, 1 + b, :], start=(b % 4 == 0), stop=False,
                          skip_group_check=True)
                for kind in range(2):
                    pe.matmul(O[:, b, :], head(new_dT[0:NB, kind, :], b), s.vkv[0:NB, TT, kind, :], start=False,
                              stop=False, skip_group_check=True)
            for b in range(NB):
                pe.wait_ge(buf_in[of[b]], 16 * (b // BUFS + 3))
                for k in range(16):
                    last = pe.matmul(O[:, b, :], head(prT[:, k, :], b), buf[of[b]][:, k, :], start=False, stop=False,
                                     skip_group_check=True)
                last.then_inc(vals_used, 1)
            pe.wait_ge(wv_in, 16 * NB)
            for b in range(NB):
                for k in range(4):
                    last = pe.matmul(O[:, b, :], head(win_prT[:, k, :], b), win_vals[b][:, k, :], start=False,
                                     stop=(b % 4 == 3 and k == 3), skip_group_check=True)
            signal(last)
            v_done()
            for b in range(NB):
                last = pe.transpose(s.ps[5][:, b * NH:(b + 1) * NH], o_rows[:, b, :], s.ident[0:NH, 0:NH])
            signal(last)

        def copy_window(eng, copy, done, odd):
            for b in range(odd, NB, 2):
                eng.wait_ge(turned, b + 1)
                copy(win_keysT[b], view(s.ps[b % 4], 0, 4, P)).then_inc(done, 1)

        def copy_keys(eng, copy, done, odd, b):
            for c in (odd, odd + 2):
                eng.wait_ge(turned, NB + 4 * b + c + 1)
                copy(keysT[b % 2][:, 4 * c:4 * c + 4, :], view(s.ps[c], 0, 4, P)).then_inc(done, 1)

        @block.scalar
        def _(act):
            ch = s.act_chain
            exps = [0]

            def exp_rows(weights, bias, total, new):
                exps[0] += 1
                act.wait_ge(v_to_a, exps[0])
                ch.link(act, act.activation(weights, weights, ACT.Exp, bias=bias, accum_out=total))
                if new is not None:
                    ch.link(act, act.activation(new, new, ACT.Exp, bias=bias))
                act.nop().then_inc(a_to_v, 1)

            copy = lambda o, i: act.activation(o, i, ACT.Copy)
            copy_window(act, copy, evac_a, 1)
            for b in range(NB):
                copy_keys(act, copy, evac_a, 1, b)
                if b == 0:
                    exp_rows(cmp_rows[:, 0:NC_S], st[:, 1:2], st[:, 2:3], None)
                if b == 3:
                    exp_rows(rows[:, 0:512], st[:, 5:6], st[:, 6:7], st[:, 4:5])
            exp_rows(rows[:, 0:2048], st[:, 5:6], st[:, 6:7], st[:, 3:4])

        @block.vector
        def _(v):
            ch = s.dve_chain
            from_pe, from_a = [0], [0]

            def pe_done():
                from_pe[0] += 1
                v.wait_ge(pe_to_v, from_pe[0])

            def act_done():
                from_a[0] += 1
                v.wait_ge(a_to_v, from_a[0])

            def compressed_scores():
                pe_done()
                v.tensor_copy(cmp_sc[0:NC_S, :], s.ps[7][0:NC_S, 0:ROWS]).then_inc(v_to_pe, 1)

            def compressed_rows():
                pe_done()
                ch.link(v, v.tensor_reduce(st[:, 1:2], s.ps[4][0:ROWS, 0:NC_S], AX.X, ALU.max, negate=True))
                ch.link(v, v.tensor_copy(cmp_rows[:, 0:NC_S], s.ps[4][0:ROWS, 0:NC_S]))
                v.nop().then_inc(v_to_a, 1)
                for kind in range(2):
                    ch.link(v, v.tensor_tensor(new_d, s.ps[4][0:ROWS, 128 + kind * NB:128 + (kind + 1) * NB], own, ALU.mult))
                    ch.link(v, v.tensor_reduce(st[:, 3 + kind:4 + kind], new_d, AX.X, ALU.add))
                act_done()
                ch.link(v, v.tensor_scalar(st[:, 2:3], st[:, 2:3], 1e-30, None, ALU.max))
                ch.link(v, v.reciprocal(st[:, 2:3], st[:, 2:3]))
                ch.link(v, v.tensor_scalar(cmp_rows[:, 0:NC_S], cmp_rows[:, 0:NC_S], st[:, 2:3], None, ALU.mult))
                v.nop().then_inc(v_to_pe, 1)

            def compressed_weights():
                pe_done()
                ch.link(v, v.tensor_copy(cmp_pT[0:NC_S, :], s.ps[7][0:NC_S, 0:ROWS]))
                ch.link(v, v.tensor_reduce(grp[0:NC_S, :], cmp_pT[0:NC_S, :].rearrange("p (x j) -> p x j", j=HPG), AX.X,
                                           ALU.add))
                ch.link(v, v.tensor_copy(grp_all[0:NC_S, :].rearrange("p (x j) -> p x j", j=HPG),
                                         bc(grp[0:NC_S, :].unsqueeze(2), (NC_S, NB * NG, HPG))))
                ch.link(v, v.tensor_scalar(cmp_rows[:, 0:NC_S], cmp_rows[:, 0:NC_S], gate[:, 0:1], None, ALU.mult))
                v.nop().then_inc(v_to_pe, 1)

            def importance():
                pe_done()
                v.tensor_copy(cmp_pT[0:NC_S, :], s.ps[7][0:NC_S, 0:ROWS])
                ch.link(v, v.tensor_copy(imp, s.ps[4][0:ROWS, 0:NS_S]))
                v.nop().then_inc(v_to_pe, 1)

            def select():
                v.memset(imp[:, 0:1], 1e9)
                ch.link(v, v.memset(imp[:, NS_S - 2:NS_S], 1e9))
                square = lambda x: x.rearrange("p (a b) -> p a b", a=NS_S)
                mine, other = bc(imp.unsqueeze(2), (ROWS, NS_S, NS_S)), bc(imp.unsqueeze(1), (ROWS, NS_S, NS_S))
                v.tensor_tensor(square(gt), other, mine, ALU.is_gt)
                ch.link(v, v.tensor_tensor(square(eq), other, mine, ALU.is_equal))
                ch.link(v, v.tensor_tensor(eq, eq, lower, ALU.mult))
                ch.link(v, v.tensor_tensor(gt, gt, eq, ALU.add))
                ch.link(v, v.tensor_reduce(pen, square(gt), AX.X, ALU.add))
                ch.link(v, v.tensor_scalar(pen, pen, NSEL - 0.5, NEG, ALU.is_gt, ALU.mult))

            def softmax(n, kind):
                new = st[:, 2 + kind:3 + kind]
                ch.link(v, v.tensor_reduce(st[:, 5:6], rows[:, 0:n], AX.X, ALU.max))
                ch.link(v, v.tensor_tensor(st[:, 5:6], st[:, 5:6], new, ALU.max))
                ch.link(v, v.tensor_scalar(st[:, 5:6], st[:, 5:6], -1.0, None, ALU.mult))
                v.nop().then_inc(v_to_a, 1)
                act_done()
                ch.link(v, v.tensor_tensor(st[:, 6:7], st[:, 6:7], new, ALU.add))
                ch.link(v, v.reciprocal(st[:, 6:7], st[:, 6:7]))
                ch.link(v, v.tensor_tensor(st[:, 6:7], st[:, 6:7], gate[:, kind:kind + 1], ALU.mult))
                v.tensor_scalar(rows[:, 0:n], rows[:, 0:n], st[:, 6:7], None, ALU.mult)
                ch.link(v, v.tensor_tensor(new, new, st[:, 6:7], ALU.mult))
                ch.link(v, v.tensor_scalar(new_d, own, new, None, ALU.mult))
                v.nop().then_inc(v_to_pe, 1)

            def window_rows():
                pe_done()
                ch.link(v, v.tensor_copy(rows[:, 0:512], s.ps[7][0:ROWS, :]))
                ch.link(v, v.memset(rows[:, 0:1], NEG))
                softmax(512, 2)

            def window_weights():
                pe_done()
                v.tensor_copy(win_prT, view(s.ps[7], 0, 4, ROWS))
                ch.link(v, v.tensor_copy(new_dT[0:NB, 1, :], s.ps[4][0:NB, 0:ROWS]))
                v.nop().then_inc(v_to_pe, 1)

            steps = (compressed_rows, compressed_weights, importance, window_rows, window_weights)
            ch.link(v, v.memset(qbd, 0.0))
            for g in range(NG):
                half = slice(g * HD, (g + 1) * HD)
                v.tensor_copy(qbd[half].rearrange("p (b g j) -> p b g j", g=NG, j=HPG)[:, :, g, :],
                              s.qT[half, :, SEQ:TOK].rearrange("p j b -> p b j"))
            v.tensor_copy(knew[:, 0, :], s.ksT[:, SEQ:TOK])
            ch.link(v, v.tensor_copy(knew[:, 1, :], s.kwT[:, SEQ:TOK]))
            v.nop().then_inc(q_ready, 1)
            compressed_scores()
            copy_window(v, v.tensor_copy, evac_v, 0)
            for b in range(NB):
                v.wait_ge(dotted, b + 1)
                v.tensor_copy(win_scT[:, :, b * NH:(b + 1) * NH], view(s.ps[5 + b % 2], 0, 4, NH)).then_inc(dots_read, 1)
            v.wait_ge(small, 64)
            for b in range(NB):
                copy_keys(v, v.tensor_copy, evac_v, 0, b)
                v.wait_ge(dotted, NB + b + 1)
                v.tensor_copy(scT[:, :, b * NH:(b + 1) * NH], view(s.ps[5 + b % 2], 0, 16, NH)).then_inc(dots_read, 1)
                if b < len(steps):
                    steps[b]()
            select()
            pe_done()
            blocks = lambda x: x.rearrange("p (t m e) -> p t m e", t=16, m=32)
            ch.link(v, v.tensor_tensor(blocks(rows), blocks(s.psall[0:ROWS, 0:2048]),
                                       bc(pen[:, 0:32].unsqueeze(1).unsqueeze(3), (ROWS, 16, 32, 4)), ALU.add))
            softmax(2048, 1)
            pe_done()
            for half in range(2):
                v.tensor_copy(prT[:, 8 * half:8 * half + 8, :], view(s.ps[half], 0, 8, ROWS))
            ch.link(v, v.tensor_copy(new_dT[0:NB, 0, :], s.ps[4][0:NB, 0:ROWS]))
            v.nop().then_inc(v_to_pe, 1)
            pe_done()
            v.tensor_copy(o_rows, O).then_inc(v_to_pe, 1)
            pe_done()
            for g in range(NG):
                half = slice(g * HD, (g + 1) * HD)
                last = v.tensor_copy(s.oN[half, :, SEQ:TOK].rearrange("p j b -> p b j"),
                                     s.ps[5][half, 0:ROWS].rearrange("p (b g j) -> p b g j", g=NG, j=HPG)[:, :, g, :])
            ch.link(v, last)


def stage_hgrn(nc, s, T, next_weights):
    kinds = (C_HQ, C_HF, C_HG)
    w_in = T["w_in"][0].rearrange("(k p) n -> p k n", p=P)
    raw = [view(s.ring, 2048 * i + 1024, KT, P) for i in range(2)]
    w_hi, w_lo = ([s.ring_short(2048 * i + at, KT, P) for i in range(2)] for at in (0, 1024))
    q, k, b, sg = ([view(s.work, 8256 + 4128 * par + 1032 * i, TOK) for par in range(2)] for i in range(4))
    E = view(s.ring, 4096, SEQ)
    state = view(s.ring, 5120, NB, P)
    vb = view(s.ring, 6144, NB, P)
    S = view(s.ring, 7168, TT, P)
    X = [view(s.work, 21360 + 1024 * i, SEQ) for i in range(2)]
    AT = view(s.work, 23408, TT, P)
    kdT = view(s.work, 24432, TT, P)
    o_tm = view(s.work, 21360 + 1024, TT, P)
    masks = view(s.work, 25456, 256).bitcast(U8).rearrange("p (l n) -> p l n", l=8)
    st = view(s.work, 25712, 192)
    lb, om, e2, most = (st[:, 4 * i:4 * i + 4] for i in (0, 1, 2, 4))
    dec, dec_d, ssq, rstd, lnv = (st[:, 24 + 8 * i:32 + 8 * i] for i in range(5))
    od, sqd, lnd, rstd_d, part = (st[:, 64 + 8 * i:72 + 8 * i] for i in range(5))
    w_loaded = [s.sem(f"g_w{i}") for i in range(2)]
    cut, split = s.sem("g_cut"), s.sem("g_split")
    masks_in, lb_sub, lb_exp = s.sem("g_masks"), s.sem("g_lb_sub"), s.sem("g_lb_exp")
    projected, evac = s.sem("g_projected"), s.sem("g_evac")
    f_ready, g_ready = s.sem("g_f"), s.sem("g_g")
    diff, exped, x_ready = s.sem("g_diff"), s.sem("g_exped"), s.sem("g_x_ready")
    level, picked = s.sem("g_level"), s.sem("g_picked")
    kd_ready, kd_turned, kd_copied = s.sem("g_kd"), s.sem("g_kd_turned"), s.sem("g_kd_copied")
    updates, states = s.sem("g_updates"), s.sem("g_states")
    new_state, dec_out, dec_sq, dec_sum = s.sem("g_new_state"), s.sem("g_dec_out"), s.sem("g_dec_sq"), s.sem("g_dec_sum")
    rstd_ready, o_ready, o_scaled, o_turned, o_read = (s.sem(f"g_{n}") for n in ("rstd", "o", "o_scaled", "o_turned", "o_read"))
    dec_in, states_out = s.sem("g_dec_in"), s.sem("g_states_out")
    SLOTS = 9
    JOBS = 9
    job = (0, 1, 3, 5, 6, 7, 8)

    with nc.Block() as block:
        @block.sync
        def _(sp):
            sp.dma_start(kdT.bitcast(I32), T["c_levels"]).then_inc(masks_in, 16)
            for h in range(HGH):
                for i, c in enumerate(kinds):
                    j = 3 * h + i
                    wait(sp, projected, 3 * (j - 1))
                    sp.dma_start(raw[j % 2], w_in[:, :, c + h * P:c + (h + 1) * P]).then_inc(w_loaded[j % 2], 16)
            sp.wait_ge(projected, SLOTS * HGH)
            next_weights.load(sp, 0, 0)

        @block.gpsimd
        def _(pool):
            def load_states(h):
                wait(pool, states_out, 32 * h)
                wait(pool, dec_out, h)
                pool.dma_start(state, T["state_hgrn"][0, :, h].rearrange("b f i -> f b i")).then_inc(dec_in, 16)
                pool.dma_start(vb, T["hi_rows"][:, h * P:(h + 1) * P].partition_broadcast(P)).then_inc(dec_in, 16)

            def take_low(j):
                pool.wait_ge(cut, j + 1)
                low(pool, w_lo[j % 2], raw[j % 2], w_hi[j % 2]).then_inc(split, 1)

            load_states(0)
            take_low(0)
            take_low(1)
            for r in range(HGH + 1):
                h = r - 1
                if r < HGH:
                    take_low(3 * r + 2)
                if r >= 1:
                    pool.wait_ge(states, h + 1)
                    pool.dma_start(T["p_hg"][0, 0, h], S[:, TT - 1, :]).then_inc(states_out, 16)
                if r < HGH - 1:
                    take_low(3 * r + 3)
                if r >= 1:
                    pool.wait_ge(new_state, h + 1)
                    pool.dma_start(T["s_hg"][0, :, h].rearrange("b f i -> f b i"), state).then_inc(states_out, 16)
                if r < HGH - 1:
                    take_low(3 * r + 4)
                if 1 <= r < HGH:
                    load_states(r)
            pool.wait_ge(states_out, 32 * HGH)

        @block.tensor
        def _(pe):
            def project(r, u):
                kind, c = u // 3, u % 3
                n = SLOTS * r + u
                j = 3 * r + kind
                if c == 0:
                    pe.wait_ge(split, j + 1)
                wait(pe, evac, n - 2)
                cols = slice(c * CH, (c + 1) * CH)
                for i in range(KT):
                    last = product(pe, s.ps[c][:, 0:CH], (w_hi[j % 2][:, i, :], w_lo[j % 2][:, i, :]),
                                   (s.hT[:, i, cols], s.xT_r[:, i, cols]), i == 0, i == KT - 1)
                last.then_inc(projected, 1)

            def attend(h, u):
                p = h % 2
                if u < 8:
                    if u < 7:
                        pe.wait_ge(x_ready, 7 * h + u + 1)
                    for half in range(2):
                        wait(pe, picked, 2 * (8 * h + u - 1) + half + 1)
                        for c in range(4 * half, 4 * half + 4):
                            cols = slice(c * P, (c + 1) * P)
                            a, x = (X[u % 2], X[u % 2]) if u < 7 else (k[p], q[p])
                            last = pe.matmul(s.ps[3 + half][:, (c % 4) * P:(c % 4 + 1) * P], a[:, cols], x[:, cols],
                                             start=True, stop=True)
                        last.then_inc(level, 1)
                if u == 1:
                    pe.wait_ge(kd_ready, h + 1)
                    wait(pe, o_read, h)
                    for c in range(TT):
                        last = pe.transpose(s.ps[6 + c // 4][:, (c % 4) * P:(c % 4 + 1) * P],
                                            X[0][:, c * P:(c + 1) * P], s.ident[:, :])
                    last.then_inc(kd_turned, 1)
                if u == 2:
                    pe.wait_ge(kd_copied, h + 1)
                    for c in range(TT):
                        last = pe.matmul(s.ps[6 + c // 4][:, (c % 4) * P:(c % 4 + 1) * P], kdT[:, c, :],
                                         s.vhi[:, c, h * P:(h + 1) * P], start=True, stop=True)
                    last.then_inc(updates, 1)
                if u == 6:
                    pe.wait_ge(new_state, h + 1)
                    for n in range(NB):
                        last = pe.matmul(s.ps[5][:, n:n + 1], state[:, n, :], q[p][:, SEQ + n:SEQ + n + 1],
                                         start=True, stop=True)
                    last.then_inc(dec_out, 1)
                if u == 8:
                    pe.wait_ge(dec_sq, h + 1)
                    pe.matmul(s.ps[5][:, NB:2 * NB], s.ones[:, :], sqd, start=True, stop=True).then_inc(dec_sum, 1)
                    pe.wait_ge(states, h + 1)
                    pe.wait_ge(picked, 16 * (h + 1))
                    for c in range(TT):
                        out = s.ps[6 + c // 4][:, (c % 4) * P:(c % 4 + 1) * P]
                        last = pe.matmul(out, AT[:, c, :], s.vhi[:, c, h * P:(h + 1) * P], start=True, stop=(c == 0))
                        if c:
                            last = pe.matmul(out, s.oH[:, h, c * P:(c + 1) * P], S[:, c - 1, :], start=False, stop=True)
                    last.then_inc(o_ready, 1)

            def turn_output(h):
                pe.wait_ge(o_scaled, h + 1)
                for c in range(TT):
                    last = pe.transpose(s.ps[6 + c // 4][:, (c % 4) * P:(c % 4 + 1) * P], o_tm[:, c, :], s.ident[:, :])
                last.then_inc(o_turned, 1)

            for r in range(HGH + 1):
                for u in range(SLOTS):
                    if r < HGH:
                        project(r, u)
                    if u == 0 and r >= 2:
                        turn_output(r - 2)
                    if r >= 1:
                        attend(r - 1, u)
            turn_output(HGH - 1)

        @block.scalar
        def _(act):
            ch = s.act_chain
            func = (ACT.Copy, ACT.Sigmoid, ACT.Silu)

            def halves(u):
                m = 64 >> u
                return E[:, 0:SEQ].rearrange("p (b h m) -> p b h m", h=2, m=m)

            def evacuate(r, u):
                kind, c = u // 3, u % 3
                dst = (q, b, sg)[kind][r % 2]
                act.wait_ge(projected, SLOTS * r + u + 1)
                act.activation(dst[:, c * CH:(c + 1) * CH], s.ps[c][:, 0:CH], func[kind]).then_inc(evac, 1)

            def attend(h, u):
                p = h % 2
                if u < 7:
                    act.wait_ge(diff, JOBS * h + job[u] + 1)
                    e = halves(u)
                    act.activation(e[:, :, 0, :], e[:, :, 0, :], ACT.Exp, scale=-1.0)
                    act.activation(e[:, :, 1, :], e[:, :, 1, :], ACT.Exp).then_inc(exped, 1)
                if u == 1:
                    act.wait_ge(diff, JOBS * h + 3)
                    act.activation(E[:, 0:SEQ], E[:, 0:SEQ], ACT.Exp, scale=-1.0).then_inc(exped, 1)
                if u == 2:
                    act.wait_ge(kd_turned, h + 1)
                    act.activation(kdT.rearrange("p c n -> p (c n)"), s.psall[:, 6 * 512:8 * 512],
                                   ACT.Copy).then_inc(kd_copied, 1)
                    act.wait_ge(diff, JOBS * h + 5)
                    act.activation(dec_d, b[p][:, SEQ:TOK], ACT.Exp)
                    act.activation(E, b[p][:, 0:SEQ], ACT.Exp).then_inc(exped, 1)
                if u == 8:
                    act.wait_ge(dec_sum, h + 1)
                    ch.link(act, act.activation(lnd, s.ps[5][:, NB:2 * NB], ACT.Ln, bias=s.eps[:, 0:1], scale=1.0 / P))
                    act.activation(rstd_d, lnd, ACT.Exp, scale=-0.5).then_inc(rstd_ready, 1)
                    act.wait_ge(o_ready, h + 1)
                    for c in range(TT):
                        last = act.activation(kdT[:, c, :], s.ps[6 + c // 4][:, (c % 4) * P:(c % 4 + 1) * P], ACT.Square,
                                              accum_out=ssq[:, c:c + 1])
                    ch.link(act, last)
                    ch.link(act, act.activation(lnv, ssq, ACT.Ln, bias=s.eps[:, 0:1], scale=1.0 / P))
                    act.activation(rstd, lnv, ACT.Exp, scale=-0.5).then_inc(rstd_ready, 1)

            act.wait_ge(lb_sub, 1)
            act.activation(st[:, 8:16], st[:, 8:16], ACT.Exp).then_inc(lb_exp, 1)
            for r in range(HGH + 1):
                for u in range(SLOTS):
                    if r >= 1:
                        attend(r - 1, u)
                    if r < HGH:
                        evacuate(r, u)
                        if u == 6:
                            act.wait_ge(f_ready, r + 1)
                            act.activation(b[r % 2], b[r % 2], ACT.Ln).then_inc(g_ready, 1)

        @block.vector
        def _(v):
            ch = s.dve_chain
            rows = s.vec[:, 64:72].rearrange("p (a r) -> p a r", a=2)
            pair = st[:, 8:16].rearrange("p (a r) -> p a r", a=2)
            ch.link(v, v.tensor_tensor(most, rows[:, 0], rows[:, 1], ALU.max))
            v.tensor_tensor(pair, rows, bc(most.unsqueeze(1), (P, 2, 4)), ALU.subtract).then_inc(lb_sub, 1)
            v.memset(AT, 0.0)
            v.wait_ge(lb_exp, 1)
            ch.link(v, v.tensor_tensor(most, pair[:, 0], pair[:, 1], ALU.add))
            ch.link(v, v.reciprocal(most, most))
            ch.link(v, v.tensor_tensor(lb, pair[:, 0], most, ALU.mult))
            ch.link(v, v.tensor_scalar(om, lb, -1.0, 1.0, ALU.mult, ALU.add))
            v.wait_ge(masks_in, 16)
            ch.link(v, v.tensor_copy(masks, kdT.bitcast(I32)))

            def cut_weights(j):
                v.wait_ge(w_loaded[j % 2], 16 * (j // 2 + 1))
                wait(v, projected, 3 * (j - 1))
                high(v, w_hi[j % 2], raw[j % 2]).then_inc(cut, 1)

            cut_weights(0)
            cut_weights(1)

            def forget(r, u):
                p = r % 2
                j = 3 * r + u // 3 + 1
                if u % 3 == 2 and 2 <= j < 3 * HGH:
                    cut_weights(j)
                if u == 6:
                    v.wait_ge(evac, SLOTS * r + 6)
                    ch.link(v, v.tensor_scalar(b[p], b[p], om[:, r:r + 1], lb[:, r:r + 1], ALU.mult, ALU.add))
                    v.tensor_scalar(k[p], b[p], -1.0, 1.0, ALU.mult, ALU.add).then_inc(f_ready, 1)
                if u == 7:
                    v.wait_ge(g_ready, r + 1)
                    for c in range(TT):
                        cols = b[p][:, c * P:(c + 1) * P]
                        last = v.tensor_tensor_scan(cols, s.ones[:, :], cols, 0.0, ALU.mult, ALU.add)
                    ch.link(v, last)

            def pick(h, u):
                for half in range(2):
                    v.wait_ge(level, 2 * (8 * h + u) + half + 1)
                    v.copy_predicated(AT[:, 4 * half:4 * half + 4, :], bc(masks[:, u, :].unsqueeze(1), (P, 4, P)),
                                      view(s.ps[3 + half], 0, 4, P)).then_inc(picked, 1)

            def attend(h, u):
                p = h % 2
                chunks = lambda x: x[:, 0:SEQ].rearrange("p (c n) -> p c n", n=P)
                if u < 7:
                    m = 64 >> u
                    halves = lambda x: x[:, 0:SEQ].rearrange("p (b h m) -> p b h m", h=2, m=m)
                    blocks = lambda x: x[:, 0:SEQ].rearrange("p (b m) -> p b m", m=2 * m)
                    v.tensor_tensor(blocks(E), blocks(b[p]), bc(blocks(b[p])[:, :, m - 1:m], (P, 512 // m, 2 * m)),
                                    ALU.subtract).then_inc(diff, 1)
                if 1 <= u:
                    if h or u:
                        pick(h, u - 1)
                if u < 7:
                    if u == 2:
                        v.wait_ge(kd_turned, h + 1)
                    if u == 1:
                        wait(v, o_turned, h)
                    if u >= 2:
                        v.wait_ge(level, 2 * (8 * h + u - 2) + 2)
                    v.wait_ge(exped, JOBS * h + job[u] + 1)
                    v.tensor_tensor(halves(X[u % 2])[:, :, 0], halves(k[p])[:, :, 0], halves(E)[:, :, 0], ALU.mult)
                    ch.link(v, v.tensor_tensor(halves(X[u % 2])[:, :, 1], halves(q[p])[:, :, 1], halves(E)[:, :, 1],
                                               ALU.mult))
                    v.nop().then_inc(x_ready, 1)
                if u == 0 and h >= 1:
                    finish(h - 1)
                if u == 1:
                    v.tensor_tensor(chunks(E), chunks(b[p]), bc(chunks(b[p])[:, :, P - 1:P], (P, TT, P)),
                                    ALU.subtract).then_inc(diff, 1)
                    v.wait_ge(exped, JOBS * h + 3)
                    v.wait_ge(level, 2 * 8 * h + 2)
                    ch.link(v, v.tensor_tensor(X[0], k[p][:, 0:SEQ], E[:, 0:SEQ], ALU.mult))
                    v.nop().then_inc(kd_ready, 1)
                if u == 2:
                    v.nop().then_inc(diff, 1)
                    v.wait_ge(exped, JOBS * h + 5)
                    v.tensor_copy(dec, chunks(E)[:, :, P - 1])
                    ch.link(v, v.tensor_tensor(s.oH[:, h, 0:SEQ], q[p][:, 0:SEQ], E[:, 0:SEQ], ALU.mult))
                if u == 3:
                    v.wait_ge(updates, h + 1)
                    wait(v, states_out, 32 * h)
                    src = view(s.psall, 6 * 512, TT, P)
                    ch.link(v, v.tensor_copy(S[:, 0, :], src[:, 0, :]))
                    for c in range(1, TT):
                        ch.link(v, v.scalar_tensor_tensor(out=S[:, c, :], in0=S[:, c - 1, :], scalar=dec[:, c:c + 1],
                                                          in1=src[:, c, :], op0=ALU.mult, op1=ALU.add))
                    v.nop().then_inc(states, 1)
                if u == 5:
                    v.wait_ge(dec_in, 32 * (h + 1))
                    v.tensor_tensor(vb, vb, bc(k[p][:, SEQ:TOK].unsqueeze(2), (P, NB, P)), ALU.mult)
                    ch.link(v, v.tensor_tensor(state, state, bc(dec_d.unsqueeze(2), (P, NB, P)), ALU.mult))
                    v.tensor_tensor(state, state, vb, ALU.add).then_inc(new_state, 1)
                if u == 7:
                    v.wait_ge(dec_out, h + 1)
                    ch.link(v, v.tensor_copy(od, s.ps[5][:, 0:NB]))
                    v.tensor_tensor(sqd, od, od, ALU.mult).then_inc(dec_sq, 1)
                if u == 8:
                    v.wait_ge(rstd_ready, 2 * h + 1)
                    ch.link(v, v.scalar_tensor_tensor(out=part, in0=od, scalar=s.vec[:, 72:73], in1=rstd_d,
                                                      op0=ALU.mult, op1=ALU.mult))
                    v.tensor_tensor(s.oH[:, h, SEQ:TOK], part, sg[p][:, SEQ:TOK], ALU.mult)
                    v.wait_ge(rstd_ready, 2 * h + 2)
                    v.tensor_tensor(o_tm, view(s.psall, 6 * 512, TT, P), bc(rstd.unsqueeze(2), (P, TT, P)),
                                    ALU.mult).then_inc(o_scaled, 1)

            def finish(h):
                v.wait_ge(o_turned, h + 1)
                v.scalar_tensor_tensor(out=s.oH[:, h, 0:SEQ], in0=s.psall[:, 6 * 512:8 * 512], scalar=s.vec[:, 72:73],
                                       in1=sg[h % 2][:, 0:SEQ], op0=ALU.mult, op1=ALU.mult).then_inc(o_read, 1)

            for r in range(HGH + 1):
                for u in range(SLOTS):
                    if r >= 1:
                        attend(r - 1, u)
                    if r < HGH:
                        forget(r, u)
            finish(HGH - 1)
            v.wait_ge(o_read, HGH)


class GateWeights:

    def __init__(self, s, T):
        self.raw = [view(t, at + 2048, 2, KT, P) for t, at in ((s.ring, 0), (s.work, 16512))]
        self.hi, self.lo = ([short(at + o, 2, KT, P) for short, at in ((s.ring_short, 0), (s.work_short, 16512))]
                            for o in (0, 2048))
        self.loaded = [s.sem(f"x_loaded{i}") for i in range(2)]
        self.w_in = T["w_in"][0].rearrange("(k p) n -> p k n", p=P)

    def load(self, sp, n, h):
        for branch, c in enumerate((C_GA, C_GB)):
            sp.dma_start(self.raw[h][:, branch], self.w_in[:, :, bass.ds(c + n * P, P)]).then_inc(self.loaded[h], 16)


def stage_mix(nc, s, T, gate_weights):
    nsa = T["w_br_nsa"][0].rearrange("(g j d) n -> g d j n", g=NG, d=HD)
    hg = T["w_br_hg"][0].rearrange("(h p) n -> p h n", p=P)
    ada = T["ada_w"].rearrange("(k p) n -> p k n", p=P)
    raw, w_hi, w_lo, loaded = gate_weights.raw, gate_weights.hi, gate_weights.lo, gate_weights.loaded
    w_br = [view(t, at + 4096, 2, 4, P) for t, at in ((s.ring, 0), (s.work, 16512))]
    panel = [view(s.ring, 5120 + 1024 * i, KT, P) for i in range(2)]
    sig = [view(s.work, 21632 + 1032 * i, TOK) for i in range(2)]
    part = view(s.work, 23696, TOK)
    mix = view(s.work, 8256, KT * TOK)
    panel_in = [s.sem(f"x_panel_in{i}") for i in range(2)]
    panel_used, ada_done, cut, split = s.sem("x_panel_used"), s.sem("x_ada_done"), s.sem("x_cut"), s.sem("x_split")
    free_a, free_v, product_done = s.sem("x_free_a"), s.sem("x_free_v"), s.sem("x_product")
    LATE = G1

    with nc.Block() as block:
        @block.sync
        def _(sp):
            def load(n, h, gates=True):
                col = n * P
                if gates:
                    gate_weights.load(sp, n, h)
                for dst, src in ((w_br[h][0:HD, 0], nsa[0, :, :, bass.ds(col, P)]),
                                 (w_br[h][HD:P, 0], nsa[1, :, :, bass.ds(col, P)]),
                                 (w_br[h][:, 1], hg[:, :, bass.ds(col, P)])):
                    sp.dma_start(dst, src).then_inc(loaded[h], 16)

            def load_panels(n, start=False):
                for q in range(4):
                    if not (start and q < 2):
                        sp.wait_ge(panel_used, 4 * n + q - 1)
                    sp.dma_start(panel[q % 2], ada[:, :, bass.ds((LATE + 4 * n + q) * P, P)]).then_inc(panel_in[q % 2], 16)

            load(0, 0, gates=False)
            load(1, 1)
            load_panels(0, True)
            with sp.Fori(0, KT // 2 - 1) as i:
                for h in range(2):
                    n = 2 * i + h
                    sp.wait_ge(product_done, 12 * n + 12)
                    load(n + 2, h)
                    load_panels(n + 1)
            load_panels(KT - 1)

        @block.gpsimd
        def _(pool):
            with pool.Fori(0, KT // 2) as i:
                for h in range(2):
                    pool.wait_ge(cut, 2 * i + h + 1)
                    low(pool, w_lo[h], raw[h], w_hi[h]).then_inc(split, 1)

        @block.tensor
        def _(pe):
            def modulate(n, q):
                pe.wait_ge(panel_in[q % 2], 32 * n + 16 * (q // 2) + 16)
                for k in range(KT):
                    last = pe.matmul(s.ps[6][:, bass.ds((4 * n + q) * 9, 9)], panel[q % 2][:, k, :], s.cT[:, k, :],
                                     start=(k == 0), stop=(k == KT - 1))
                last.then_inc(panel_used, 1)

            with pe.Fori(0, KT // 2) as i:
                for h in range(2):
                    n = 2 * i + h
                    pe.wait_ge(split, n + 1)
                    for kind in range(4):
                        branch = kind // 2
                        for c in range(3):
                            cols = slice(c * CH, (c + 1) * CH)
                            out = s.ps[3 * (kind % 2) + c][:, 0:CH]
                            pe.wait_ge(free_v if kind % 2 else free_a, 6 * n + 3 * branch + c + 1)
                            if kind % 2 == 0:
                                for k in range(KT):
                                    last = product(pe, out, (w_hi[h][:, branch, k, :], w_lo[h][:, branch, k, :]),
                                                   (s.hT[:, k, cols], s.xT_r[:, k, cols]), k == 0, k == KT - 1)
                            else:
                                src = s.oH if branch else s.oN
                                for k in range(4):
                                    last = pe.matmul(out, w_br[h][:, branch, k, :], src[:, k, cols], start=(k == 0), stop=(k == 3))
                            last.then_inc(product_done, 1)
                        modulate(n, kind)
            pe.wait_ge(panel_used, 4 * KT)
            pe.sem_inc(ada_done, 1)

        @block.scalar
        def _(act):
            act.sem_inc(free_a, 3)
            with act.Fori(0, KT // 2) as i:
                for h in range(2):
                    n = 2 * i + h
                    for branch in range(2):
                        act.wait_ge(free_v, 6 * n + (3 if branch else 1))
                        for c in range(3):
                            act.wait_ge(product_done, 12 * n + 6 * branch + c + 1)
                            act.activation(sig[branch][:, c * CH:(c + 1) * CH], s.ps[c][:, 0:CH],
                                           ACT.Sigmoid).then_inc(free_a, 1)

        @block.vector
        def _(v):
            ch = s.dve_chain
            v.sem_inc(free_v, 3)

            def cut_weights(h, times):
                v.wait_ge(loaded[h], 80 * times)
                high(v, w_hi[h], raw[h]).then_inc(cut, 1)

            def body(n, h, i, more):
                for branch in range(2):
                    for c in range(3):
                        v.wait_ge(free_a, 6 * n + 3 * branch + c + 4)
                        v.wait_ge(product_done, 12 * n + 6 * branch + c + 4)
                        cols = slice(c * CH, (c + 1) * CH)
                        at = mix[:, bass.ds(n * TOK + c * CH, CH)]
                        ch.link(v, v.tensor_tensor(part[:, cols] if branch else at, sig[branch][:, cols],
                                                   s.ps[3 + c][:, 0:CH], ALU.mult))
                        v.nop().then_inc(free_v, 1)
                        if branch:
                            v.tensor_tensor(at, at, part[:, cols], ALU.add)
                if more:
                    cut_weights(h, i + 2)

            cut_weights(0, 1)
            cut_weights(1, 1)
            with v.Fori(0, KT // 2 - 1) as i:
                ch.enter(i, 12)
                for h in range(2):
                    body(2 * i + h, h, i, True)
            ch.leave(KT // 2 - 1)
            for h in range(2):
                body(KT - 2 + h, h, 0, False)
            v.wait_ge(ada_done, 1)
            finish_modulation(s, v, LATE, 6 * KT, s.ps[6])
            scale_gain(s, v, s.A2, SC2, 56)


def stage_out_projection(nc, s, T, norm):
    w = T["w_out"].rearrange("(k p) n -> p k n", p=P)
    mix, mix_hi, mix_lo = view(s.work, 8256, KT, TOK), s.work_short(16512, KT, TOK), s.work_short(8256, KT, TOK)
    raw = [view(s.ring, 2048 * i + 1024, KT, P) for i in range(2)]
    w_hi, w_lo = ([s.ring_short(2048 * i + at, KT, P) for i in range(2)] for at in (0, 1024))
    part = view(s.ring, 4096, NB)
    loaded = [s.sem(f"w_loaded{i}") for i in range(2)]
    x_in, cut, split = s.sem("w_x_in"), s.sem("w_cut"), s.sem("w_split")
    mix_ready, mix_cut, made, added = s.sem("w_mix_ready"), s.sem("w_mix_cut"), s.sem("w_made"), s.sem("w_added")
    mix_ready_p = s.sem("w_mix_ready_p")
    BANKS = 5

    with nc.Block() as block:
        @block.sync
        def _(sp):
            for n in range(2):
                sp.dma_start(raw[n], w[:, :, n * P:(n + 1) * P]).then_inc(loaded[n], 16)
            sp.dma_start(s.xT[:, :, :], T["x_spill"]).then_inc(x_in, 16)
            for n in range(2, KT):
                sp.wait_ge(made, 3 * (n - 1))
                sp.dma_start(raw[n % 2], w[:, :, n * P:(n + 1) * P]).then_inc(loaded[n % 2], 16)

        @block.gpsimd
        def _(pool):
            for n in range(KT):
                if n == 1:
                    for k in range(2, KT, 3):
                        pool.wait_ge(mix_cut, k + 1)
                        low(pool, mix_lo[:, k, :], mix[:, k, :], mix_hi[:, k, :]).then_inc(mix_ready_p, 1)
                pool.wait_ge(cut, n + 1)
                low(pool, w_lo[n % 2], raw[n % 2], w_hi[n % 2]).then_inc(split, 1)

        @block.tensor
        def _(pe):
            for n in range(KT):
                pe.wait_ge(split, n + 1)
                if n == 0:
                    for k in range(KT):
                        if k % 3 == 2:
                            pe.wait_ge(mix_ready_p, (k + 1) // 3)
                        else:
                            pe.wait_ge(mix_ready, k + 1 - (k + 1) // 3)
                        for c in range(3):
                            cols = slice(c * CH, (c + 1) * CH)
                            last = product(pe, s.ps[c][:, 0:CH], (w_hi[0][:, k, :], w_lo[0][:, k, :]),
                                           (mix_hi[:, k, cols], mix_lo[:, k, cols]), k == 0, k == KT - 1)
                            if k == KT - 1:
                                last.then_inc(made, 1)
                for c in range(3 if n else 0):
                    cols = slice(c * CH, (c + 1) * CH)
                    wait(pe, added, 3 * n + c - BANKS + 1)
                    for k in range(KT):
                        last = product(pe, s.ps[(3 * n + c) % BANKS][:, 0:CH], (w_hi[n % 2][:, k, :], w_lo[n % 2][:, k, :]),
                                       (mix_hi[:, k, cols], mix_lo[:, k, cols]), k == 0, k == KT - 1)
                    last.then_inc(made, 1)
                if n >= 1:
                    norm.sum(pe, n - 1)
            norm.sum(pe, KT - 1)

        @block.scalar
        def _(act):
            for k in range(KT):
                act.activation(mix_hi[:, k, :], mix[:, k, :], ACT.Copy).then_inc(mix_cut, 1)
            for n in range(KT):
                act.wait_ge(added, 3 * n + 3)
                norm.square(act, n)
            norm.root(act)

        @block.vector
        def _(v):
            ch = s.dve_chain

            def cut_weights(n):
                v.wait_ge(loaded[n % 2], 16 * (n // 2 + 1))
                high(v, w_hi[n % 2], raw[n % 2]).then_inc(cut, 1)

            cut_weights(0)
            cut_weights(1)
            for k in range(KT):
                if k % 3 != 2:
                    v.wait_ge(mix_cut, k + 1)
                    low(v, mix_lo[:, k, :], mix[:, k, :], mix_hi[:, k, :]).then_inc(mix_ready, 1)
            v.wait_ge(x_in, 16)
            for n in range(KT):
                for c in range(3):
                    ps = s.ps[(3 * n + c) % BANKS]
                    v.wait_ge(made, 3 * n + c + 1)
                    m = CH if c < 2 else CH - NB
                    at = s.xT[:, n, c * CH:c * CH + m]
                    last = v.scalar_tensor_tensor(out=at, in0=ps[:, 0:m], scalar=s.mod[:, G1 + n, 0:1], in1=at,
                                                  op0=ALU.mult, op1=ALU.add)
                    if c < 2:
                        last.then_inc(added, 1)
                ch.link(v, v.tensor_tensor(part, ps[:, m:CH], s.mod[:, G1 + n, 1:NB + 1], ALU.mult))
                ch.link(v, v.tensor_tensor(s.xT[:, n, SEQ:TOK], s.xT[:, n, SEQ:TOK], part, ALU.add))
                v.nop().then_inc(added, 1)
                if n + 2 < KT:
                    cut_weights(n + 2)


class UpWeights:

    def __init__(self, s, T):
        self.raw = [view(s.ring, 4096 * f + 2048, 2, KT, P) for f in range(2)]
        self.split = [[s.ring_short(4096 * f + 2048 * i, 2, KT, P) for i in range(2)] for f in range(2)]
        self.rows = view(s.work, 19208, DFF)
        self.loaded, self.rows_in = [s.sem(f"f_up_in{i}") for i in range(2)], s.sem("f_rows_in")
        self.w_up = T["w_up"].rearrange("(k p) n -> p k n", p=P)
        self.state = T["state_ffn_conv"]

    def load(self, sp, f, h):
        for part in range(2):
            sp.dma_start(self.raw[h][:, part], self.w_up[:, :, bass.ds(part * DFF + f * P, P)]).then_inc(self.loaded[h], 16)

    def load_ahead(self, sp):
        sp.dma_start(self.rows[0:2 * NB, :], self.state[0].rearrange("b j f -> (b j) f")).then_inc(self.rows_in, 16)
        self.load(sp, 0, 0)
        self.load(sp, 1, 1)


def stage_ffn(nc, s, T, up_weights, norm):
    GR = FT // 2
    w_dn = T["w_down"].rearrange("(g e p) n -> p (g e) n", e=2, p=P)
    hi, lo = s.hT, s.work_short(0, KT, TOK)
    a = [view(s.work, 12384 + 2064 * i, 2, TOK) for i in range(2)]
    aH, aL = ([s.work_short(at + 2064 * i, 2, TOK) for i in range(2)] for at in (8256, 12384))
    u = view(s.work, 16512, SEQ + 2)
    y = view(s.work, 17540, TOK)
    tails = view(s.work, 18572, FT * (NB + 2))
    bufT = view(s.work, 18792, FT * 2 * NB)
    dec = view(s.work, 19144, KT, NB)
    rows = up_weights.rows
    raw_d = view(s.work, 19208 + 2048, 2, D)
    wd = [s.work_short(19208 + 2048 * i, 2, D) for i in range(2)]
    raw_last, wd_last = view(s.ring, 2048, 2, D), [s.ring_short(2048 * i, 2, D) for i in range(2)]
    raw_u, wu, up_in, load_up = up_weights.raw, up_weights.split, up_weights.loaded, up_weights.load
    dn_in, up_cut, dn_cut = s.sem("f_dn_in"), s.sem("f_up_cut"), s.sem("f_dn_cut")
    last_in = s.sem("f_last_in")
    up_split, dn_split, a_ready = s.sem("f_up_split"), s.sem("f_dn_split"), s.sem("f_a_ready")
    u_made, v_made, d_made, added = s.sem("f_u_made"), s.sem("f_v_made"), s.sem("f_d_made"), s.sem("f_added")
    buf_out, turned, copied, out = s.sem("f_buf_out"), s.sem("f_turned"), s.sem("f_copied"), s.sem("f_out")
    u_read, v_read, silu_done, conv_a, conv_v = (s.sem(f"f_{n}") for n in ("u_read", "v_read", "silu", "conv_a", "conv_v"))
    conv = s.conv[:, :, :].rearrange("p j f -> p (j f)")
    x = s.xT

    def groups(eng, body, per=None, ch=None):
        body(0, 0, True, False)
        with eng.Fori(0, GR // 2) as i:
            if ch:
                ch.enter(i, per)
            body(2 * i + 1, 1, True, True)
            body(2 * i + 2, 0, True, True)
        if ch:
            ch.leave(GR // 2)
        body(GR, 1, False, True)

    with nc.Block() as block:
        @block.sync
        def _(sp):
            def load_down(g):
                sp.wait_ge(d_made, 24 * g + 1)
                sp.dma_start(raw_d, w_dn[:, bass.ds(2 * g, 2), :]).then_inc(dn_in, 16)

            up_weights.load_ahead(sp)
            sp.wait_ge(copied, 1)
            with sp.Fori(0, GR - 1) as g:
                for h in range(2):
                    f = 2 * g + 2 + h
                    sp.wait_ge(v_made, 3 * (f - 1))
                    load_up(sp, f, h)
                load_down(g)
            sp.wait_ge(v_made, 3 * (FT - 1))
            sp.dma_start(raw_last, w_dn[:, 2 * GR - 2:2 * GR, :]).then_inc(last_in, 16)
            sp.wait_ge(copied, 1 + (FT + 3) // 4)
            sp.dma_start(T["p_cf"][0, 0], rows[0:2, :]).then_inc(out, 16)
            sp.dma_start(T["s_cf"][0, :, 1], rows[2:2 + NB, :]).then_inc(out, 16)
            sp.wait_ge(out, 32)

        @block.gpsimd
        def _(pool):
            pool.dma_start(T["s_cf"][0, :, 0], T["state_ffn_conv"][0, :, 1]).then_inc(buf_out, 16)

            def low_up(f, h):
                pool.wait_ge(up_cut, f + 1)
                low(pool, wu[h][1], raw_u[h], wu[h][0]).then_inc(up_split, 1)

            def body(g, par, up, down):
                if up:
                    low_up(2 * g + 1, 1)
                if down:
                    pool.wait_ge(dn_cut, g)
                    low(pool, wd[1], raw_d, wd[0]).then_inc(dn_split, 1)
                if up:
                    if up != "last":
                        low_up(2 * g + 2, 0)
                    else:
                        pool.wait_ge(dn_cut, GR)
                        low(pool, wd_last[1], raw_last, wd_last[0]).then_inc(dn_split, 1)

            low_up(0, 0)
            body(0, 0, True, False)
            with pool.Fori(0, GR // 2 - 1) as i:
                body(2 * i + 1, 1, True, True)
                body(2 * i + 2, 0, True, True)
            body(GR - 2, 1, True, True)
            body(GR - 1, 0, "last", True)
            pool.wait_ge(buf_out, 16)

        @block.tensor
        def _(pe):
            pe.sem_inc(d_made, 1)
            pe.wait_ge(up_weights.rows_in, 16)
            for f in range(FT):
                last = pe.transpose(s.ps[6][:, f * 16:(f + 1) * 16], rows[0:2 * NB, f * P:(f + 1) * P],
                                    s.ident[0:2 * NB, 0:2 * NB])
            last.then_inc(turned, 1)
            pe.wait_ge(copied, 1)

            def body(g, par, up, down):
                for h in range(2 if up else 0):
                    f = 2 * g + h
                    pe.wait_ge(up_split, f + 1)
                    if isinstance(f, int) and f == 0:
                        pe.wait_ge(u_read, 1)
                        pe.wait_ge(v_read, 1)
                        for k in range(KT):
                            pe.wait_ge(norm.ready, k + 1)
                            for part, made in enumerate((u_made, v_made)):
                                for c in range(3):
                                    cols = slice(c * CH, (c + 1) * CH)
                                    last = product(pe, s.ps[3 * part + c][:, 0:CH], [w[:, part, k, :] for w in wu[h]],
                                                   (hi[:, k, cols], lo[:, k, cols]), k == 0, k == KT - 1)
                                    if k == KT - 1:
                                        last.then_inc(made, 1)
                        continue
                    for part, (read, made) in enumerate(((u_read, u_made), (v_read, v_made))):
                        pe.wait_ge(read, 3 * f + 1)
                        for c in range(3):
                            cols = slice(c * CH, (c + 1) * CH)
                            for k in range(KT):
                                last = product(pe, s.ps[3 * part + c][:, 0:CH], [w[:, part, k, :] for w in wu[h]],
                                               (hi[:, k, cols], lo[:, k, cols]), k == 0, k == KT - 1)
                            last.then_inc(made, 1)
                if down:
                    weights = wd if up else wd_last
                    pe.wait_ge(dn_split, g)
                    pe.wait_ge(a_ready, 2 * g)
                    for n in range(KT):
                        for c in range(3):
                            cols = slice(c * CH, (c + 1) * CH)
                            pe.wait_ge(added, 24 * (g - 1) + 3 * n + c + 1)
                            for e in range(2):
                                last = product(pe, s.ps[6 + (3 * n + c) % 2][:, 0:CH], [w[:, e, n * P:(n + 1) * P] for w in weights],
                                               (aH[1 - par][:, e, cols], aL[1 - par][:, e, cols]), e == 0, e == 1)
                            last.then_inc(d_made, 1)

            groups(pe, body)
            pe.wait_ge(added, 24 * GR + 2)
            for f in range(FT):
                if f % 4 == 0 and f >= 8:
                    pe.wait_ge(copied, f // 4)
                last = pe.transpose(s.ps[6 + f // 4 % 2][0:NB + 2, (f % 4) * P:(f % 4 + 1) * P],
                                    tails[:, f * 10:(f + 1) * 10], s.ident[:, :])
                if f % 4 == 3 or f == FT - 1:
                    last.then_inc(turned, 1)

        @block.scalar
        def _(act):
            ch = s.act_chain
            act.sem_inc(u_read, 1)
            norm.take_high(act)
            act.wait_ge(copied, 1)

            def body(g, par, up, down):
                for h in range(2 if up else 0):
                    f = 2 * g + h
                    act.wait_ge(conv_v, f + 1)
                    for c in range(3):
                        m = CH if c < 2 else CH - NB
                        act.wait_ge(u_made, 3 * f + c + 1)
                        last = act.activation(u[:, 2 + c * CH:2 + c * CH + m], s.ps[c][:, 0:m], ACT.Copy)
                        if c < 2:
                            last.then_inc(u_read, 1)
                    ch.link(act, last)
                    act.activation(tails[:, bass.ds(10 * f, 2)], s.ps[2][:, m - 2:m], ACT.Copy)
                    ch.link(act, act.activation(tails[:, bass.ds(10 * f + 2, NB)], s.ps[2][:, m:CH], ACT.Copy))
                    act.nop().then_inc(u_read, 1)
                    tap, bias = conv[:, bass.ds(2 * FT + f, 1)], conv[:, bass.ds(3 * FT + f, 1)]
                    act.wait_ge(v_read, 3 * f + 1)
                    act.activation(y[:, 0:SEQ], u[:, 2:SEQ + 2], ACT.Identity, scale=tap, bias=bias)
                    act.activation(y[:, SEQ:TOK], tails[:, bass.ds(10 * f + 2, NB)], ACT.Identity, scale=tap,
                                   bias=bias).then_inc(conv_a, 1)
                    act.wait_ge(conv_v, f + 2)
                    act.activation(y, y, ACT.Silu).then_inc(silu_done, 1)

            groups(act, body, 8, ch)

        @block.vector
        def _(v):
            ch = s.dve_chain
            ch.link(v, v.memset(u[:, 0:2], 0.0))
            v.memset(dec, 0.0)

            def cut_up(f, h, times):
                v.wait_ge(up_in[h], 32 * times)
                if not (isinstance(f, int) and f < 2):
                    v.wait_ge(v_made, 3 * (f - 1))
                high(v, wu[h][0], raw_u[h]).then_inc(up_cut, 1)

            v.wait_ge(turned, 1)
            v.tensor_copy(bufT.rearrange("p (f j b) -> p f j b", j=2, b=NB),
                          view(s.ps[6], 0, FT, NB, 2).rearrange("p f b j -> p f j b")).then_inc(copied, 1)
            v.wait_ge(copied, 1)
            v.sem_inc(v_read, 1)
            v.sem_inc(conv_v, 1)
            v.sem_inc(added, 2)
            cut_up(0, 0, 1)
            norm.scale_and_take_low(v)

            def convolve(f):
                v.wait_ge(conv_a, f + 1)
                taps = [conv[:, bass.ds(j * FT + f, 1)] for j in range(2)]
                ch.link(v, v.scalar_tensor_tensor(out=y[:, 0:SEQ], in0=u[:, 1:SEQ + 1], scalar=taps[1],
                                                  in1=y[:, 0:SEQ], op0=ALU.mult, op1=ALU.add))
                v.scalar_tensor_tensor(out=y[:, 0:SEQ], in0=u[:, 0:SEQ], scalar=taps[0], in1=y[:, 0:SEQ],
                                       op0=ALU.mult, op1=ALU.add)
                yd = y[:, SEQ:TOK]
                ch.link(v, v.scalar_tensor_tensor(out=yd, in0=bufT[:, bass.ds(16 * f + NB, NB)], scalar=taps[1],
                                                  in1=yd, op0=ALU.mult, op1=ALU.add))
                v.scalar_tensor_tensor(out=yd, in0=bufT[:, bass.ds(16 * f, NB)], scalar=taps[0], in1=yd,
                                       op0=ALU.mult, op1=ALU.add).then_inc(conv_v, 1)

            def hidden(f, h, par):
                whole, hi, lo = (t[par][:, h, :] for t in (a, aH, aL))
                v.wait_ge(silu_done, f + 1)
                for c in range(3):
                    cols = slice(c * CH, (c + 1) * CH)
                    v.wait_ge(v_made, 3 * f + c + 1)
                    last = v.tensor_tensor(whole[:, cols], y[:, cols], s.ps[3 + c][:, 0:CH], ALU.mult)
                    if c < 2:
                        last.then_inc(v_read, 1)
                ch.link(v, last)
                v.nop().then_inc(v_read, 1)
                ch.link(v, high(v, hi, whole))
                low(v, lo, whole, hi).then_inc(a_ready, 1)

            def body(g, par, up, down, more=True):
                if up:
                    cut_up(2 * g + 1, 1, g + 1)
                if down and up:
                    v.wait_ge(dn_in, 16 * g)
                    v.wait_ge(d_made, 24 * (g - 1) + 1)
                    high(v, wd[0], raw_d).then_inc(dn_cut, 1)
                if up:
                    convolve(2 * g)
                    hidden(2 * g, 0, par)
                    if more:
                        cut_up(2 * g + 2, 0, g + 2)
                    else:
                        v.wait_ge(last_in, 16)
                        v.wait_ge(v_made, 3 * (FT - 1))
                        high(v, wd_last[0], raw_last).then_inc(dn_cut, 1)
                    convolve(2 * g + 1)
                if down:
                    for n in range(KT):
                        for c in range(3):
                            m = CH if c < 2 else CH - NB
                            ps = s.ps[6 + (3 * n + c) % 2]
                            v.wait_ge(d_made, 24 * (g - 1) + 3 * n + c + 2)
                            if c == 2:
                                ch.link(v, v.tensor_tensor(dec[:, n, :], dec[:, n, :], ps[:, m:CH], ALU.add))
                            at = x[:, n, c * CH:c * CH + m]
                            v.scalar_tensor_tensor(out=at, in0=ps[:, 0:m], scalar=s.mod[:, G2 + n, 0:1], in1=at,
                                                   op0=ALU.mult, op1=ALU.add).then_inc(added, 1)
                if up:
                    hidden(2 * g + 1, 1, par)

            body(0, 0, True, False)
            with v.Fori(0, GR // 2 - 1) as i:
                ch.enter(i, 2 * (8 + KT))
                body(2 * i + 1, 1, True, True)
                body(2 * i + 2, 0, True, True)
            ch.leave(GR // 2 - 1)
            body(GR - 2, 1, True, True)
            body(GR - 1, 0, True, True, more=False)
            body(GR, 1, False, True)
            v.wait_ge(added, 24 * GR + 2)
            ch.link(v, v.tensor_tensor(dec, dec, s.mod[:, G2:G2 + KT, 1:NB + 1], ALU.mult))
            ch.link(v, v.tensor_tensor(x[:, :, SEQ:TOK], x[:, :, SEQ:TOK], dec, ALU.add))
            for g in range((FT + 3) // 4):
                n = min(4, FT - 4 * g) * P
                v.wait_ge(turned, g + 2)
                v.tensor_copy(rows[0:NB + 2, 512 * g:512 * g + n], s.ps[6 + g % 2][0:NB + 2, 0:n]).then_inc(copied, 1)


def stage_output(nc, s, T):
    y = [view(s.ring, 1024 * i, D) for i in range(2)]
    turned, done = s.sem("o_turned"), [s.sem("o_done_v"), s.sem("o_done_a")]
    sent = [s.sem(f"o_sent{i}") for i in range(2)]

    with nc.Block() as block:
        @block.tensor
        def _(pe):
            for t in range(TT + 1):
                n = rows_of(t)
                for half in range(2):
                    g = 2 * t + half
                    wait(pe, done[half], t - 3)
                    for j in range(4):
                        last = pe.transpose(s.ps[g % 8][0:n, j * P:(j + 1) * P],
                                            s.xT[:, 4 * half + j, t * P:t * P + n], s.ident[:, :])
                    last.then_inc(turned, 1)

        def copy_half(eng, copy, half):
            for t in range(TT + 1):
                n = rows_of(t)
                eng.wait_ge(turned, 2 * t + half + 1)
                wait(eng, sent[t % 2], 16 * (t // 2))
                copy(y[t % 2][0:n, 512 * half:512 * (half + 1)], s.ps[(2 * t + half) % 8][0:n, :]).then_inc(done[half], 1)

        @block.vector
        def _(v):
            copy_half(v, v.tensor_copy, 0)

        @block.scalar
        def _(act):
            copy_half(act, lambda o, i: act.activation(o, i, ACT.Copy), 1)

        @block.sync
        def _(sp):
            for t in range(TT + 1):
                for half in range(2):
                    sp.wait_ge(done[half], t + 1)
                dst = T["y_prompt"][0, t * P:(t + 1) * P] if t < TT else T["y_sample"][:, 0]
                sp.dma_start(dst, y[t % 2][0:rows_of(t), :]).then_inc(sent[t % 2], 16)
            for b in range(2):
                sp.wait_ge(sent[b], 16 * len(range(b, TT + 1, 2)))


def program(nc, T):
    s = allocate(nc)
    projections = TokenMajorWeights(s, T)
    norm = Norm(s, "n1", s.A1, SH1, s.xT, s.xT_r, [view(s.work, 10760 + 1032 * i, TOK) for i in range(2)],
                view(s.work, 12824, TOK), view(s.work, 13856, TOK), view(s.work, 14888, KT, NB), (1, 6, 7))
    stage_modulation(nc, s, T, norm, projections)
    stage_token_major(nc, s, T, projections, norm)
    stage_compress(nc, s, T)
    stage_prompt_attention(nc, s, T)
    recycle(nc, s)
    stage_decode_attention(nc, s, T)
    gate_weights = GateWeights(s, T)
    stage_hgrn(nc, s, T, gate_weights)
    stage_mix(nc, s, T, gate_weights)
    norm = Norm(s, "n2", s.A2, SH2, view(s.work, 0, KT, TOK), s.work_short(0, KT, TOK),
                [view(s.ring, 4104 + 1032 * i, TOK) for i in range(2)], view(s.ring, 6168, TOK),
                view(s.work, 24768, TOK), view(s.work, 25800, KT, NB), (5, 6, 7))
    stage_out_projection(nc, s, T, norm)
    stage_ffn(nc, s, T, UpWeights(s, T), norm)
    stage_output(nc, s, T)


_INS = ["x_prompt", "x_sample", "cache_cmp_k", "cache_cmp_v", "cache_slc_k", "cache_slc_v", "cache_win_k",
        "cache_win_v", "state_hgrn", "state_ffn_conv", "page_table", "c_prompt", "c_sample", "ada_w", "ada_b",
        "norm_attn", "norm_ffn", "w_in", "q_gain", "k_gain", "cmp_w1", "cmp_w2", "cmp_pe", "hg_lb", "hg_norm",
        "w_br_nsa", "w_br_hg", "w_out", "w_up", "conv_w", "conv_b", "w_down"]
_OUTS = [("y_prompt", (1, SEQ, D)), ("y_sample", (NB, 1, D)),
         ("p_ck", (1, 1, SEQ, NG, HD)), ("p_cv", (1, 1, SEQ, NG, HD)), ("p_sk", (1, 1, SEQ, NG, HD)),
         ("p_sv", (1, 1, SEQ, NG, HD)), ("p_wk", (1, 1, WIN, NG, HD)), ("p_wv", (1, 1, WIN, NG, HD)),
         ("p_hg", (1, 1, HGH, P, P)), ("p_cf", (1, 1, 2, DFF)),
         ("s_ck", (1, NB, 1, NG, HD)), ("s_cv", (1, NB, 1, NG, HD)), ("s_sk", (1, NB, 1, NG, HD)),
         ("s_sv", (1, NB, 1, NG, HD)), ("s_wk", (1, NB, WIN, NG, HD)), ("s_wv", (1, NB, WIN, NG, HD)),
         ("s_hg", (1, NB, HGH, P, P)), ("s_cf", (1, NB, 2, DFF))]


def kernel(**inputs):
    from concourse import bacc
    from concourse.bass_utils import run_bass_kernel_spmd

    nc = bacc.Bacc("TRN2", target_bir_lowering=False, num_devices=1)
    arrays, T = {}, {}
    given = {name: np.ascontiguousarray(inputs[name]) for name in _INS if name != "page_table"}
    given.update(constants())
    for name, a in given.items():
        arrays[f"in_{name}"] = a
        T[name] = nc.dram_tensor(f"in_{name}", a.shape, mybir.dt.from_np(a.dtype), kind="ExternalInput").ap()
    for name, shape in _OUTS:
        T[name] = nc.dram_tensor(f"out_{name}", shape, F32, kind="ExternalOutput").ap()
    T["x_spill"] = nc.dram_tensor("x_spill", (P, KT, TOK), F32).ap()
    T["hi_rows"] = nc.dram_tensor("hi_rows", (NB, 512), F32).ap()
    T["gate_rows"] = nc.dram_tensor("gate_rows", (NB, 24), F32).ap()
    pages = np.ascontiguousarray(np.repeat(inputs["page_table"].T, SUB_PER_PAGE, axis=0))
    arrays["in_page_rows"] = pages
    T["page_rows"] = nc.dram_tensor("in_page_rows", pages.shape, I32, kind="ExternalInput").ap()
    T["ada_w"], T["w_up"], T["w_down"], T["w_out"] = T["ada_w"][0], T["w_up"][0], T["w_down"][0], T["w_out"][0]
    program(nc, T)
    r = run_bass_kernel_spmd(nc, [arrays], core_ids=[0])
    return tuple(r.results[0][f"out_{name}"] for name, _ in _OUTS)
```
